# Optimizing a Trainium2 kernel written in Bass

```python
import math
import jax, jax.numpy as jnp
from jax import lax
import numpy as np

D_MODEL = 1024
BATCH = 1
SEQ = 512
DEPTH = 1
DEC_BATCH = 1
DEC_SEQ = 512
PAST_LEN = 128

DA_HEADS = 8
DA_HEAD_DIM = 64
DA_QK = DA_HEADS * 2 * DA_HEAD_DIM
DA_V = DA_HEADS * 2 * DA_HEAD_DIM
Q_BLOCK = 128
DIL_GROUPS = ((128, 1), (512, 4), (2048, 16))
DIL_HEADS = 8
DIL_HEAD_DIM = 64
DIL_QKV = len(DIL_GROUPS) * DIL_HEADS * DIL_HEAD_DIM
DIL_OUT = DIL_HEADS * DIL_HEAD_DIM
IN_COLS = 2 * DA_QK + DA_V + 3 * DIL_QKV + 2 * D_MODEL
NUM_BUCKETS = 32
MAX_DISTANCE = 1024
N_REL_HEADS = DA_HEADS + len(DIL_GROUPS) * DIL_HEADS
PEER_HEADS = 8
N_KEYS = 128
N_EXPERTS = N_KEYS * N_KEYS
PEER_QUERY_DIM = 256
PEER_HALF = PEER_QUERY_DIM // 2
PEER_TOPK = 16
TOK_CHUNK = 128
EPS = 1e-6
NEG_BIG = -1e30

kernel_name = 'hybrid_diffattn_dilated_peer_encoder'

def rms_norm(x, g):
    xf = x.astype(jnp.float32)
    y = xf * lax.rsqrt(jnp.mean(xf * xf, axis=-1, keepdims=True) + EPS)
    return (y * g.astype(jnp.float32)).astype(x.dtype)

def rel_bucket(rel):
    half = NUM_BUCKETS // 2
    max_exact = half // 2
    ret = jnp.where(rel > 0, half, 0).astype(jnp.int32)
    n = jnp.abs(rel).astype(jnp.int32)
    nf = jnp.maximum(n, max_exact).astype(jnp.float32)
    large = max_exact + (jnp.log(nf / max_exact) / math.log(MAX_DISTANCE / max_exact)
                         * (half - max_exact)).astype(jnp.int32)
    large = jnp.minimum(large, half - 1)
    return ret + jnp.where(n < max_exact, n, large)

def diff_attention(q, k, v, lam, bias_table):
    B, S, H, _, d = q.shape
    nb = S // Q_BLOCK
    scale = d ** -0.5
    k1, k2 = k[:, :, :, 0], k[:, :, :, 1]
    qb = q.reshape(B, nb, Q_BLOCK, H, 2, d).transpose(1, 0, 2, 3, 4, 5)
    starts = jnp.arange(nb, dtype=jnp.int32) * Q_BLOCK
    kpos = jnp.arange(S, dtype=jnp.int32)

    def one_block(args):
        qblk, start = args
        qpos = start + jnp.arange(Q_BLOCK, dtype=jnp.int32)
        bias = bias_table[rel_bucket(kpos[None, :] - qpos[:, None])]
        bias = bias.astype(jnp.float32).transpose(2, 0, 1)[None]
        s1 = jnp.einsum('bqhd,bkhd->bhqk', qblk[:, :, :, 0], k1, preferred_element_type=jnp.float32) * scale + bias
        s2 = jnp.einsum('bqhd,bkhd->bhqk', qblk[:, :, :, 1], k2, preferred_element_type=jnp.float32) * scale + bias
        attn = jax.nn.softmax(s1, axis=-1) - lam * jax.nn.softmax(s2, axis=-1)
        return jnp.einsum('bhqk,bkhe->bqhe', attn.astype(v.dtype), v, preferred_element_type=jnp.float32)

    out = lax.map(one_block, (qb, starts))
    return out.transpose(1, 0, 2, 3, 4).reshape(B, S, H, v.shape[-1])

def dilated_group(q, k, v, window, dilation, bias_table):
    B, S, H, d = q.shape
    r = dilation
    hs = window // (2 * r)
    L = S // r
    n = -(-L // hs)
    Lp = n * hs
    scale = d ** -0.5

    def sub(t):
        return t.reshape(B, L, r, H, d).transpose(0, 2, 1, 3, 4)

    qs = jnp.pad(sub(q), ((0, 0), (0, 0), (0, Lp - L), (0, 0), (0, 0))).reshape(B, r, n, hs, H, d)
    pad_kv = ((0, 0), (0, 0), (hs, Lp - L + hs), (0, 0), (0, 0))
    kp = jnp.pad(sub(k), pad_kv).reshape(B, r, n + 2, hs, H, d)
    vp = jnp.pad(sub(v), pad_kv).reshape(B, r, n + 2, hs, H, d)
    kw = jnp.concatenate([kp[:, :, :-2], kp[:, :, 1:-1], kp[:, :, 2:]], axis=3)
    vw = jnp.concatenate([vp[:, :, :-2], vp[:, :, 1:-1], vp[:, :, 2:]], axis=3)
    rel_sub = jnp.arange(3 * hs, dtype=jnp.int32)[None, :] - hs - jnp.arange(hs, dtype=jnp.int32)[:, None]
    bias = bias_table[rel_bucket(r * rel_sub)].astype(jnp.float32).transpose(2, 0, 1)
    kj = jnp.arange(n, dtype=jnp.int32)[:, None] * hs + jnp.arange(3 * hs, dtype=jnp.int32)[None, :] - hs
    valid = (jnp.abs(rel_sub)[None] <= hs) & (kj[:, None, :] >= 0) & (kj[:, None, :] < L)
    s = jnp.einsum('brnqhd,brnkhd->brnhqk', qs, kw, preferred_element_type=jnp.float32) * scale + bias
    s = jnp.where(valid[None, None, :, None], s, NEG_BIG)
    m = jnp.max(s, axis=-1, keepdims=True)
    p = jnp.exp(s - m)
    den = jnp.sum(p, axis=-1, keepdims=True)
    o = jnp.einsum('brnhqk,brnkhd->brnhqd', p.astype(v.dtype), vw, preferred_element_type=jnp.float32) / den
    lse = (m + jnp.log(den))[..., 0]
    o = o.transpose(0, 1, 2, 4, 3, 5).reshape(B, r, Lp, H, d)[:, :, :L]
    o = o.transpose(0, 2, 1, 3, 4).reshape(B, S, H, d)
    lse = lse.transpose(0, 1, 2, 4, 3).reshape(B, r, Lp, H)[:, :, :L]
    lse = lse.transpose(0, 2, 1, 3).reshape(B, S, H)
    return o, lse

def token_mixers(h, layer, w_in, w_proj_a, w_proj_b, w_out,
                 lambda_q1, lambda_k1, lambda_q2, lambda_k2, g_subln, rel_bias):
    B, S, _ = h.shape
    p = h @ w_in
    cuts = np.cumsum([DA_QK, DA_QK, DA_V, DIL_QKV, DIL_QKV, DIL_QKV, D_MODEL]).tolist()
    qa, ka, va, qb, kb, vb, ga, gb = jnp.split(p, cuts, axis=-1)
    lam_init = 0.8 - 0.6 * math.exp(-0.3 * layer)
    lam = (jnp.exp(jnp.sum(lambda_q1.astype(jnp.float32) * lambda_k1.astype(jnp.float32)))
           - jnp.exp(jnp.sum(lambda_q2.astype(jnp.float32) * lambda_k2.astype(jnp.float32))) + lam_init)
    oa = diff_attention(qa.reshape(B, S, DA_HEADS, 2, DA_HEAD_DIM), ka.reshape(B, S, DA_HEADS, 2, DA_HEAD_DIM),
                        va.reshape(B, S, DA_HEADS, 2 * DA_HEAD_DIM), lam, rel_bias[:, :DA_HEADS])
    oa = rms_norm(oa, g_subln) * (1.0 - lam_init)
    oa = oa.reshape(B, S, DA_V).astype(h.dtype) @ w_proj_a
    G = len(DIL_GROUPS)
    qb = qb.reshape(B, S, G, DIL_HEADS, DIL_HEAD_DIM)
    kb = kb.reshape(B, S, G, DIL_HEADS, DIL_HEAD_DIM)
    vb = vb.reshape(B, S, G, DIL_HEADS, DIL_HEAD_DIM)
    outs, lses = [], []
    for gi, (window, dilation) in enumerate(DIL_GROUPS):
        cols = rel_bias[:, DA_HEADS + gi * DIL_HEADS: DA_HEADS + (gi + 1) * DIL_HEADS]
        o_g, lse_g = dilated_group(qb[:, :, gi], kb[:, :, gi], vb[:, :, gi], window, dilation, cols)
        outs.append(o_g)
        lses.append(lse_g)
    wts = jax.nn.softmax(jnp.stack(lses, axis=-1), axis=-1)
    ob = jnp.sum(jnp.stack(outs, axis=-1) * wts[:, :, :, None, :], axis=-1)
    ob = ob.reshape(B, S, DIL_OUT).astype(h.dtype) @ w_proj_b
    merged = jax.nn.sigmoid(ga) * oa + jax.nn.sigmoid(gb) * ob
    return merged @ w_out

def peer(h, w_query, sub_keys_1, sub_keys_2, expert_u, expert_v):
    B, S, D = h.shape
    xt = h.reshape((B * S) // TOK_CHUNK, TOK_CHUNK, D)

    def chunk(xc):
        q = (xc @ w_query).reshape(TOK_CHUNK, PEER_HEADS, 2, PEER_HALF)
        s1 = jnp.einsum('thd,hkd->thk', q[:, :, 0], sub_keys_1, preferred_element_type=jnp.float32)
        s2 = jnp.einsum('thd,hkd->thk', q[:, :, 1], sub_keys_2, preferred_element_type=jnp.float32)
        v1, i1 = lax.top_k(s1, PEER_TOPK)
        v2, i2 = lax.top_k(s2, PEER_TOPK)
        cand = (v1[..., :, None] + v2[..., None, :]).reshape(TOK_CHUNK, PEER_HEADS, PEER_TOPK * PEER_TOPK)
        vals, ids = lax.top_k(cand, PEER_TOPK)
        e1 = jnp.take_along_axis(i1, ids // PEER_TOPK, axis=-1)
        e2 = jnp.take_along_axis(i2, ids % PEER_TOPK, axis=-1)
        experts = e1 * N_KEYS + e2
        g = jax.nn.softmax(vals, axis=-1)
        u = jnp.take(expert_u, experts, axis=0)
        vv = jnp.take(expert_v, experts, axis=0)
        a = jax.nn.gelu(jnp.einsum('td,thkd->thk', xc, u, preferred_element_type=jnp.float32), approximate=False) * g
        return jnp.einsum('thk,thkd->td', a.astype(vv.dtype), vv, preferred_element_type=jnp.float32)

    return lax.map(chunk, xt).reshape(B, S, D)

def encoder(x, c, w_ada, b_ada, g_norm_mix, g_norm_ffn, w_in, w_proj_a, w_proj_b, w_out,
            lambda_q1, lambda_k1, lambda_q2, lambda_k2, g_subln, rel_bias,
            w_query, sub_keys_1, sub_keys_2, expert_u, expert_v, g_final):
    B = x.shape[0]
    for l in range(DEPTH):
        mod = (jax.nn.silu(c) @ w_ada[l] + b_ada[l]).reshape(B, 1, 6, D_MODEL)
        shift1, scale1, gate1 = mod[:, :, 0], mod[:, :, 1], mod[:, :, 2]
        shift2, scale2, gate2 = mod[:, :, 3], mod[:, :, 4], mod[:, :, 5]
        h = rms_norm(x, g_norm_mix[l]) * (1.0 + scale1) + shift1
        mix = token_mixers(h, l, w_in[l], w_proj_a[l], w_proj_b[l], w_out[l],
                           lambda_q1[l], lambda_k1[l], lambda_q2[l], lambda_k2[l], g_subln[l], rel_bias)
        x = x + (gate1 * mix).astype(x.dtype)
        h = rms_norm(x, g_norm_ffn[l]) * (1.0 + scale2) + shift2
        ff = peer(h, w_query[l], sub_keys_1[l], sub_keys_2[l], expert_u[l], expert_v[l])
        x = x + (gate2 * ff).astype(x.dtype)
    return rms_norm(x, g_final)

def setup_inputs(seed: int = 0) -> dict:
    key = jax.random.key(seed)
    ks = jax.random.split(key, 26)

    def nrm(k, shape, scale):
        return jax.random.normal(k, shape, jnp.float32) * scale

    D = D_MODEL
    return {
        'x_prompt': nrm(ks[0], (BATCH, SEQ, D), 1.0),
        'x_sample': nrm(ks[1], (DEC_BATCH, DEC_SEQ, D), 1.0),
        'c_prompt': nrm(ks[2], (BATCH, D), 1.0),
        'c_sample': nrm(ks[3], (DEC_BATCH, D), 1.0),
        'w_ada': nrm(ks[4], (DEPTH, D, 6 * D), 0.5 * D ** -0.5),
        'b_ada': nrm(ks[5], (DEPTH, 6 * D), 0.01),
        'g_norm_mix': 1.0 + nrm(ks[6], (DEPTH, D), 0.02),
        'g_norm_ffn': 1.0 + nrm(ks[7], (DEPTH, D), 0.02),
        'w_in': nrm(ks[8], (DEPTH, D, IN_COLS), D ** -0.5),
        'w_proj_a': nrm(ks[9], (DEPTH, DA_V, D), DA_V ** -0.5),
        'w_proj_b': nrm(ks[10], (DEPTH, DIL_OUT, D), DIL_OUT ** -0.5),
        'w_out': nrm(ks[11], (DEPTH, D, D), D ** -0.5),
        'lambda_q1': nrm(ks[12], (DEPTH, DA_HEAD_DIM), 0.1),
        'lambda_k1': nrm(ks[13], (DEPTH, DA_HEAD_DIM), 0.1),
        'lambda_q2': nrm(ks[14], (DEPTH, DA_HEAD_DIM), 0.1),
        'lambda_k2': nrm(ks[15], (DEPTH, DA_HEAD_DIM), 0.1),
        'g_subln': 1.0 + nrm(ks[16], (DEPTH, 2 * DA_HEAD_DIM), 0.02),
        'rel_bias': nrm(ks[17], (NUM_BUCKETS, N_REL_HEADS), 0.5),
        'w_query': nrm(ks[18], (DEPTH, D, PEER_HEADS * PEER_QUERY_DIM), D ** -0.5),
        'sub_keys_1': nrm(ks[19], (DEPTH, PEER_HEADS, N_KEYS, PEER_HALF), PEER_HALF ** -0.5),
        'sub_keys_2': nrm(ks[20], (DEPTH, PEER_HEADS, N_KEYS, PEER_HALF), PEER_HALF ** -0.5),
        'expert_u': nrm(ks[21], (DEPTH, N_EXPERTS, D), D ** -0.5),
        'expert_v': nrm(ks[22], (DEPTH, N_EXPERTS, D), 0.5),
        'g_final': 1.0 + nrm(ks[23], (D,), 0.02),
    }

def reference(x_prompt, x_sample, c_prompt, c_sample, w_ada, b_ada, g_norm_mix, g_norm_ffn,
              w_in, w_proj_a, w_proj_b, w_out, lambda_q1, lambda_k1, lambda_q2, lambda_k2,
              g_subln, rel_bias, w_query, sub_keys_1, sub_keys_2, expert_u, expert_v, g_final):
    y_prompt = encoder(x_prompt, c_prompt, w_ada, b_ada, g_norm_mix, g_norm_ffn, w_in, w_proj_a, w_proj_b, w_out,
                       lambda_q1, lambda_k1, lambda_q2, lambda_k2, g_subln, rel_bias,
                       w_query, sub_keys_1, sub_keys_2, expert_u, expert_v, g_final)
    y_sample = encoder(x_sample, c_sample, w_ada, b_ada, g_norm_mix, g_norm_ffn, w_in, w_proj_a, w_proj_b, w_out,
                       lambda_q1, lambda_k1, lambda_q2, lambda_k2, g_subln, rel_bias,
                       w_query, sub_keys_1, sub_keys_2, expert_u, expert_v, g_final)
    return (y_prompt, y_sample)


_drawn_inputs = setup_inputs


def setup_inputs(seed=0):
    import zlib

    import numpy as np

    out = dict(_drawn_inputs(seed))
    spreads = {}
    factors = {'b_ada': 4.469,
     'g_norm_mix': 8.0,
     'g_norm_ffn': 12.526,
     'lambda_q1': 6.569,
     'lambda_k1': 3.42,
     'lambda_q2': 64.0,
     'lambda_k2': 6.376,
     'g_subln': 27.91,
     'g_final': 8.152}
    for name, (base, spread) in spreads.items():
        noise = np.random.default_rng([zlib.crc32(name.encode()), seed]).standard_normal(out[name].shape)
        drawn = base * np.exp(spread * noise) if base else spread * noise
        out[name] = __import__('jax').numpy.asarray(drawn.astype(out[name].dtype))
    for name, factor in factors.items():
        out[name] = (out[name] * factor).astype(out[name].dtype)
    return out
```

```python
import math
from contextlib import ExitStack, contextmanager

import numpy as np

import concourse.bass as bass
from concourse import mybir

F32 = mybir.dt.float32
U32 = mybir.dt.uint32
ALU = mybir.AluOpType
ACT = mybir.ActivationFunctionType
AX_X = mybir.AxisListType.X
ds = bass.ds

P = 128
D = 1024
C = D // P
F = 512
NT = F // P
SEQS = 2
HEADS = 8
DH = 64
GROUPS = ((128, 1), (512, 4), (2048, 16))
PAIRS = HEADS // 2
BUCKETS = 32
MAX_DISTANCE = 1024
BIAS_ROWS = HEADS * (1 + len(GROUPS))
K16 = 16
SLOTS = HEADS * K16
GS = 4
GPT = SLOTS // GS
EPS = 1e-6
MASKED = -1e30
LOWEST = -3e38
LAM_INIT = 0.8 - 0.6 * math.exp(0.0)

W_FREE = 28 * P
WADA_COLS = 384
WADA_SLABS = 6 * D // WADA_COLS

Z_WIDE = 896
Z_BAND = 384
Z_PAIR = Z_BAND + 2 * Z_WIDE
SC_FREE = 2 * F + Z_BAND
R_Z = 0
R_SC = R_Z + 2 * Z_PAIR
R_PT = R_SC + 2 * SC_FREE
R_QKV = R_PT + 2 * SC_FREE
R_END = R_QKV + 9 * F
R_MOD, R_BADA, R_ONEHOT, R_MASK = 0, 6 * D, 12 * D, 13 * D
R_RT, R_SQ = R_SC, R_SC + F
R_GATE = R_SC
R_MERGED = R_PT
R_X1T = R_Z
R_XR = R_SC
R_STAGE = R_SC + 3 * F
R_ROUTE = R_STAGE + 2 * D


class Tally:

    def __init__(self):
        self.start, self.step = 0, 0

    @property
    def n(self):
        return self.start + self.step

    def up(self, k=1):
        self.step += k


@contextmanager
def turns(eng, count, tallies, per_turn):
    assert set(per_turn) <= set(tallies)
    starts = {t: tallies[t].n for t in tallies}
    with eng.Fori(0, count) as i:
        for t in tallies:
            k = per_turn.get(t, 0)
            tallies[t].start = i * k + starts[t] if k else starts[t]
            tallies[t].step = 0
        yield i
        for t in tallies:
            assert tallies[t].step == per_turn.get(t, 0), (t, tallies[t].step, per_turn.get(t, 0))
    for t in tallies:
        tallies[t].start, tallies[t].step = starts[t] + count * per_turn.get(t, 0), 0


def key_tiles(tile):
    return range(max(tile - 1, 0), min(tile + 2, NT))


class Hooks:

    def __init__(self, gather, seq):
        self.gather, self.seq = gather, seq

    def begin(self, tile):
        if self.gather:
            n = NT * self.seq + tile
            self.gather[0](n, tile % 2, n // 2 + 1)

    def front(self, group, tile):
        if self.gather:
            self.gather[1]((NT * self.seq + tile) * GPT + group, group, tile % 2)

    def back(self, group, tile):
        if self.gather:
            self.gather[2]((NT * self.seq + tile) * GPT + group, group, tile % 2)

    def end(self, tile):
        if self.gather:
            self.gather[3](NT * self.seq + tile, self.seq, tile)


def gather_alone(eng, gather, tallies, per_turn):
    begin, front, back, end = gather
    seq = SEQS - 1
    with turns(eng, NT // 2, tallies, per_turn) as i:
        for b in range(2):
            tile = 2 * i + (NT * seq + b)
            begin(tile, b, i + (NT * seq // 2 + 1))
            with eng.Fori(0, GPT) as group:
                front(tile * GPT + group, group, b)
                back(tile * GPT + group, group, b)
            end(tile, seq, 2 * i + b)


def build(nc, ins, y):
    es = ExitStack()
    with es:
        def sb(name, shape, dt=F32):
            return es.enter_context(nc.sbuf_tensor(name, shape, dt))

        def sem(name):
            return es.enter_context(nc.semaphore(name))

        def scratch(name, shape, dt=F32):
            return nc.dram_tensor(name, shape, dt, kind="Internal").ap()

        bias_d = scratch("bias_rows", [BIAS_ROWS, 2 * F])
        gate2_d = scratch("gate2_rows", [SEQS, P, D])
        x1_d = scratch("x1_tiles", [SEQS * NT, P, D])
        h2_d = scratch("h2_tiles", [SEQS * NT, P, D])
        experts_d = scratch("experts", [SEQS * NT, P, SLOTS], U32)
        shares_d = scratch("shares", [SEQS * NT, P, SLOTS])

        hT = sb("hT", [P, C, F])
        oaT = sb("oaT", [P, HEADS, F])
        obT = sb("obT", [P, PAIRS, F])
        region = sb("region", [P, R_END])
        w = sb("w", [P, 2, W_FREE])
        urows = sb("urows", [P, GS, D])
        vrows = sb("vrows", [P, GS, D])
        h2_tile = sb("h2_tile", [P, 2, D])
        x1_tile = sb("x1_tile", [P, D])
        gate2 = sb("gate2", [P, D])
        gfin = sb("gfin", [P, D])
        vsum = sb("vsum", [P, F])
        vdiag = sb("vdiag", [P, GS, P])
        experts = sb("experts_tile", [P, 2, SLOTS], U32)
        shares = sb("shares_tile", [P, 2, SLOTS])
        now = sb("experts_now", [P, 2, GS], U32)
        dots = sb("dots", [P, GS])
        gelus = sb("gelus", [P, GS])
        weights = sb("weights", [P, GS])
        fstat = sb("fstat", [P, 4])
        ident = sb("ident", [P, P])
        flip = sb("flip", [P, P])
        ones = sb("ones", [P, P])
        zeros = sb("zeros", [P, P])
        eps = sb("eps", [P, 1])
        pdiag = sb("pdiag", [P, 2, 2, P])
        mx = sb("mx", [P, 2, 4])
        nm = sb("nm", [P, 2, 2])
        den = sb("den", [P, 2, 2])
        rden = sb("rden", [P, 2, 2])
        cvec = sb("cvec", [P, C, SEQS])
        gmix = sb("gmix", [P, C])
        gffn = sb("gffn", [P, C])
        gsub = sb("gsub", [P, 1])
        lamv = sb("lamv", [P, 4, DH])
        lam = sb("lam", [P, 4])
        mixsign = sb("mixsign", [P, 2])
        relb = sb("relb", [BUCKETS, BIAS_ROWS])
        pick = sb("pick", [SEQS, SEQS * P])
        modT = sb("modT", [P, 6 * C, SEQS])
        scale1 = sb("scale1", [P, SEQS, C])
        scale2 = sb("scale2", [P, SEQS, C])
        iota16 = sb("iota16", [P, K16])
        chosen = sb("chosen", [P, 2, NT * K16], U32)
        share = sb("share", [P, 2, NT * K16])
        pad = sb("pad", [1, 64])
        pad_a = sb("pad_a", [P, 1])
        pad_p = sb("pad_p", [1, 128])
        turn_of = {pad.name: 0, pad_p.name: 0}

        def spare(scrap):
            turn_of[scrap.name] = (turn_of[scrap.name] + 1) % scrap.shape[1]
            return scrap[:, turn_of[scrap.name]:turn_of[scrap.name] + 1]

        def reg(at, size):
            return region[:, at:at + size]

        zbuf = [reg(R_Z + j * Z_PAIR, Z_PAIR) for j in range(2)]
        scores_sb = [reg(R_SC + j * SC_FREE, SC_FREE) for j in range(2)]
        probsT = [reg(R_PT + j * SC_FREE, SC_FREE) for j in range(2)]
        qkv = [[reg(R_QKV + (3 * g + x) * F, F) for x in range(3)] for g in range(3)]
        o_square, o_root = probsT[1][:, F:2 * F], probsT[0][:, F:2 * F]
        mod = region[0:SEQS, R_MOD:R_MOD + 6 * D]
        b_ada = region[0:SEQS, R_BADA:R_BADA + 6 * D]
        onehot = region[0:BUCKETS, R_ONEHOT:R_ONEHOT + 2 * F]
        mask = region[0:BIAS_ROWS, R_MASK:R_MASK + 2 * F]
        root = reg(R_RT, F)
        square = [reg(R_SQ + j * F, F) for j in range(2)]
        gate_sb = [reg(R_GATE + j * F, F) for j in range(4)]
        merged = reg(R_MERGED, C * F).rearrange("p (c f) -> p c f", c=C)
        x1T = reg(R_X1T, C * F).rearrange("p (c f) -> p c f", c=C)
        xr = [reg(R_XR + j * F, F) for j in range(2)]
        stage = [reg(R_STAGE + j * D, D) for j in range(2)]
        at = R_ROUTE

        def route(size, dt=F32):
            nonlocal at
            at += size
            assert at <= R_END
            r = region[:, at - size:at]
            return r if dt == F32 else r.bitcast(dt)

        TK = NT * K16
        qhalf = [route(F) for _ in range(2)]
        topv = [route(TK).rearrange("p (t k) -> p t k", k=K16) for _ in range(2)]
        topi = [route(TK, U32).rearrange("p (t k) -> p t k", k=K16) for _ in range(2)]
        topf = [route(TK) for _ in range(2)]
        rest = route(F).rearrange("p (t k) -> p t k", k=P)
        cand = route(NT * 256).rearrange("p (t k) -> p t k", k=256)
        cand2 = route(NT * 256).rearrange("p (t k) -> p t k", k=256)
        candv = route(TK).rearrange("p (t k) -> p t k", k=K16)
        candi = route(TK, U32).rearrange("p (t k) -> p t k", k=K16)
        parti = [route(TK, U32) for _ in range(2)]
        partf = [route(TK) for _ in range(2)]
        hot = cand.rearrange("p t k -> p (t k)")
        hot2 = cand2.rearrange("p t k -> p (t k)")
        keyno = [route(TK) for _ in range(2)]
        expert_f = route(TK)
        gap = route(TK)
        gexp = route(TK)
        gsum = route(NT)
        grec = route(NT)

        class Bank:
            def __init__(self, name):
                self.t = es.enter_context(nc.psum_tensor(name, [P, F], F32))
                self.filled, self.emptied = sem(name + "_filled"), sem(name + "_emptied")

            def __getitem__(self, i):
                return self.t[i]

        PA, XA = Bank("bank_pa"), Bank("bank_xa")
        PV, XV = Bank("bank_pv"), Bank("bank_xv")
        S = [Bank("bank_s0"), Bank("bank_s1")]
        O, G = Bank("bank_o"), Bank("bank_g")
        BANKS = [PA, XA, PV, XV, *S, O, G]

        consts_in = sem("consts_in")
        consts_set = sem("consts_set")
        silu_done = sem("silu_done")
        lam_exp = sem("lam_exp")
        mod_ready = sem("mod_ready")
        rows_ready = sem("rows_ready")
        rows_out = sem("rows_out")
        setup_done = sem("setup_done")
        slab_in = [sem(f"slab_in{j}") for j in range(2)]
        slab_begun = sem("slab_begun")
        x_in = sem("x_in")
        z_in = [sem(f"z_in{j}") for j in range(2)]
        z_read = [sem(f"z_read{j}") for j in range(2)]
        step = sem("dve_step")
        squared = sem("squared")
        square_read = sem("square_read")
        h_ready = sem("h_ready")
        maxed = sem("maxed")
        exped = sem("exped")
        diag_ready = sem("diag_ready")
        o_squared = sem("o_squared")
        oa_ready = sem("oa_ready")
        gated = sem("gated")
        xr_in = [sem(f"xr_in{j}") for j in range(2)]
        x1_ready = sem("x1_ready")
        staged_a = sem("staged_a")
        staged_v = sem("staged_v")
        stage_out = [sem(f"stage_out{j}") for j in range(2)]
        gap_ready = sem("gap_ready")
        gap_exped = sem("gap_exped")
        record_ready = sem("record_ready")
        record_out = [sem(f"record_out{j}") for j in range(2)]
        tile_in = [sem(f"tile_in{j}") for j in range(2)]
        now_set = sem("now_set")
        u_in = [sem(f"u_in{k}") for k in range(GS)]
        v_in = [sem(f"v_in{k}") for k in range(GS)]
        u_read = [sem(f"u_read{k}") for k in range(GS)]
        v_read_pe = [sem(f"v_read_pe{k}") for k in range(GS)]
        v_read_dve = [sem(f"v_read_dve{k}") for k in range(GS)]
        gelu_done = sem("gelu_done")
        weighed = sem("weighed")
        vdiag_ready = sem("vdiag_ready")
        final_in = sem("final_in")
        fsum_ready = sem("fsum_ready")
        froot_ready = sem("froot_ready")
        y_ready = sem("y_ready")
        y_out = sem("y_out")

        S1_PER_SEQ = NT * HEADS + PAIRS * 12 + HEADS

        Z_PER_SEQ = 16 * (HEADS // 2) * (1 + len(GROUPS))

        block = es.enter_context(nc.Block())

        @block.sync
        def _(sp):
            t = {"slab": Tally(), "xr": Tally(), "z0": Tally(), "z1": Tally()}
            for dst, name in ((cvec[:, :, :], "c_t"), (gmix[:, :], "g_mix"), (gffn[:, :], "g_ffn"),
                              (gsub[:, :], "g_sub"), (lamv[:, :, :], "lambdas"), (relb[:, :], "rel_bias"),
                              (pick[:, :], "pick"), (ident[:, :], "ident"), (flip[:, :], "flip"), (iota16[:, :], "iota16"),
                              (b_ada, "b_ada"), (onehot, "onehot"), (mask, "mask"), (gfin[:, :], "g_final")):
                sp.dma_start(dst, ins[name]).then_inc(consts_in, 16)

            def slab(name, index, j, width):
                sp.wait_ge(slab_begun, t["slab"].n)
                sp.dma_start(w[:, j, 0:width], ins[name][ds(index, 1), :, :].rearrange("a p n -> (a p) n"))\
                    .then_inc(slab_in[j], 16)
                t["slab"].up()

            with turns(sp, WADA_SLABS // 2, t, {"slab": 2}) as i:
                for j in range(2):
                    slab("w_ada", 2 * i + j, j, C * WADA_COLS)

            sp.wait_ge(rows_ready, 1)
            sp.dma_start(bias_d, oaT[0:BIAS_ROWS, 0:2, :].rearrange("p a f -> p (a f)")).then_inc(rows_out, 16)
            for s in range(SEQS):
                sp.dma_start(gate2_d[s], oaT[:, 2 + 2 * s:4 + 2 * s, :].rearrange("p a f -> p (a f)"))\
                    .then_inc(rows_out, 16)
            sp.wait_ge(rows_out, 48)

            def z_load(j, row, start, width, at):
                src = bass.AP(tensor=bias_d.tensor, offset=row * 2 * F + (start - 384 + F - (P - 1)),
                              ap=[[1, P], [1, width]])
                sp.dma_start(zbuf[j][:, at:at + width], src).then_inc(z_in[j], 16)

            for s in range(SEQS):
                if s == 0:
                    sp.wait_ge(setup_done, 1)
                else:
                    sp.wait_ge(S[1].filled, s * S1_PER_SEQ)
                sp.dma_start(hT[:, :, :], ins["x_t"][s]).then_inc(x_in, 16)
                with turns(sp, HEADS // 2, t, {"slab": 2, "z0": 1, "z1": 1}) as i:
                    for j in range(2):
                        sp.wait_ge(z_read[j], t[f"z{j}"].n)
                        t[f"z{j}"].up()
                        z_load(j, 2 * i + j, 0, Z_WIDE, 0)
                        slab("w_heads", 2 * i + j, j, C * 3 * P)
                with turns(sp, PAIRS // 2, t, {"slab": 6, "z0": 2, "z1": 2}) as i:
                    for b in range(2):
                        for j in range(2):
                            sp.wait_ge(z_read[j], t[f"z{j}"].n)
                            t[f"z{j}"].up()
                            for g in range(3):
                                row = HEADS + g * HEADS + 2 * b + j + i * 4
                                z_load(j, row, *((256, Z_BAND, 2 * Z_WIDE) if g == 0 else (0, Z_WIDE, (g - 1) * Z_WIDE)))
                        for g in range(3):
                            slab("w_heads", HEADS + 6 * i + 3 * b + g, (3 * b + g) % 2, C * 3 * P)
                with turns(sp, C // 2, t, {"slab": 2}) as i:
                    for j in range(2):
                        slab("w_merge", 2 * i + j, j, 28 * P)
                sp.wait_ge(gated, C * (s + 1))
                with turns(sp, C // 2, t, {"slab": 2, "xr": 2}) as i:
                    for j in range(2):
                        slab("w_out", 2 * i + j, j, C * P)
                        sp.wait_ge(x1_ready, t["xr"].n - j)
                        sp.dma_start(xr[j], ins["x_t"][s, :, ds(2 * i + j, 1), :].rearrange("p a f -> p (a f)"))\
                            .then_inc(xr_in[j], 16)
                        t["xr"].up()
                for tile in range(NT):
                    for which, dst in ((0, x1_d), (1, h2_d)):
                        n = 2 * (NT * s + tile) + which + 1
                        sp.wait_ge(staged_a, n)
                        sp.wait_ge(staged_v, n)
                        sp.dma_start(dst[NT * s + tile], stage[which]).then_inc(stage_out[which], 16)

                def query_slabs(head):
                    for j in range(2):
                        slab("w_query", 2 * head + j, j, (C + 1) * P)

                def store_record(head, b):
                    sp.wait_ge(record_ready, s * HEADS + head + 1)
                    for dst, src in ((experts_d, chosen), (shares_d, share)):
                        sp.dma_start(
                            dst[s * NT:(s + 1) * NT, :, ds(head * K16, K16)].rearrange("t p k -> p t k"),
                            src[:, b, :].rearrange("p (t k) -> p t k", k=K16)).then_inc(record_out[b], 16)

                query_slabs(0)
                with turns(sp, HEADS // 2 - 1, t, {"slab": 4}) as i:
                    for b in range(2):
                        query_slabs(2 * i + b + 1)
                        store_record(2 * i + b, b)
                query_slabs(HEADS - 1)
                store_record(HEADS - 2, 0)
                store_record(HEADS - 1, 1)

        @block.gpsimd
        def _(pool):
            def fence():
                pool.tensor_tensor(spare(pad_p), zeros[0:1, 0:1], zeros[0:1, 0:1], ALU.add)

            pool.memset(ones[:, :], 1.0)
            pool.memset(zeros[:, :], 0.0)
            pool.memset(eps[:, :], EPS).then_inc(consts_set, 1)
            pool.wait_ge(consts_set, 1)
            for s in range(SEQS):
                for j in range(2):
                    pool.wait_ge(stage_out[j], 16 * NT * (s + 1))
                    pool.wait_ge(record_out[j], 16 * HEADS * (s + 1))
                with pool.Fori(0, NT // 2) as i:
                    for b in range(2):
                        tile = NT * s + 2 * i + b
                        for dst, src in ((experts[:, b, :], experts_d), (shares[:, b, :], shares_d),
                                         (h2_tile[:, b, :], h2_d)):
                            pool.dma_start(dst, src[ds(tile, 1), :, :].rearrange("a p n -> (a p) n"))\
                                .then_inc(tile_in[b], 16)
                        pool.wait_ge(tile_in[b], (NT // 2 * s + i + 1) * 48)
                        fence()
                        with pool.Fori(0, GPT // 2) as g:
                            for h in range(2):
                                n = tile * GPT + 2 * g + h
                                pool.tensor_copy(now[:, h, :], experts[:, b, ds((2 * g + h) * GS, GS)])\
                                    .then_inc(now_set, 1)
                                pool.wait_ge(now_set, n + 1)
                                for k in range(GS):
                                    pool.wait_ge(u_read[k], n)
                                    fence()
                                    pool.indirect_dma_start(
                                        out=urows[:, k, :], out_offset=None, in_=ins["expert_u"],
                                        in_offset=bass.IndirectOffsetOnAxis(ap=now[:, h, k:k + 1], axis=0))\
                                        .then_inc(u_in[k], 16)
                                for k in range(GS):
                                    pool.wait_ge(v_read_pe[k], n)
                                    pool.wait_ge(v_read_dve[k], n)
                                    fence()
                                    pool.indirect_dma_start(
                                        out=vrows[:, k, :], out_offset=None, in_=ins["expert_v"],
                                        in_offset=bass.IndirectOffsetOnAxis(ap=now[:, h, k:k + 1], axis=0))\
                                        .then_inc(v_in[k], 16)
                        pool.wait_ge(y_out, tile * 16)
                        fence()
                        pool.dma_start(x1_tile[:, :], x1_d[ds(tile, 1), :, :].rearrange("a p n -> (a p) n"))\
                            .then_inc(final_in, 16)
                        pool.dma_start(gate2[:, :], gate2_d[s]).then_inc(final_in, 16)

        @block.tensor
        def _(pe):
            used = {b: Tally() for b in BANKS}
            t = {**used, "slab": Tally(), "diag": Tally(), "osq": Tally()}
            slabs = t["slab"]

            def product(bank, j, lhsT, rhs, n, out=None, first=False, last=True):
                out = bank[:, :] if out is None else out
                for c in range(n):
                    mm = pe.matmul(out, lhsT(c), rhs(c), start=(c == 0), stop=(c == n - 1))
                    if first and c == 0:
                        mm.then_inc(slab_begun, 1)
                if last:
                    mm.then_inc(bank.filled, 1)
                    used[bank].up()

            pe.wait_ge(consts_in, 14 * 16)
            pe.wait_ge(consts_set, 1)
            pe.wait_ge(silu_done, 1)
            with turns(pe, WADA_SLABS // 2, t, {"slab": 2, PV: 1, XV: 1}) as i:
                for j, bank in ((0, PV), (1, XV)):
                    pe.wait_ge(slab_in[j], 16 * (i + 1))
                    pe.wait_ge(bank.emptied, used[bank].n)
                    product(bank, j, lambda c: cvec[:, c, :],
                            lambda c: w[:, j, c * WADA_COLS:(c + 1) * WADA_COLS], C,
                            out=bank[0:SEQS, 0:WADA_COLS], first=True)
                    slabs.up()
            pe.wait_ge(mod_ready, WADA_SLABS)
            pe.wait_ge(PV.emptied, used[PV].n)
            for c in range(6 * C):
                mm = pe.transpose(PV[:, SEQS * c:SEQS * (c + 1)], mod[:, c * P:(c + 1) * P],
                                  ident[0:SEQS, 0:SEQS])
            mm.then_inc(PV.filled, 1)
            used[PV].up()
            for s in range(SEQS):
                for half, bank in ((0, XV), (1, PV)):
                    pe.wait_ge(bank.emptied, used[bank].n)
                    pe.matmul(bank[:, :], pick[:, s * P:(s + 1) * P],
                              mod[:, 5 * D + half * F:5 * D + (half + 1) * F], start=True, stop=True)\
                        .then_inc(bank.filled, 1)
                    used[bank].up()
            for half, bank in ((0, XV), (1, PV)):
                pe.wait_ge(bank.emptied, used[bank].n)
                pe.matmul(bank[0:BIAS_ROWS, :], relb[:, :], onehot[:, half * F:(half + 1) * F],
                          start=True, stop=True).then_inc(bank.filled, 1)
                used[bank].up()

            def gather_begin(tile, b, turn):
                pe.wait_ge(G.emptied, tile)
                pe.matmul(G[:, :], zeros[:, :], gfin[:, 0:F], start=True, stop=False, skip_group_check=True)

            def gather_front(n, group, b):
                pass

            def gather_back(n, group, b):
                for k in range(GS):
                    pe.wait_ge(vdiag_ready, n * GS + k + 1)
                    pe.wait_ge(v_in[k], (n + 1) * 16)
                    pe.matmul(G[:, :], vdiag[:, k, :], vrows[:, k, 0:F], start=False, stop=False,
                              skip_group_check=True).then_inc(v_read_pe[k], 1)

            def gather_end(tile, s, row):
                pe.matmul(G[:, :], zeros[:, :], gfin[:, 0:F], start=False, stop=True, skip_group_check=True)\
                    .then_inc(G.filled, 1)

            gather = (gather_begin, gather_front, gather_back, gather_end)

            def squares_sum(s, which):
                pe.wait_ge(PA.emptied, used[PA].n)
                for c in range(C):
                    pe.wait_ge(squared, (2 * s + which) * C + c + 1)
                    pe.matmul(PA[:, :], ones[:, :], square[c % 2], start=(c == 0), stop=(c == C - 1))\
                        .then_inc(square_read if c < C - 1 else PA.filled, 1)
                used[PA].up()

            def project(turn, j, g):
                pe.wait_ge(slab_in[j], 16 * turn)
                for x, bank in ((0, PA), (1, PV)):
                    pe.wait_ge(bank.emptied, used[bank].n)
                    product(bank, j, lambda c: w[:, j, (3 * c + x) * P:(3 * c + x + 1) * P],
                            lambda c: hT[:, c, :], C, first=(x == 0))
                pe.wait_ge(XA.emptied, used[XA].n)
                for tile in range(NT):
                    product(XA, j, lambda c: hT[:, c, tile * P:(tile + 1) * P],
                            lambda c: w[:, j, (3 * c + 2) * P:(3 * c + 3) * P], C,
                            out=XA[:, tile * P:(tile + 1) * P], last=(tile == NT - 1))
                slabs.up()

            def attend(s, hooks):
                nonlocal slab_base
                squares_sum(s, 0)
                pe.wait_ge(h_ready, 2 * C * s + C)

                hook = Hooks(hooks, s - 1)
                hook.begin(0)
                base = slab_base // 2
                with turns(pe, HEADS // 2, t, {"slab": 2, PA: 4, PV: 2, XA: 6, XV: 4, S[0]: 8, S[1]: 8, O: 2,
                                               "diag": 8, "osq": 2}) as i:
                    for j in range(2):
                        project(base + i + 1, j, 0)
                        q, k, v = qkv[0]

                        def scores(tile):
                            for x in range(2):
                                pe.wait_ge(S[x].emptied, used[S[x]].n)
                                rows = slice(x * DH, (x + 1) * DH)
                                pe.matmul(S[x][:, :], q[rows, tile * P:(tile + 1) * P], k[rows, :],
                                          start=True, stop=True).then_inc(S[x].filled, 1)
                                used[S[x]].up()

                        def transposes(tile):
                            bank = (XA, XV)[tile % 2]
                            pe.wait_ge(bank.emptied, used[bank].n)
                            pe.wait_ge(diag_ready, t["diag"].n + 1)
                            t["diag"].up()
                            for kt in range(NT):
                                for x in range(2):
                                    mm = pe.matmul(bank[:, kt * P:(kt + 1) * P],
                                                   scores_sb[tile % 2][:, x * F + kt * P:x * F + (kt + 1) * P],
                                                   pdiag[:, tile % 2, x, :], start=(x == 0), stop=(x == 1))
                            mm.then_inc(bank.filled, 1)
                            used[bank].up()

                        def weigh(tile):
                            bank = (XA, XV)[tile % 2]
                            pe.wait_ge(bank.emptied, evac[tile])
                            if tile == 0:
                                pe.wait_ge(O.emptied, used[O].n)
                            for kt in range(NT):
                                mm = pe.matmul(O[:, tile * P:(tile + 1) * P], v[:, kt * P:(kt + 1) * P],
                                               probsT[tile % 2][:, kt * P:(kt + 1) * P],
                                               start=(kt == 0), stop=(kt == NT - 1))
                            if tile == NT - 1:
                                mm.then_inc(O.filled, 1)
                                used[O].up()

                        evac = {}
                        pe.wait_ge(PA.emptied, used[PA].n)
                        pe.wait_ge(PV.emptied, used[PV].n)
                        scores(0)
                        for tile in range(NT):
                            if tile + 1 < NT:
                                scores(tile + 1)
                            if tile == 0:
                                pe.wait_ge(XA.emptied, used[XA].n)
                            else:
                                weigh(tile - 1)
                            transposes(tile)
                            evac[tile] = used[(XA, XV)[tile % 2]].n
                            hook.back(i * 8 + (NT * j + tile), 0)
                        weigh(NT - 1)
                        pe.wait_ge(o_squared, t["osq"].n + 1)
                        t["osq"].up()
                        pe.wait_ge(PA.emptied, used[PA].n)
                        pe.matmul(PA[:, :], ones[:, :], o_square, start=True, stop=True).then_inc(PA.filled, 1)
                        used[PA].up()
                slab_base += HEADS
                hook.end(0)

                hook.begin(1)
                base = slab_base // 2
                with turns(pe, PAIRS // 2, t, {"slab": 6, PA: 6, PV: 6, XA: 38, XV: 16, S[0]: 24, S[1]: 24, O: 4,
                                               "diag": 16}) as i:
                    for b in range(2):
                        for g in range(3):
                            at = 3 * b + g
                            project(base + 3 * i + at // 2 + 1, at % 2, g)
                            if g == 2:
                                pe.wait_ge(PA.emptied, used[PA].n)
                                pe.wait_ge(PV.emptied, used[PV].n)
                            qkv_in = used[XA].n

                        def scores(u):
                            j, tile = divmod(u, NT)
                            rows = slice(j * DH, (j + 1) * DH)
                            for x, g in enumerate((1, 2, 0)):
                                bank = S[(3 * u + x) % 2]
                                kts = key_tiles(tile) if g == 0 else range(NT)
                                cols = slice(kts[0] * P, (kts[-1] + 1) * P)
                                pe.wait_ge(bank.emptied, used[bank].n)
                                pe.matmul(bank[:, 0:len(kts) * P], qkv[g][0][rows, tile * P:(tile + 1) * P],
                                          qkv[g][1][rows, cols], start=True, stop=True).then_inc(bank.filled, 1)
                                used[bank].up()

                        def transposes(u):
                            tile = u % NT
                            pe.wait_ge(diag_ready, t["diag"].n + 1)
                            t["diag"].up()
                            for bank, col, n in ((XA, 0, NT), (XV, F, NT), (XA, 2 * F, len(key_tiles(tile)))):
                                pe.wait_ge(bank.emptied, used[bank].n)
                                for kt in range(n):
                                    mm = pe.matmul(bank[:, kt * P:(kt + 1) * P],
                                                   scores_sb[u % 2][:, col + kt * P:col + (kt + 1) * P],
                                                   pdiag[:, u % 2, 0, :], start=True, stop=True)
                                mm.then_inc(bank.filled, 1)
                                used[bank].up()

                        def weigh(u):
                            j, tile = divmod(u, NT)
                            pe.wait_ge(XA.emptied, evac[u][0])
                            pe.wait_ge(XV.emptied, evac[u][1])
                            if tile == 0:
                                pe.wait_ge(O.emptied, used[O].n)
                            blocks = [(1, kt, kt) for kt in range(NT)] + [(2, kt, NT + kt) for kt in range(NT)]
                            blocks += [(0, kt, 2 * NT + n) for n, kt in enumerate(key_tiles(tile))]
                            for n, (g, kt, col) in enumerate(blocks):
                                mm = pe.matmul(O[:, tile * P:(tile + 1) * P], qkv[g][2][:, kt * P:(kt + 1) * P],
                                               probsT[u % 2][:, col * P:(col + 1) * P],
                                               start=(n == 0), stop=(n == len(blocks) - 1))
                            if tile == NT - 1:
                                mm.then_inc(O.filled, 1)
                                used[O].up()

                        evac = {}
                        scores(0)
                        for u in range(2 * NT):
                            if u + 1 < 2 * NT:
                                scores(u + 1)
                            if u == 0:
                                pe.wait_ge(XA.emptied, qkv_in)
                            else:
                                weigh(u - 1)
                            transposes(u)
                            evac[u] = used[XA].n, used[XV].n
                            hook.back(i * 16 + (8 * b + u), 1)
                        weigh(2 * NT - 1)
                slab_base += 3 * PAIRS
                hook.end(1)

                hook.begin(2)
                base = slab_base // 2
                pe.wait_ge(oa_ready, HEADS * (s + 1))
                pe.wait_ge(O.emptied, used[O].n)
                with turns(pe, C // 2, t, {"slab": 2, PA: 2, XA: 2, PV: 2, XV: 2}) as i:
                    for j in range(2):
                        pe.wait_ge(slab_in[j], 16 * (base + i + 1))
                        for bank, first, n, rhs in ((PA, 0, C, hT), (XA, C, C, hT), (PV, 2 * C, C, oaT),
                                                    (XV, 3 * C, PAIRS, obT)):
                            pe.wait_ge(bank.emptied, used[bank].n)
                            product(bank, j, lambda c: w[:, j, (first + c) * P:(first + c + 1) * P],
                                    lambda c: rhs[:, c, :], n, first=(first == 0))
                        slabs.up()
                        for x in range(2):
                            hook.back(i * 4 + (2 * j + x), 2)
                slab_base += C

                base = slab_base // 2
                pe.wait_ge(gated, C * (s + 1))
                with turns(pe, C // 2, t, {"slab": 2, PV: 2}) as i:
                    for j in range(2):
                        pe.wait_ge(slab_in[j], 16 * (base + i + 1))
                        pe.wait_ge(PV.emptied, used[PV].n)
                        product(PV, j, lambda c: w[:, j, c * P:(c + 1) * P], lambda c: merged[:, c, :], C,
                                first=True)
                        slabs.up()
                        for x in range(2):
                            hook.back(i * 4 + (16 + 2 * j + x), 2)
                slab_base += C
                hook.end(2)

                squares_sum(s, 1)
                pe.wait_ge(h_ready, 2 * C * s + 2 * C)
                for tile in range(NT):
                    for src in (x1T, hT):
                        for bank, first in ((XA, 0), (XV, NT)):
                            pe.wait_ge(bank.emptied, used[bank].n)
                            for c in range(4):
                                mm = pe.transpose(bank[:, c * P:(c + 1) * P],
                                                  src[:, first + c, tile * P:(tile + 1) * P], ident[:, :])
                            mm.then_inc(bank.filled, 1)
                            used[bank].up()

                hook.begin(3)
                base = slab_base // 2
                with turns(pe, HEADS // 2, t, {"slab": 4, PA: 2, XA: 2, S[0]: 2, S[1]: 2}) as i:
                    for b in range(2):
                        for j, bank in ((0, PA), (1, XA)):
                            pe.wait_ge(slab_in[j], 16 * (base + 2 * i + b + 1))
                            pe.wait_ge(bank.emptied, used[bank].n)
                            product(bank, j, lambda c: w[:, j, c * P:(c + 1) * P], lambda c: hT[:, c, :], C,
                                    first=(j == 0))
                            slabs.up()
                        for j, bank in ((0, PA), (1, XA)):
                            pe.wait_ge(bank.emptied, used[bank].n)
                            pe.wait_ge(S[j].emptied, used[S[j]].n)
                            for tile in range(NT):
                                mm = pe.matmul(S[j][:, tile * P:(tile + 1) * P],
                                               qhalf[j][:, tile * P:(tile + 1) * P],
                                               w[:, j, C * P:(C + 1) * P], start=True, stop=True)
                                if (j, tile) == (1, 0):
                                    mm.then_inc(slab_begun, 1)
                            mm.then_inc(S[j].filled, 1)
                            used[S[j]].up()
                        for x in range(4):
                            hook.back(i * 8 + (4 * b + x), 3)
                slab_base += 2 * HEADS
                hook.end(3)

            slab_base = WADA_SLABS
            attend(0, None)
            attend(1, gather)
            gather_alone(pe, gather, t, {})

        @block.scalar
        def _(act):
            used = {b: Tally() for b in (PA, XA, O)}
            t = {**used, "exp": Tally(), "gate": Tally(), "rec": Tally()}

            act.wait_ge(consts_in, 14 * 16)
            act.wait_ge(consts_set, 1)
            act.activation(cvec[:, :, :], cvec[:, :, :], ACT.Silu).then_inc(silu_done, 1)
            act.wait_ge(lam_exp, 1)
            act.activation(lam[:, 2:4], lam[:, 0:2], ACT.Exp).then_inc(lam_exp, 1)

            def gather_begin(tile, b, turn):
                pass

            def gather_front(n, group, b):
                act.wait_ge(u_read[GS - 1], n + 1)
                act.activation(gelus[:, :], dots[:, :], ACT.Gelu).then_inc(gelu_done, 1)

            def gather_back(n, group, b):
                act.wait_ge(weighed, n + 1)
                for k in range(GS):
                    act.wait_ge(v_read_pe[k], n)
                    act.activation(vdiag[:, k, :], ident[:, :], ACT.Copy, scale=weights[:, k:k + 1])\
                        .then_inc(vdiag_ready, 1)

            def gather_end(tile, s, row):
                act.wait_ge(fsum_ready, tile + 1)
                act.activation(fstat[:, 1:2], fstat[:, 0:1], ACT.Sqrt, bias=eps[:, 0:1], scale=1.0 / D)\
                    .then_inc(froot_ready, 1)
                act.wait_ge(y_ready, tile + 1)
                act.dma_start(y[s][ds(row * P, P), :], x1_tile[:, :])\
                    .then_inc(y_out, 16)

            gather = (gather_begin, gather_front, gather_back, gather_end)

            def norm_root(s, which, src):
                for c in range(C):
                    if c >= 2:
                        act.wait_ge(square_read, (2 * s + which) * (C - 1) + c - 1)
                    act.activation(square[c % 2], src[:, c, :], ACT.Square).then_inc(squared, 1)
                act.wait_ge(PA.filled, used[PA].n + 1)
                act.activation(root, PA[:, :], ACT.Sqrt, bias=eps[:, 0:1], scale=1.0 / D)\
                    .then_inc(PA.emptied, 1)
                used[PA].up()

            def empty(bank, dst, src=None, scale=1.0, func=ACT.Copy):
                act.wait_ge(bank.filled, used[bank].n + 1)
                act.activation(dst, bank[:, :] if src is None else src, func, scale=scale)\
                    .then_inc(bank.emptied, 1)
                used[bank].up()

            def by_tile(bank):
                return bank[:, :].rearrange("p (t q) -> p t q", q=P)

            def backwards(dst):
                row = dst.ap[0][0]
                return bass.AP(tensor=dst.tensor, offset=dst.offset + P - 1, ap=[[row, P], [P, NT], [-1, P]])

            def exps(u, n):
                act.wait_ge(maxed, t["exp"].n + 1)
                t["exp"].up()
                for x in range(len(n)):
                    e = act.activation(scores_sb[u % 2][:, x * F:x * F + n[x]],
                                       scores_sb[u % 2][:, x * F:x * F + n[x]], ACT.Exp,
                                       bias=nm[:, u % 2, x:x + 1], accum_out=den[:, u % 2, x:x + 1])
                e.then_inc(exped, 1)

            def attend(s, hooks):
                if s == 0:
                    act.wait_ge(setup_done, 1)
                act.wait_ge(x_in, 16 * (s + 1))
                norm_root(s, 0, hT)
                hook = Hooks(hooks, s - 1)
                hook.begin(0)
                with turns(act, HEADS // 2, t, {PA: 4, XA: 6, O: 2, "exp": 8}) as i:
                    for j in range(2):
                        empty(PA, backwards(qkv[0][0]), src=by_tile(PA), scale=DH ** -0.5)
                        empty(XA, qkv[0][2])
                        exps(0, (F, F))
                        for tile in range(NT):
                            if tile + 1 < NT:
                                exps(tile + 1, (F, F))
                            if tile % 2 == 0:
                                empty(XA, probsT[0][:, 0:F])
                            hook.front(i * 8 + (NT * j + tile), 0)
                            hook.back(i * 8 + (NT * j + tile), 0)
                        act.wait_ge(O.filled, used[O].n + 1)
                        used[O].up()
                        act.activation(o_square, O[:, :], ACT.Square).then_inc(o_squared, 1)
                        act.wait_ge(PA.filled, used[PA].n + 1)
                        act.activation(o_root, PA[:, :], ACT.Sqrt, bias=eps[:, 0:1], scale=1.0 / P)\
                            .then_inc(PA.emptied, 1)
                        used[PA].up()
                hook.end(0)

                hook.begin(1)
                with turns(act, PAIRS // 2, t, {PA: 6, XA: 38, "exp": 16}) as i:
                    for b in range(2):
                        for g in range(3):
                            empty(PA, backwards(qkv[g][0]), src=by_tile(PA), scale=DH ** -0.5)
                            empty(XA, qkv[g][2])
                        width = [2 * F + len(key_tiles(u % NT)) * P for u in range(2 * NT)]
                        exps(0, (width[0],))
                        for u in range(2 * NT):
                            if u + 1 < 2 * NT:
                                exps(u + 1, (width[u + 1],))
                            empty(XA, probsT[u % 2][:, 0:F])
                            n = width[u] - 2 * F
                            empty(XA, probsT[u % 2][:, 2 * F:width[u]], src=XA[:, 0:n])
                            hook.front(i * 16 + (8 * b + u), 1)
                            hook.back(i * 16 + (8 * b + u), 1)
                hook.end(1)
                used[O].up(2 * PAIRS)

                hook.begin(2)
                with turns(act, C // 2, t, {PA: 2, XA: 2, "gate": 2}) as i:
                    for j in range(2):
                        act.wait_ge(gated, t["gate"].n)
                        t["gate"].up()
                        empty(PA, gate_sb[0], func=ACT.Sigmoid)
                        empty(XA, gate_sb[1], func=ACT.Sigmoid)
                        for x in range(2):
                            hook.front(i * 4 + (2 * j + x), 2)
                            hook.back(i * 4 + (2 * j + x), 2)
                if hooks:
                    with act.Fori(0, C // 2) as i:
                        for x in range(4):
                            hook.front(i * 4 + (16 + x), 2)
                            hook.back(i * 4 + (16 + x), 2)
                hook.end(2)

                act.wait_ge(x1_ready, C * (s + 1))
                norm_root(s, 1, x1T)
                for tile in range(NT):
                    for which in range(2):
                        if NT * s + tile:
                            act.wait_ge(stage_out[which], 16 * (NT * s + tile))
                        act.wait_ge(XA.filled, used[XA].n + 1)
                        act.activation(stage[which][:, 0:F], XA[:, :], ACT.Copy).then_inc(XA.emptied, 1)
                        used[XA].up()
                        act.wait_ge(XA.emptied, used[XA].n)
                        act.activation(pad_a[:, :], eps[:, :], ACT.Copy).then_inc(staged_a, 1)

                hook.begin(3)
                with turns(act, HEADS // 2, t, {PA: 2, XA: 2, "rec": 2}) as i:
                    for b in range(2):
                        empty(PA, qhalf[0])
                        empty(XA, qhalf[1])
                        for x in range(2):
                            hook.front(i * 8 + (4 * b + x), 3)
                            hook.back(i * 8 + (4 * b + x), 3)
                        act.wait_ge(gap_ready, t["rec"].n + 1)
                        t["rec"].up()
                        act.activation(gexp, gap, ACT.Exp).then_inc(gap_exped, 1)
                        for x in range(2, 4):
                            hook.front(i * 8 + (4 * b + x), 3)
                            hook.back(i * 8 + (4 * b + x), 3)
                hook.end(3)

            attend(0, None)
            attend(1, gather)
            gather_alone(act, gather, t, {})
            act.wait_ge(y_out, 16 * SEQS * NT)

        @block.vector
        def _(dve):
            used = {b: Tally() for b in BANKS}
            t = {**used, "step": Tally(), "exp": Tally(), "gate": Tally(),
                 "x1": Tally(), "rec": Tally()}
            steps = t["step"]

            def then(ins):
                ins.then_inc(step, 1)
                steps.up()
                dve.wait_ge(step, steps.n)

            def fence():
                dve.memset(spare(pad), 0.0)

            dve.wait_ge(consts_in, 14 * 16)
            then(dve.tensor_tensor(lamv[:, 0, :], lamv[:, 0, :], lamv[:, 1, :], ALU.mult))
            dve.tensor_reduce(lam[:, 0:1], lamv[:, 0, :], AX_X, ALU.add)
            then(dve.tensor_tensor(lamv[:, 2, :], lamv[:, 2, :], lamv[:, 3, :], ALU.mult))
            dve.tensor_reduce(lam[:, 1:2], lamv[:, 2, :], AX_X, ALU.add).then_inc(lam_exp, 1)
            dve.memset(mixsign[:, 0:1], 1.0)
            then(dve.tensor_scalar(gsub[:, :], gsub[:, :], 1.0 - LAM_INIT, None, ALU.mult))
            with turns(dve, WADA_SLABS // 2, t, {PV: 1, XV: 1}) as i:
                for j, bank in ((0, PV), (1, XV)):
                    dve.wait_ge(bank.filled, used[bank].n + 1)
                    dst = mod[:, ds((2 * i + j) * WADA_COLS, WADA_COLS)]
                    dve.tensor_tensor(dst, bank[0:SEQS, 0:WADA_COLS],
                                      b_ada[:, ds((2 * i + j) * WADA_COLS, WADA_COLS)], ALU.add)\
                        .then_inc(bank.emptied, 1)
                    used[bank].up()
                    dve.wait_ge(bank.emptied, used[bank].n)
                    dve.memset(spare(pad), 0.0).then_inc(mod_ready, 1)
            dve.wait_ge(lam_exp, 2)
            then(dve.tensor_tensor(lam[:, 0:1], lam[:, 3:4], lam[:, 2:3], ALU.subtract))
            then(dve.tensor_scalar(mixsign[:, 1:2], lam[:, 0:1], -LAM_INIT, None, ALU.add))
            dve.wait_ge(PV.filled, used[PV].n + 1)
            dve.tensor_copy(modT[:, :, :].rearrange("p c s -> p (c s)"), PV[:, 0:6 * C * SEQS])\
                .then_inc(PV.emptied, 1)
            used[PV].up()
            dve.wait_ge(PV.emptied, used[PV].n)
            for s in range(SEQS):
                for dst, part, g in ((scale1, 1, gmix), (scale2, 4, gffn)):
                    then(dve.scalar_tensor_tensor(out=dst[:, s, :], in0=modT[:, part * C:(part + 1) * C, s],
                                                  scalar=1.0, in1=g[:, :], op0=ALU.add, op1=ALU.mult))
            for s in range(SEQS):
                for half, bank in ((0, XV), (1, PV)):
                    dve.wait_ge(bank.filled, used[bank].n + 1)
                    dve.tensor_copy(oaT[:, 2 + 2 * s + half, :], bank[:, :]).then_inc(bank.emptied, 1)
                    used[bank].up()
            for half, bank in ((0, XV), (1, PV)):
                dve.wait_ge(bank.filled, used[bank].n + 1)
                dve.tensor_tensor(oaT[0:BIAS_ROWS, half, :], bank[0:BIAS_ROWS, :],
                                  mask[:, half * F:(half + 1) * F], ALU.add).then_inc(bank.emptied, 1)
                used[bank].up()
                dve.wait_ge(bank.emptied, used[bank].n)
            dve.memset(spare(pad), 0.0).then_inc(rows_ready, 1)
            dve.wait_ge(rows_out, 48)
            dve.memset(spare(pad), 0.0).then_inc(setup_done, 1)

            def gather_begin(tile, b, turn):
                then(dve.memset(vsum[:, :], 0.0))
                dve.wait_ge(tile_in[b], turn * 48)
                fence()

            def gather_front(n, group, b):
                for k in range(GS):
                    dve.wait_ge(u_in[k], (n + 1) * 16)
                    dve.tensor_tensor_reduce(urows[:, k, :], urows[:, k, :], h2_tile[:, b, :], 1.0, 0.0,
                                             ALU.mult, ALU.add, dots[:, k:k + 1]).then_inc(u_read[k], 1)

            def gather_back(n, group, b):
                dve.wait_ge(gelu_done, n + 1)
                dve.wait_ge(vdiag_ready, n * GS)
                dve.tensor_tensor(weights[:, :], gelus[:, :], shares[:, b, ds(group * GS, GS)], ALU.mult)\
                    .then_inc(weighed, 1)
                dve.wait_ge(weighed, n + 1)
                for k in range(GS):
                    dve.wait_ge(v_in[k], (n + 1) * 16)
                    dve.scalar_tensor_tensor(out=vsum[:, :], in0=vrows[:, k, F:D], scalar=weights[:, k:k + 1],
                                             in1=vsum[:, :], op0=ALU.mult, op1=ALU.add)\
                        .then_inc(v_read_dve[k], 1)
                    dve.wait_ge(v_read_dve[k], n + 1)

            def gather_end(tile, s, row):
                dve.wait_ge(final_in, (tile + 1) * 32)
                then(dve.tensor_tensor(vsum[:, :], vsum[:, :], gate2[:, F:D], ALU.mult))
                then(dve.tensor_tensor(x1_tile[:, F:D], x1_tile[:, F:D], vsum[:, :], ALU.add))
                dve.wait_ge(G.filled, tile + 1)
                dve.tensor_tensor(vsum[:, :], G[:, :], gate2[:, 0:F], ALU.mult).then_inc(G.emptied, 1)
                dve.wait_ge(G.emptied, tile + 1)
                then(dve.tensor_tensor(x1_tile[:, 0:F], x1_tile[:, 0:F], vsum[:, :], ALU.add))
                for half in range(2):
                    cols = slice(half * F, (half + 1) * F)
                    then(dve.tensor_tensor_reduce(vsum[:, :], x1_tile[:, cols], x1_tile[:, cols], 1.0, 0.0,
                                                  ALU.mult, ALU.add, fstat[:, 2 + half:3 + half]))
                dve.tensor_tensor(fstat[:, 0:1], fstat[:, 2:3], fstat[:, 3:4], ALU.add).then_inc(fsum_ready, 1)
                dve.wait_ge(froot_ready, tile + 1)
                then(dve.reciprocal(fstat[:, 2:3], fstat[:, 1:2]))
                dve.scalar_tensor_tensor(out=x1_tile[:, :], in0=x1_tile[:, :], scalar=fstat[:, 2:3],
                                         in1=gfin[:, :], op0=ALU.mult, op1=ALU.mult).then_inc(y_ready, 1)

            gather = (gather_begin, gather_front, gather_back, gather_end)

            def modulate(s, which, src):
                used[PA].up()
                dve.wait_ge(PA.emptied, used[PA].n)
                then(dve.reciprocal(root, root))
                scale, shift = ((scale1, 0), (scale2, 3))[which]
                for c in range(C):
                    last = dve.tensor_tensor(hT[:, c, :], src[:, c, :], root, ALU.mult)
                then(last)
                for c in range(C):
                    dve.tensor_scalar(hT[:, c, :], hT[:, c, :], scale[:, s, c:c + 1],
                                      modT[:, shift * C + c, s:s + 1], ALU.mult, ALU.add).then_inc(h_ready, 1)

            def bias_max(u, parts):
                for x, (bank, col, n, z) in enumerate(parts):
                    dve.wait_ge(bank.filled, used[bank].n + 1)
                    fence()
                    dve.tensor_tensor_reduce(scores_sb[u % 2][:, col:col + n], bank[:, 0:n], z, 1.0, LOWEST,
                                             ALU.add, ALU.max, mx[:, u % 2, x:x + 1]).then_inc(bank.emptied, 1)
                    used[bank].up()
                dve.wait_ge(parts[-1][0].emptied, used[parts[-1][0]].n)

            def attend(s, hooks):
                dve.wait_ge(x_in, 16 * (s + 1))
                modulate(s, 0, hT)
                hook = Hooks(hooks, s - 1)
                hook.begin(0)
                with turns(dve, HEADS // 2, t, {PA: 4, PV: 2, XV: 4, S[0]: 8, S[1]: 8, O: 2,
                                                "exp": 8, "step": 18}) as i:
                    for j in range(2):
                        used[PA].up()
                        dve.wait_ge(PV.filled, used[PV].n + 1)
                        dve.tensor_copy(qkv[0][1], PV[:, :]).then_inc(PV.emptied, 1)
                        used[PV].up()
                        dve.wait_ge(z_in[j], (i + 1) * 16 + s * Z_PER_SEQ)

                        def unit_max(tile):
                            at = 384 - tile * P
                            bias_max(tile, [(S[x], x * F, F, zbuf[j][:, at:at + F]) for x in range(2)])
                            dve.tensor_scalar(nm[:, tile % 2, :], mx[:, tile % 2, 0:2], -1.0, None, ALU.mult)\
                                .then_inc(maxed, 1)

                        def unit_diag(tile):
                            dve.wait_ge(exped, t["exp"].n + 1)
                            t["exp"].up()
                            then(dve.reciprocal(rden[:, tile % 2, :], den[:, tile % 2, :]))
                            then(dve.tensor_tensor(rden[:, tile % 2, :], rden[:, tile % 2, :], mixsign[:, :],
                                                   ALU.mult))
                            for x in range(2):
                                d = dve.tensor_scalar(pdiag[:, tile % 2, x, :], flip[:, :],
                                                      rden[:, tile % 2, x:x + 1], None, ALU.mult)
                            d.then_inc(diag_ready, 1)

                        unit_max(0)
                        for tile in range(NT):
                            if tile + 1 < NT:
                                unit_max(tile + 1)
                            if tile == NT - 2:
                                dve.memset(spare(pad), 0.0).then_inc(z_read[j], 1)
                            unit_diag(tile)
                            hook.front(i * 8 + (NT * j + tile), 0)
                            if tile % 2 == 1:
                                dve.wait_ge(XV.filled, used[XV].n + 1)
                                dve.tensor_copy(probsT[1][:, 0:F], XV[:, :]).then_inc(XV.emptied, 1)
                                used[XV].up()
                            hook.back(i * 8 + (NT * j + tile), 0)
                        used[PA].up()
                        dve.wait_ge(PA.emptied, used[PA].n)
                        then(dve.reciprocal(o_root, o_root))
                        dve.wait_ge(O.filled, used[O].n + 1)
                        dve.scalar_tensor_tensor(
                            out=oaT[:, ds(2 * i + j, 1), :].rearrange("p a f -> p (a f)"), in0=O[:, :],
                            scalar=gsub[:, 0:1], in1=o_root, op0=ALU.mult, op1=ALU.mult).then_inc(O.emptied, 1)
                        used[O].up()
                dve.wait_ge(O.emptied, used[O].n)
                dve.memset(spare(pad), 0.0).then_inc(oa_ready, HEADS)
                hook.end(0)

                hook.begin(1)
                with turns(dve, PAIRS // 2, t, {PV: 6, XV: 16, S[0]: 24, S[1]: 24, O: 4,
                                                "exp": 16, "step": 16}) as i:
                    for b in range(2):
                        for g in range(3):
                            dve.wait_ge(PV.filled, used[PV].n + 1)
                            dve.tensor_copy(qkv[g][1], PV[:, :]).then_inc(PV.emptied, 1)
                            used[PV].up()

                        def unit_max(u):
                            j, tile = divmod(u, NT)
                            if tile == 0:
                                dve.wait_ge(z_in[j], (2 * i + b + 1) * 48 + (s * Z_PER_SEQ + HEADS // 2 * 16))
                            at = 384 - tile * P
                            kts = key_tiles(tile)
                            band = 2 * Z_WIDE + (kts[0] - tile + 1) * P
                            z = zbuf[j]
                            bias_max(u, [(S[(3 * u) % 2], 0, F, z[:, at:at + F]),
                                         (S[(3 * u + 1) % 2], F, F, z[:, Z_WIDE + at:Z_WIDE + at + F]),
                                         (S[(3 * u + 2) % 2], 2 * F, len(kts) * P,
                                          z[:, band:band + len(kts) * P])])
                            dve.tensor_reduce(nm[:, u % 2, 0:1], mx[:, u % 2, 0:3], AX_X, ALU.max, negate=True)\
                                .then_inc(maxed, 1)
                            if tile == NT - 1:
                                dve.memset(spare(pad), 0.0).then_inc(z_read[j], 1)

                        def unit_diag(u):
                            dve.wait_ge(exped, t["exp"].n + 1)
                            t["exp"].up()
                            then(dve.reciprocal(rden[:, u % 2, 0:1], den[:, u % 2, 0:1]))
                            dve.tensor_scalar(pdiag[:, u % 2, 0, :], flip[:, :], rden[:, u % 2, 0:1], None,
                                              ALU.mult).then_inc(diag_ready, 1)

                        def head_out(j):
                            rows = slice(j * DH, (j + 1) * DH)
                            dve.wait_ge(O.filled, used[O].n + 1)
                            dve.tensor_copy(obT[rows, ds(2 * i + b, 1), :].rearrange("p a f -> p (a f)"),
                                            O[rows, :]).then_inc(O.emptied, 1)
                            used[O].up()

                        unit_max(0)
                        for u in range(2 * NT):
                            if u + 1 < 2 * NT:
                                unit_max(u + 1)
                            unit_diag(u)
                            hook.front(i * 16 + (8 * b + u), 1)
                            dve.wait_ge(XV.filled, used[XV].n + 1)
                            dve.tensor_copy(probsT[u % 2][:, F:2 * F], XV[:, :]).then_inc(XV.emptied, 1)
                            used[XV].up()
                            if u == NT:
                                head_out(0)
                            hook.back(i * 16 + (8 * b + u), 1)
                        head_out(1)
                used[PA].up(3 * PAIRS)
                hook.end(1)

                hook.begin(2)
                used[XA].up(3 * HEADS + 19 * PAIRS)
                with turns(dve, C // 2, t, {PA: 2, XA: 2, PV: 2, XV: 2, "gate": 2}) as i:
                    for j in range(2):
                        for x, (gate, bank) in enumerate(((PA, PV), (XA, XV))):
                            used[gate].up()
                            dve.wait_ge(gate.emptied, used[gate].n)
                            dve.wait_ge(bank.filled, used[bank].n + 1)
                            dve.tensor_tensor(gate_sb[2 + x], bank[:, :], gate_sb[x], ALU.mult)\
                                .then_inc(bank.emptied, 1)
                            used[bank].up()
                        dve.wait_ge(XV.emptied, used[XV].n)
                        dve.tensor_tensor(merged[:, ds(2 * i + j, 1), :].rearrange("p a f -> p (a f)"),
                                          gate_sb[2], gate_sb[3], ALU.add).then_inc(gated, 1)
                        t["gate"].up()
                        for x in range(2):
                            hook.front(i * 4 + (2 * j + x), 2)
                            hook.back(i * 4 + (2 * j + x), 2)
                with turns(dve, C // 2, t, {PV: 2, "x1": 2}) as i:
                    for j in range(2):
                        dve.wait_ge(PV.filled, used[PV].n + 1)
                        dve.wait_ge(xr_in[j], (i + (1 + s * C // 2)) * 16)
                        dve.scalar_tensor_tensor(
                            out=x1T[:, ds(2 * i + j, 1), :].rearrange("p a f -> p (a f)"), in0=PV[:, :],
                            scalar=modT[:, ds(2 * C + 2 * i + j, 1), s:s + 1].rearrange("p a b -> p (a b)"),
                            in1=xr[j], op0=ALU.mult, op1=ALU.add).then_inc(PV.emptied, 1)
                        used[PV].up()
                        dve.wait_ge(PV.emptied, used[PV].n)
                        dve.memset(spare(pad), 0.0).then_inc(x1_ready, 1)
                        t["x1"].up()
                        for x in range(2):
                            hook.front(i * 4 + (16 + 2 * j + x), 2)
                            hook.back(i * 4 + (16 + 2 * j + x), 2)
                hook.end(2)

                modulate(s, 1, x1T)
                for tile in range(NT):
                    for which in range(2):
                        if NT * s + tile:
                            dve.wait_ge(stage_out[which], 16 * (NT * s + tile))
                        dve.wait_ge(XV.filled, used[XV].n + 1)
                        dve.tensor_copy(stage[which][:, F:D], XV[:, :]).then_inc(XV.emptied, 1)
                        used[XV].up()
                        used[XA].up()
                        dve.wait_ge(XV.emptied, used[XV].n)
                        dve.memset(spare(pad), 0.0).then_inc(staged_v, 1)

                hook.begin(3)
                with turns(dve, HEADS // 2, t, {S[0]: 2, S[1]: 2, "rec": 2, "step": 48}) as i:
                    for b in range(2):
                        for j in range(2):
                            dve.wait_ge(S[j].filled, used[S[j]].n + 1)
                            fence()
                            sc = S[j][:, :].rearrange("p (t k) -> p t k", k=P)
                            for tile in range(NT):
                                last = dve.max(topv[j][:, tile, 0:8], sc[:, tile, :])
                            then(last)
                            fence()
                            for tile in range(NT):
                                dve.match_replace(rest[:, tile, :], topv[j][:, tile, 0:8], sc[:, tile, :], LOWEST)
                            for tile in range(NT):
                                last = dve.max_index(topi[j][:, tile, 0:8], topv[j][:, tile, 0:8], sc[:, tile, :])
                            last.then_inc(S[j].emptied, 1)
                            used[S[j]].up()
                            dve.wait_ge(S[j].emptied, used[S[j]].n)
                            fence()
                            for tile in range(NT):
                                last = dve.max(topv[j][:, tile, 8:16], rest[:, tile, :])
                            then(last)
                            fence()
                            for tile in range(NT):
                                last = dve.max_index(topi[j][:, tile, 8:16], topv[j][:, tile, 8:16],
                                                     rest[:, tile, :])
                            then(last)
                            then(dve.tensor_copy(topf[j], topi[j].rearrange("p t k -> p (t k)")))
                            hook.front(i * 8 + (4 * b + j), 3)
                            hook.back(i * 8 + (4 * b + j), 3)
                        for tile in range(NT):
                            last = dve.tensor_tensor(
                                cand[:, tile, :].rearrange("p (a b) -> p a b", b=K16),
                                topv[0][:, tile, :].unsqueeze(2).broadcast_to([P, K16, K16]),
                                topv[1][:, tile, :].unsqueeze(1).broadcast_to([P, K16, K16]), ALU.add)
                        then(last)
                        fence()
                        for tile in range(NT):
                            last = dve.max(candv[:, tile, 0:8], cand[:, tile, :])
                        then(last)
                        fence()
                        for tile in range(NT):
                            dve.match_replace(cand2[:, tile, :], candv[:, tile, 0:8], cand[:, tile, :], LOWEST)
                        for tile in range(NT):
                            last = dve.max_index(candi[:, tile, 0:8], candv[:, tile, 0:8], cand[:, tile, :])
                        then(last)
                        fence()
                        for tile in range(NT):
                            last = dve.max(candv[:, tile, 8:16], cand2[:, tile, :])
                        then(last)
                        dve.tensor_tensor(gap.rearrange("p (t k) -> p t k", k=K16), candv,
                                          candv[:, :, 0:1].broadcast_to([P, NT, K16]), ALU.subtract)\
                            .then_inc(gap_ready, 1)
                        for tile in range(NT):
                            last = dve.max_index(candi[:, tile, 8:16], candv[:, tile, 8:16], cand2[:, tile, :])
                        then(last)
                        flat = candi.rearrange("p t k -> p (t k)")
                        dve.tensor_single_scalar(parti[0], flat, 4, op=ALU.logical_shift_right)
                        then(dve.tensor_single_scalar(parti[1], flat, 15, op=ALU.bitwise_and))
                        dve.tensor_copy(partf[0], parti[0])
                        then(dve.tensor_copy(partf[1], parti[1]))
                        for j in range(2):
                            then(dve.tensor_tensor(
                                hot.rearrange("p (a b) -> p a b", b=K16),
                                partf[j].unsqueeze(2).broadcast_to([P, TK, K16]),
                                iota16[:, :].unsqueeze(1).broadcast_to([P, TK, K16]), ALU.is_equal))
                            then(dve.tensor_tensor(
                                hot2.rearrange("p (t a b) -> p t a b", t=NT, b=K16),
                                hot.rearrange("p (t a b) -> p t a b", t=NT, b=K16),
                                topf[j].rearrange("p (t k) -> p t k", k=K16).unsqueeze(2)
                                .broadcast_to([P, NT, K16, K16]), ALU.mult))
                            then(dve.tensor_reduce(keyno[j], hot2.rearrange("p (a b) -> p a b", b=K16), AX_X,
                                                   ALU.add))
                        then(dve.scalar_tensor_tensor(out=expert_f, in0=keyno[0], scalar=float(P), in1=keyno[1],
                                                      op0=ALU.mult, op1=ALU.add))
                        dve.wait_ge(record_out[b], (i + s * HEADS // 2) * 32)
                        dve.tensor_copy(chosen[:, b, :], expert_f)
                        dve.wait_ge(gap_exped, t["rec"].n + 1)
                        then(dve.tensor_reduce(gsum, gexp.rearrange("p (t k) -> p t k", k=K16), AX_X, ALU.add))
                        then(dve.reciprocal(grec, gsum))
                        dve.tensor_tensor(share[:, b, :].rearrange("p (t k) -> p t k", k=K16),
                                          gexp.rearrange("p (t k) -> p t k", k=K16),
                                          grec.unsqueeze(2).broadcast_to([P, NT, K16]), ALU.mult)\
                            .then_inc(record_ready, 1)
                        t["rec"].up()
                        for x in range(2, 4):
                            hook.front(i * 8 + (4 * b + x), 3)
                            hook.back(i * 8 + (4 * b + x), 3)
                used[PA].up(HEADS)
                used[XA].up(HEADS)
                for j in range(2):
                    dve.wait_ge(stage_out[j], 16 * NT * (s + 1))
                hook.end(3)

            attend(0, None)
            attend(1, gather)
            gather_alone(dve, gather, t, {"step": 14})


def slabs_of(weight, columns):
    rows = weight.shape[0] // P
    return np.stack([np.ascontiguousarray(weight[:, cols].reshape(rows, P, -1).transpose(1, 0, 2)).reshape(P, -1)
                     for cols in columns])


def bucket_table():
    rel = np.arange(2 * F) - F
    half, exact = BUCKETS // 2, BUCKETS // 4
    n = np.abs(rel)
    nf = np.maximum(n, exact).astype(np.float32)
    large = exact + (np.log(nf / np.float32(exact)) / np.float32(math.log(MAX_DISTANCE / exact))
                     * np.float32(half - exact)).astype(np.int32)
    bucket = np.where(rel > 0, half, 0) + np.where(n < exact, n, np.minimum(large, half - 1))
    return (np.arange(BUCKETS)[:, None] == bucket[None, :]).astype(np.float32)


def band_table():
    rel = np.arange(2 * F) - F
    out = np.zeros((BIAS_ROWS, 2 * F), np.float32)
    for g, (window, dilation) in enumerate(GROUPS):
        reach = (np.abs(rel) <= window // 2) & (rel % dilation == 0)
        out[HEADS * (1 + g):HEADS * (2 + g)] = np.where(reach, 0.0, MASKED)
    return out


def layout(inputs):
    def col(v):
        return np.ascontiguousarray(v.reshape(-1, P).T)

    a = {k: np.asarray(v) for k, v in inputs.items()}
    w_in, span = a["w_in"][0], np.arange(P)
    heads = [np.concatenate([x * D + h * P + span for x in range(3)]) for h in range(HEADS)]
    qkv_b = len(GROUPS) * HEADS * DH
    for pair in range(PAIRS):
        for g in range(len(GROUPS)):
            heads.append(np.concatenate([3 * D + x * qkv_b + g * HEADS * DH + pair * P + span for x in range(3)]))
    gates = 3 * D + 3 * qkv_b
    chunks = [c * P + span for c in range(C)]
    ga = slabs_of(w_in, [gates + c for c in chunks])
    gb = slabs_of(w_in, [gates + D + c for c in chunks])
    keys = np.stack([a["sub_keys_1"][0], a["sub_keys_2"][0]], 1).reshape(2 * HEADS, P, P).transpose(0, 2, 1)
    xs = [a["x_prompt"][0], a["x_sample"][0]]
    return {
        "x_t": np.stack([x.T.reshape(C, P, F).transpose(1, 0, 2) for x in xs]),
        "c_t": np.stack([col(a["c_prompt"][0]), col(a["c_sample"][0])], -1),
        "w_ada": slabs_of(a["w_ada"][0], [n * WADA_COLS + np.arange(WADA_COLS) for n in range(WADA_SLABS)]),
        "b_ada": np.stack([a["b_ada"][0]] * SEQS),
        "g_mix": col(a["g_norm_mix"][0]),
        "g_ffn": col(a["g_norm_ffn"][0]),
        "g_final": np.stack([a["g_final"]] * P),
        "g_sub": col(a["g_subln"][0]),
        "lambdas": np.stack([np.stack([a[f"lambda_{x}"][0] for x in ("q1", "k1", "q2", "k2")])] * P),
        "rel_bias": a["rel_bias"],
        "w_heads": slabs_of(w_in, heads),
        "w_merge": np.concatenate([ga, gb, slabs_of(a["w_proj_a"][0], chunks), slabs_of(a["w_proj_b"][0], chunks)], 2),
        "w_out": slabs_of(a["w_out"][0], chunks),
        "w_query": np.concatenate([slabs_of(a["w_query"][0], [m * P + span for m in range(2 * HEADS)]), keys], 2),
        "expert_u": a["expert_u"][0],
        "expert_v": a["expert_v"][0],
        "ident": np.eye(P, dtype=np.float32),
        "flip": np.eye(P, dtype=np.float32)[::-1],
        "iota16": np.stack([np.arange(K16, dtype=np.float32)] * P),
        "pick": np.repeat(np.eye(SEQS, dtype=np.float32), P, 1),
        "onehot": bucket_table(),
        "mask": band_table(),
    }


def kernel(**inputs):
    import concourse.bacc as bacc
    from concourse.bass_utils import run_bass_kernel_spmd

    nc = bacc.Bacc("TRN2", target_bir_lowering=False, num_devices=1)
    arrays = {"in_" + name: np.ascontiguousarray(v) for name, v in layout(inputs).items()}
    ins = {name[3:]: nc.dram_tensor(name, v.shape, mybir.dt.from_np(v.dtype), kind="ExternalInput").ap()
           for name, v in arrays.items()}
    y = [nc.dram_tensor(name, (F, D), F32, kind="ExternalOutput").ap() for name in ("y_prompt", "y_sample")]
    build(nc, ins, y)
    r = run_bass_kernel_spmd(nc, [arrays], core_ids=[0])
    return tuple(r.results[0][name].reshape(1, F, D) for name in ("y_prompt", "y_sample"))
```

```python
import math
from contextlib import ExitStack, contextmanager

import numpy as np

import concourse.bass as bass
from concourse import mybir

F32 = mybir.dt.float32
U32 = mybir.dt.uint32
ALU = mybir.AluOpType
ACT = mybir.ActivationFunctionType
AX_X = mybir.AxisListType.X
ds = bass.ds

P = 128
D = 1024
C = D // P
F = 512
NT = F // P
SEQS = 2
HEADS = 8
DH = 64
GROUPS = ((128, 1), (512, 4), (2048, 16))
PAIRS = HEADS // 2
STRIDE = 4
BUCKETS = 32
MAX_DISTANCE = 1024
BIAS_ROWS = HEADS * (1 + len(GROUPS))
K16 = 16
SLOTS = HEADS * K16
GS = 4
GPT = SLOTS // GS
EPS = 1e-6
MASKED = -1e30
LOWEST = -3e38
LAM_INIT = 0.8 - 0.6 * math.exp(0.0)

W_FREE = 28 * P
WADA_COLS = 384
WADA_SLABS = 6 * D // WADA_COLS

Z_WIDE = 896
Z_BAND = 384
SUB = 2 * P
DIL_FREE = 2 * P + Z_BAND
R_Z = 0
R_SC = R_Z + 2 * Z_WIDE
R_PT = R_SC + 2 * 2 * F
R_QKV = R_PT + 2 * DIL_FREE
R_RAW = R_QKV + 9 * F
R_END = R_RAW + 3 * PAIRS * F
R_MOD, R_BADA, R_ONEHOT, R_MASK = 0, 6 * D, 12 * D, 12 * D + 2 * F + SUB
R_ROWS = R_SC
R_PART = R_QKV
R_RT, R_SQ = R_SC, R_SC + F
R_GATE = R_SC
R_MERGED = R_QKV
R_X1T = R_RAW
R_XR = R_PT
R_STAGE = R_QKV
R_ROUTE = R_RAW


class Tally:

    def __init__(self):
        self.start, self.step = 0, 0

    @property
    def n(self):
        return self.start + self.step

    def up(self, k=1):
        self.step += k


@contextmanager
def turns(eng, count, tallies, per_turn):
    assert set(per_turn) <= set(tallies)
    starts = {t: tallies[t].n for t in tallies}
    with eng.Fori(0, count) as i:
        for t in tallies:
            k = per_turn.get(t, 0)
            tallies[t].start = i * k + starts[t] if k else starts[t]
            tallies[t].step = 0
        yield i
        for t in tallies:
            assert tallies[t].step == per_turn.get(t, 0), (t, tallies[t].step, per_turn.get(t, 0))
    for t in tallies:
        tallies[t].start, tallies[t].step = starts[t] + count * per_turn.get(t, 0), 0


def key_tiles(tile):
    return range(max(tile - 1, 0), min(tile + 2, NT))


def rounds(peel, eng, count, tallies, per_turn):
    with turns(eng, count - 1 if peel else count, tallies, per_turn) as i:
        yield i
    if peel:
        yield count - 1


class Hooks:

    def __init__(self, gather, seq):
        self.gather, self.seq = gather, seq

    def begin(self, tile):
        if self.gather:
            n = NT * self.seq + tile
            self.gather[0](n, tile % 2, n // 2 + 1)

    def front(self, base, k, tile):
        if self.gather:
            group = base + k
            last = isinstance(group, int) and group == GPT - 1
            self.gather[1]((NT * self.seq + tile) * GPT + group, group, k % 2, tile % 2, last)

    def back(self, base, k, tile):
        if self.gather:
            group = base + k
            self.gather[2]((NT * self.seq + tile) * GPT + group, group, tile % 2)

    def end(self, tile):
        if self.gather:
            self.gather[3](NT * self.seq + tile, self.seq, tile)


def gather_alone(eng, gather, tallies, per_turn):
    begin, front, back, end = gather
    seq = SEQS - 1
    with turns(eng, NT // 2, tallies, per_turn) as i:
        for b in range(2):
            tile = 2 * i + (NT * seq + b)
            begin(tile, b, i + (NT * seq // 2 + 1))
            with eng.Fori(0, GPT // 2 - 1) as g:
                for p in range(2):
                    front(tile * GPT + (2 * g + p), 2 * g + p, p, b, False)
                    back(tile * GPT + (2 * g + p), 2 * g + p, b)
            for p in range(2):
                front(tile * GPT + (GPT - 2 + p), GPT - 2 + p, p, b, p == 1)
                back(tile * GPT + (GPT - 2 + p), GPT - 2 + p, b)
            end(tile, seq, 2 * i + b)


def build(nc, ins, y):
    es = ExitStack()
    with es:
        def sb(name, shape, dt=F32):
            return es.enter_context(nc.sbuf_tensor(name, shape, dt))

        def sem(name):
            return es.enter_context(nc.semaphore(name))

        def scratch(name, shape, dt=F32):
            return nc.dram_tensor(name, shape, dt, kind="Internal").ap()

        bias_d = scratch("bias_rows", [BIAS_ROWS, 2 * F])
        bias_sub_d = scratch("bias_rows_stride", [BIAS_ROWS, SUB])
        gate2_d = scratch("gate2_rows", [SEQS, P, D])
        x1_d = scratch("x1_tiles", [SEQS * NT, P, D])
        h2_d = scratch("h2_tiles", [SEQS * NT, P, D])
        experts_d = scratch("experts", [SEQS * NT, P, SLOTS], U32)
        shares_d = scratch("shares", [SEQS * NT, P, SLOTS])

        hT = sb("hT", [P, C, F])
        oaT = sb("oaT", [P, HEADS, F])
        region = sb("region", [P, R_END])
        w = sb("w", [P, 2, W_FREE])
        urows = sb("urows", [P, GS, D])
        vrows = sb("vrows", [P, GS, D])
        h2_tile = sb("h2_tile", [P, 2, D])
        x1_tile = sb("x1_tile", [P, D])
        gate2 = sb("gate2", [P, D])
        gfin = sb("gfin", [P, D])
        vsum = sb("vsum", [P, F])
        vdiag = sb("vdiag", [P, GS, P])
        experts = sb("experts_tile", [P, 2, SLOTS], U32)
        shares = sb("shares_tile", [P, 2, SLOTS])
        now_u = sb("experts_now_u", [P, 2, GS], U32)
        now_v = sb("experts_now_v", [P, 2, GS], U32)
        dots = sb("dots", [P, 2, GS])
        gelus = sb("gelus", [P, GS])
        weights = sb("weights", [P, GS])
        fstat = sb("fstat", [P, 4])
        ident = sb("ident", [P, P])
        flip = sb("flip", [P, P])
        ones = sb("ones", [P, P])
        zeros = sb("zeros", [P, P])
        eps = sb("eps", [P, 1])
        mx = sb("mx", [P, 2, 4])
        nm = sb("nm", [P, 2, 2])
        den = sb("den", [P, 2, 2])
        rden = sb("rden", [P, 2, 2])
        unit_stat = sb("unit_stat", [P, 2, 2, 3, NT])
        stat = sb("stat", [P, 2, 3, NT, HEADS])
        spread = sb("spread", [HEADS, PAIRS * P])
        cvec = sb("cvec", [P, C, SEQS])
        gmix = sb("gmix", [P, C])
        gffn = sb("gffn", [P, C])
        gsub = sb("gsub", [P, 1])
        lamv = sb("lamv", [P, 4, DH])
        lam = sb("lam", [P, 4])
        mixsign = sb("mixsign", [P, 2])
        relb = sb("relb", [BUCKETS, BIAS_ROWS])
        pick = sb("pick", [SEQS, SEQS * P])
        modT = sb("modT", [P, 6 * C, SEQS])
        scale1 = sb("scale1", [P, SEQS, C])
        scale2 = sb("scale2", [P, SEQS, C])
        iota16 = sb("iota16", [P, K16])
        chosen = sb("chosen", [P, 2, NT * K16], U32)
        share = sb("share", [P, 2, NT * K16])
        pad = sb("pad", [1, 64])
        pad_a = sb("pad_a", [P, 1])
        pad_p = sb("pad_p", [1, 128])
        turn_of = {pad.name: 0, pad_p.name: 0}

        def spare(scrap):
            turn_of[scrap.name] = (turn_of[scrap.name] + 1) % scrap.shape[1]
            return scrap[:, turn_of[scrap.name]:turn_of[scrap.name] + 1]

        def reg(at, size):
            return region[:, at:at + size]

        zbuf = [reg(R_Z + j * Z_WIDE, Z_WIDE) for j in range(2)]
        scores_sb = [reg(R_SC + j * 2 * F, 2 * F) for j in range(2)]
        probsT = [reg(R_PT + j * DIL_FREE, DIL_FREE) for j in range(2)]
        qkv = [[reg(R_QKV + (3 * g + x) * F, F) for x in range(3)] for g in range(3)]
        raw = reg(R_RAW, 3 * PAIRS * F).rearrange("p (g a f) -> p g a f", g=3, a=PAIRS)
        obT = raw[:, 2, :, :]
        o_square, o_root = reg(R_RAW, F), reg(R_RAW + F, F)
        rows = region[0:HEADS, R_ROWS:R_ROWS + 6 * F].rearrange("p (k g f) -> p k g f", k=2, g=3)
        least = region[0:HEADS, R_PART:R_PART + F]
        total = region[0:HEADS, R_PART + F:R_PART + 2 * F]
        addend = [reg(R_PART + (2 + x) * F, F) for x in range(2)]
        mod = region[0:SEQS, R_MOD:R_MOD + 6 * D]
        b_ada = region[0:SEQS, R_BADA:R_BADA + 6 * D]
        onehot = region[0:BUCKETS, R_ONEHOT:R_ONEHOT + 2 * F + SUB]
        mask = region[0:BIAS_ROWS, R_MASK:R_MASK + 2 * F + SUB]
        root = reg(R_RT, F)
        square = [reg(R_SQ + j * F, F) for j in range(2)]
        gate_sb = [reg(R_GATE + j * F, F) for j in range(4)]
        merged = reg(R_MERGED, C * F).rearrange("p (c f) -> p c f", c=C)
        x1T = reg(R_X1T, C * F).rearrange("p (c f) -> p c f", c=C)
        xr = [reg(R_XR + j * F, F) for j in range(2)]
        stage = [reg(R_STAGE + j * D, D) for j in range(2)]
        at = R_ROUTE

        def route(size, dt=F32):
            nonlocal at
            at += size
            assert at <= R_END
            r = region[:, at - size:at]
            return r if dt == F32 else r.bitcast(dt)

        TK = NT * K16
        qhalf = [route(F) for _ in range(2)]
        topv = [route(TK).rearrange("p (t k) -> p t k", k=K16) for _ in range(2)]
        topi = [route(TK, U32).rearrange("p (t k) -> p t k", k=K16) for _ in range(2)]
        topf = [route(TK) for _ in range(2)]
        rest = route(F).rearrange("p (t k) -> p t k", k=P)
        cand = route(NT * 256).rearrange("p (t k) -> p t k", k=256)
        cand2 = route(NT * 256).rearrange("p (t k) -> p t k", k=256)
        candv = route(TK).rearrange("p (t k) -> p t k", k=K16)
        candi = route(TK, U32).rearrange("p (t k) -> p t k", k=K16)
        parti = [route(TK, U32) for _ in range(2)]
        partf = [route(TK) for _ in range(2)]
        hot = cand.rearrange("p t k -> p (t k)")
        hot2 = cand2.rearrange("p t k -> p (t k)")
        keyno = [route(TK) for _ in range(2)]
        expert_f = route(TK)
        gap = route(TK)
        gexp = route(TK)
        gsum = route(NT)
        grec = route(NT)

        class Bank:
            def __init__(self, name):
                self.t = es.enter_context(nc.psum_tensor(name, [P, F], F32))
                self.filled, self.emptied = sem(name + "_filled"), sem(name + "_emptied")

            def __getitem__(self, i):
                return self.t[i]

        PA, XA = Bank("bank_pa"), Bank("bank_xa")
        PV, XV = Bank("bank_pv"), Bank("bank_xv")
        S = [Bank("bank_s0"), Bank("bank_s1")]
        O, G = Bank("bank_o"), Bank("bank_g")
        BANKS = [PA, XA, PV, XV, *S, O, G]

        consts_in = sem("consts_in")
        consts_set = sem("consts_set")
        silu_done = sem("silu_done")
        lam_exp = sem("lam_exp")
        mod_ready = sem("mod_ready")
        rows_ready = sem("rows_ready")
        rows_out = sem("rows_out")
        setup_done = sem("setup_done")
        slab_in = [sem(f"slab_in{j}") for j in range(2)]
        slab_begun = sem("slab_begun")
        x_in = sem("x_in")
        z_in = [sem(f"z_in{j}") for j in range(2)]
        z_read = [sem(f"z_read{j}") for j in range(2)]
        step = sem("dve_step")
        squared = sem("squared")
        square_read = sem("square_read")
        h_ready = sem("h_ready")
        maxed = sem("maxed")
        exped = sem("exped")
        mixed = sem("mixed")
        dil_exped = sem("dil_exped")
        stats_ready = sem("stats_ready")
        gaps_ready = sem("gaps_ready")
        gaps_exped = sem("gaps_exped")
        factors_ready = sem("factors_ready")
        ob_ready = sem("ob_ready")
        o_squared = sem("o_squared")
        oa_ready = sem("oa_ready")
        gated = sem("gated")
        xr_in = [sem(f"xr_in{j}") for j in range(2)]
        x1_ready = sem("x1_ready")
        staged_a = sem("staged_a")
        staged_v = sem("staged_v")
        stage_out = [sem(f"stage_out{j}") for j in range(2)]
        gap_ready = sem("gap_ready")
        gap_exped = sem("gap_exped")
        record_ready = sem("record_ready")
        record_out = [sem(f"record_out{j}") for j in range(2)]
        tile_in = [sem(f"tile_in{j}") for j in range(2)]
        now_u_set = sem("now_u_set")
        now_v_set = sem("now_v_set")
        u_in = [sem(f"u_in{k}") for k in range(GS)]
        v_in = [sem(f"v_in{k}") for k in range(GS)]
        u_read = [sem(f"u_read{k}") for k in range(GS)]
        v_read_pe = [sem(f"v_read_pe{k}") for k in range(GS)]
        v_read_dve = [sem(f"v_read_dve{k}") for k in range(GS)]
        gelu_done = sem("gelu_done")
        weighed = sem("weighed")
        vdiag_ready = sem("vdiag_ready")
        final_in = sem("final_in")
        fsum_ready = sem("fsum_ready")
        froot_ready = sem("froot_ready")
        y_ready = sem("y_ready")
        y_out = sem("y_out")

        S1_PER_SEQ = NT * HEADS + NT * HEADS + HEADS

        Z_PER_SEQ = 16 * (HEADS // 2) * (1 + 2)

        block = es.enter_context(nc.Block())

        @block.sync
        def _(sp):
            t = {"slab": Tally(), "xr": Tally(), "z0": Tally(), "z1": Tally()}
            for dst, name in ((cvec[:, :, :], "c_t"), (gmix[:, :], "g_mix"), (gffn[:, :], "g_ffn"),
                              (gsub[:, :], "g_sub"), (lamv[:, :, :], "lambdas"), (relb[:, :], "rel_bias"),
                              (pick[:, :], "pick"), (ident[:, :], "ident"), (flip[:, :], "flip"),
                              (spread[:, :], "spread"), (iota16[:, :], "iota16"),
                              (b_ada, "b_ada"), (onehot, "onehot"), (mask, "mask"), (gfin[:, :], "g_final")):
                sp.dma_start(dst, ins[name]).then_inc(consts_in, 16)

            def slab(name, index, j, width):
                sp.wait_ge(slab_begun, t["slab"].n)
                sp.dma_start(w[:, j, 0:width], ins[name][ds(index, 1), :, :].rearrange("a p n -> (a p) n"))\
                    .then_inc(slab_in[j], 16)
                t["slab"].up()

            with turns(sp, WADA_SLABS // 2, t, {"slab": 2}) as i:
                for j in range(2):
                    slab("w_ada", 2 * i + j, j, C * WADA_COLS)

            sp.wait_ge(rows_ready, 1)
            sp.dma_start(bias_d, oaT[0:BIAS_ROWS, 0:2, :].rearrange("p a f -> p (a f)")).then_inc(rows_out, 16)
            sp.dma_start(bias_sub_d, oaT[0:BIAS_ROWS, 6, 0:SUB]).then_inc(rows_out, 16)
            for s in range(SEQS):
                sp.dma_start(gate2_d[s], oaT[:, 2 + 2 * s:4 + 2 * s, :].rearrange("p a f -> p (a f)"))\
                    .then_inc(rows_out, 16)
            sp.wait_ge(rows_out, 64)

            def z_load(j, table, start, width, at, rows=1, apart=0):
                src = bass.AP(tensor=table.tensor, offset=start - (P - 1), ap=[[1, P], [apart, rows], [1, width]])
                sp.dma_start(zbuf[j][:, at:at + rows * width].rearrange("p (a n) -> p a n", a=rows), src)\
                    .then_inc(z_in[j], 16)

            for s in range(SEQS):
                if s == 0:
                    sp.wait_ge(setup_done, 1)
                else:
                    sp.wait_ge(S[1].filled, s * S1_PER_SEQ)
                sp.dma_start(hT[:, :, :], ins["x_t"][s]).then_inc(x_in, 16)
                with turns(sp, HEADS // 2, t, {"slab": 2, "z0": 1, "z1": 1}) as i:
                    for j in range(2):
                        sp.wait_ge(z_read[j], t[f"z{j}"].n)
                        t[f"z{j}"].up()
                        z_load(j, bias_d, (2 * i + j) * 2 * F + (F - 384), Z_WIDE, 0)
                        slab("w_heads", 2 * i + j, j, C * 3 * P)
                with turns(sp, PAIRS // 2, t, {"slab": 6, "z0": 2, "z1": 2}) as i:
                    for b in range(2):
                        for j in range(2):
                            sp.wait_ge(z_read[j], t[f"z{j}"].n)
                            t[f"z{j}"].up()
                            head = 2 * b + j + i * 4
                            z_load(j, bias_sub_d, (head + 2 * HEADS) * SUB + P, P, 0, 2, HEADS * SUB)
                            z_load(j, bias_d, (head + HEADS) * 2 * F + (F - P), Z_BAND, 2 * P)
                        for g in range(3):
                            slab("w_heads", HEADS + 6 * i + 3 * b + g, (3 * b + g) % 2, C * 3 * P)
                with turns(sp, C // 2, t, {"slab": 2}) as i:
                    for j in range(2):
                        slab("w_merge", 2 * i + j, j, 28 * P)
                sp.wait_ge(gated, C * (s + 1))
                with turns(sp, C // 2, t, {"slab": 2, "xr": 2}) as i:
                    for j in range(2):
                        slab("w_out", 2 * i + j, j, C * P)
                        sp.wait_ge(x1_ready, t["xr"].n - j)
                        sp.dma_start(xr[j], ins["x_t"][s, :, ds(2 * i + j, 1), :].rearrange("p a f -> p (a f)"))\
                            .then_inc(xr_in[j], 16)
                        t["xr"].up()
                for tile in range(NT):
                    for which, dst in ((0, x1_d), (1, h2_d)):
                        n = 2 * (NT * s + tile) + which + 1
                        sp.wait_ge(staged_a, n)
                        sp.wait_ge(staged_v, n)
                        sp.dma_start(dst[NT * s + tile], stage[which]).then_inc(stage_out[which], 16)

                def query_slabs(head):
                    for j in range(2):
                        slab("w_query", 2 * head + j, j, (C + 1) * P)

                def store_record(head, b):
                    sp.wait_ge(record_ready, s * HEADS + head + 1)
                    for dst, src in ((experts_d, chosen), (shares_d, share)):
                        sp.dma_start(
                            dst[s * NT:(s + 1) * NT, :, ds(head * K16, K16)].rearrange("t p k -> p t k"),
                            src[:, b, :].rearrange("p (t k) -> p t k", k=K16)).then_inc(record_out[b], 16)

                query_slabs(0)
                with turns(sp, HEADS // 2 - 1, t, {"slab": 4}) as i:
                    for b in range(2):
                        query_slabs(2 * i + b + 1)
                        store_record(2 * i + b, b)
                query_slabs(HEADS - 1)
                store_record(HEADS - 2, 0)
                store_record(HEADS - 1, 1)

        @block.gpsimd
        def _(pool):
            def fence():
                pool.tensor_tensor(spare(pad_p), zeros[0:1, 0:1], zeros[0:1, 0:1], ALU.add)

            pool.memset(ones[:, :], 1.0)
            pool.memset(zeros[:, :], 0.0)
            pool.memset(eps[:, :], EPS).then_inc(consts_set, 1)
            pool.wait_ge(consts_set, 1)
            for s in range(SEQS):
                for j in range(2):
                    pool.wait_ge(stage_out[j], 16 * NT * (s + 1))
                    pool.wait_ge(record_out[j], 16 * HEADS * (s + 1))
                with pool.Fori(0, NT // 2) as i:
                    for b in range(2):
                        tile = NT * s + 2 * i + b
                        for dst, src in ((experts[:, b, :], experts_d), (shares[:, b, :], shares_d),
                                         (h2_tile[:, b, :], h2_d)):
                            pool.dma_start(dst, src[ds(tile, 1), :, :].rearrange("a p n -> (a p) n"))\
                                .then_inc(tile_in[b], 16)
                        pool.wait_ge(tile_in[b], (NT // 2 * s + i + 1) * 48)
                        fence()

                        def gather_u(group, h):
                            n = tile * GPT + group
                            pool.tensor_copy(now_u[:, h, :], experts[:, b, ds(group * GS, GS)])\
                                .then_inc(now_u_set, 1)
                            pool.wait_ge(now_u_set, n + 1)
                            for k in range(GS):
                                pool.wait_ge(u_read[k], n)
                                fence()
                                pool.indirect_dma_start(
                                    out=urows[:, k, :], out_offset=None, in_=ins["expert_u"],
                                    in_offset=bass.IndirectOffsetOnAxis(ap=now_u[:, h, k:k + 1], axis=0))\
                                    .then_inc(u_in[k], 16)

                        def gather_v(group, h):
                            n = tile * GPT + group
                            pool.tensor_copy(now_v[:, h, :], experts[:, b, ds(group * GS, GS)])\
                                .then_inc(now_v_set, 1)
                            pool.wait_ge(now_v_set, n + 1)
                            for k in range(GS):
                                pool.wait_ge(v_read_pe[k], n)
                                pool.wait_ge(v_read_dve[k], n)
                                fence()
                                pool.indirect_dma_start(
                                    out=vrows[:, k, :], out_offset=None, in_=ins["expert_v"],
                                    in_offset=bass.IndirectOffsetOnAxis(ap=now_v[:, h, k:k + 1], axis=0))\
                                    .then_inc(v_in[k], 16)

                        gather_u(0, 0)
                        with pool.Fori(0, GPT // 2 - 1) as g:
                            for h in range(2):
                                gather_u(2 * g + (h + 1), 1 - h)
                                gather_v(2 * g + h, h)
                        gather_u(GPT - 1, 1)
                        gather_v(GPT - 2, 0)
                        gather_v(GPT - 1, 1)
                        pool.wait_ge(y_out, tile * 16)
                        fence()
                        pool.dma_start(x1_tile[:, :], x1_d[ds(tile, 1), :, :].rearrange("a p n -> (a p) n"))\
                            .then_inc(final_in, 16)
                        pool.dma_start(gate2[:, :], gate2_d[s]).then_inc(final_in, 16)

        @block.tensor
        def _(pe):
            used = {b: Tally() for b in BANKS}
            t = {**used, "slab": Tally(), "mix": Tally(), "exp": Tally(), "osq": Tally()}
            slabs = t["slab"]

            def product(bank, j, lhsT, rhs, n, out=None, first=False, last=True):
                out = bank[:, :] if out is None else out
                for c in range(n):
                    mm = pe.matmul(out, lhsT(c), rhs(c), start=(c == 0), stop=(c == n - 1))
                    if first and c == 0:
                        mm.then_inc(slab_begun, 1)
                if last:
                    mm.then_inc(bank.filled, 1)
                    used[bank].up()

            pe.wait_ge(consts_in, 15 * 16)
            pe.wait_ge(consts_set, 1)
            pe.wait_ge(silu_done, 1)
            with turns(pe, WADA_SLABS // 2, t, {"slab": 2, PV: 1, XV: 1}) as i:
                for j, bank in ((0, PV), (1, XV)):
                    pe.wait_ge(slab_in[j], 16 * (i + 1))
                    pe.wait_ge(bank.emptied, used[bank].n)
                    product(bank, j, lambda c: cvec[:, c, :],
                            lambda c: w[:, j, c * WADA_COLS:(c + 1) * WADA_COLS], C,
                            out=bank[0:SEQS, 0:WADA_COLS], first=True)
                    slabs.up()
            pe.wait_ge(mod_ready, WADA_SLABS)
            pe.wait_ge(PV.emptied, used[PV].n)
            for c in range(6 * C):
                mm = pe.transpose(PV[:, SEQS * c:SEQS * (c + 1)], mod[:, c * P:(c + 1) * P],
                                  ident[0:SEQS, 0:SEQS])
            mm.then_inc(PV.filled, 1)
            used[PV].up()
            for s in range(SEQS):
                for half, bank in ((0, XV), (1, PV)):
                    pe.wait_ge(bank.emptied, used[bank].n)
                    pe.matmul(bank[:, :], pick[:, s * P:(s + 1) * P],
                              mod[:, 5 * D + half * F:5 * D + (half + 1) * F], start=True, stop=True)\
                        .then_inc(bank.filled, 1)
                    used[bank].up()
            for half, bank in ((0, XV), (1, PV)):
                pe.wait_ge(bank.emptied, used[bank].n)
                pe.matmul(bank[0:BIAS_ROWS, :], relb[:, :], onehot[:, half * F:(half + 1) * F],
                          start=True, stop=True).then_inc(bank.filled, 1)
                used[bank].up()
            pe.wait_ge(XV.emptied, used[XV].n)
            pe.matmul(XV[0:BIAS_ROWS, 0:SUB], relb[:, :], onehot[:, 2 * F:2 * F + SUB],
                      start=True, stop=True).then_inc(XV.filled, 1)
            used[XV].up()

            def gather_begin(tile, b, turn):
                pe.wait_ge(G.emptied, tile)
                pe.matmul(G[:, :], zeros[:, :], gfin[:, 0:F], start=True, stop=False, skip_group_check=True)

            def gather_front(n, group, p, b, last):
                pass

            def gather_back(n, group, b):
                for k in range(GS):
                    pe.wait_ge(vdiag_ready, n * GS + k + 1)
                    pe.wait_ge(v_in[k], (n + 1) * 16)
                    pe.matmul(G[:, :], vdiag[:, k, :], vrows[:, k, 0:F], start=False, stop=False,
                              skip_group_check=True).then_inc(v_read_pe[k], 1)

            def gather_end(tile, s, row):
                pe.matmul(G[:, :], zeros[:, :], gfin[:, 0:F], start=False, stop=True, skip_group_check=True)\
                    .then_inc(G.filled, 1)

            gather = (gather_begin, gather_front, gather_back, gather_end)

            def squares_sum(s, which):
                pe.wait_ge(PA.emptied, used[PA].n)
                for c in range(C):
                    pe.wait_ge(squared, (2 * s + which) * C + c + 1)
                    pe.matmul(PA[:, :], ones[:, :], square[c % 2], start=(c == 0), stop=(c == C - 1))\
                        .then_inc(square_read if c < C - 1 else PA.filled, 1)
                used[PA].up()

            def tokens(g, tile, c):
                if g == 0:
                    return hT[:, c, tile * P:(tile + 1) * P]
                return hT[:, c, :].rearrange("p (i r) -> p r i", r=STRIDE)[:, tile, :]

            def project(turn, j, g):
                pe.wait_ge(slab_in[j], 16 * turn)
                for x, bank in ((0, PA), (1, PV)):
                    pe.wait_ge(bank.emptied, used[bank].n)
                    product(bank, j, lambda c: w[:, j, (3 * c + x) * P:(3 * c + x + 1) * P],
                            lambda c: hT[:, c, :], C, first=(x == 0))
                pe.wait_ge(XA.emptied, used[XA].n)
                for tile in range(NT):
                    product(XA, j, lambda c: tokens(g, tile, c),
                            lambda c: w[:, j, (3 * c + 2) * P:(3 * c + 3) * P], C,
                            out=XA[:, tile * P:(tile + 1) * P], last=(tile == NT - 1))
                slabs.up()

            def attend(s, hooks):
                nonlocal slab_base
                squares_sum(s, 0)
                pe.wait_ge(h_ready, 2 * C * s + C)

                hook = Hooks(hooks, s - 1)
                hook.begin(0)
                base = slab_base // 2
                for i in rounds(bool(hooks), pe, HEADS // 2, t, {"slab": 2, PA: 4, PV: 2, XA: 6, XV: 4, S[0]: 8, S[1]: 8, O: 2,
                                               "mix": 8, "osq": 2}):
                    for j in range(2):
                        project(base + i + 1, j, 0)
                        q, k, v = qkv[0]

                        def scores(tile):
                            for x in range(2):
                                pe.wait_ge(S[x].emptied, used[S[x]].n)
                                rows = slice(x * DH, (x + 1) * DH)
                                pe.matmul(S[x][:, :], q[rows, tile * P:(tile + 1) * P], k[rows, :],
                                          start=True, stop=True).then_inc(S[x].filled, 1)
                                used[S[x]].up()

                        def transposes(tile):
                            bank = (XA, XV)[tile % 2]
                            pe.wait_ge(bank.emptied, used[bank].n)
                            pe.wait_ge(mixed, t["mix"].n + 1)
                            t["mix"].up()
                            for kt in range(NT):
                                mm = pe.transpose(bank[:, kt * P:(kt + 1) * P],
                                                  scores_sb[tile % 2][:, kt * P:(kt + 1) * P], flip[:, :])
                            mm.then_inc(bank.filled, 1)
                            used[bank].up()

                        def weigh(tile):
                            bank = (XA, XV)[tile % 2]
                            pe.wait_ge(bank.emptied, evac[tile])
                            if tile == 0:
                                pe.wait_ge(O.emptied, used[O].n)
                            for kt in range(NT):
                                mm = pe.matmul(O[:, tile * P:(tile + 1) * P], v[:, kt * P:(kt + 1) * P],
                                               probsT[tile % 2][:, kt * P:(kt + 1) * P],
                                               start=(kt == 0), stop=(kt == NT - 1))
                            if tile == NT - 1:
                                mm.then_inc(O.filled, 1)
                                used[O].up()

                        evac = {}
                        pe.wait_ge(PA.emptied, used[PA].n)
                        pe.wait_ge(PV.emptied, used[PV].n)
                        scores(0)
                        scores(1)
                        pe.wait_ge(XA.emptied, used[XA].n)
                        for tile in range(NT):
                            if tile:
                                weigh(tile - 1)
                            transposes(tile)
                            evac[tile] = used[(XA, XV)[tile % 2]].n
                            if tile + 2 < NT:
                                scores(tile + 2)
                            if tile == NT - 1:
                                weigh(tile)
                            hook.back(i * 8, NT * j + tile, 0)
                        pe.wait_ge(o_squared, t["osq"].n + 1)
                        t["osq"].up()
                        pe.wait_ge(PA.emptied, used[PA].n)
                        pe.matmul(PA[:, :], ones[:, :], o_square, start=True, stop=True).then_inc(PA.filled, 1)
                        used[PA].up()
                slab_base += HEADS
                hook.end(0)

                hook.begin(1)
                base = slab_base // 2
                for i in rounds(bool(hooks), pe, PAIRS // 2, t, {"slab": 6, PA: 6, PV: 6, XA: 22, XV: 16, S[0]: 16, S[1]: 16, O: 16,
                                               "exp": 16}):
                    for b in range(2):
                        for g in range(3):
                            at = 3 * b + g
                            project(base + 3 * i + at // 2 + 1, at % 2, g)
                            if g == 2:
                                pe.wait_ge(PA.emptied, used[PA].n)
                                pe.wait_ge(PV.emptied, used[PV].n)
                            qkv_in = used[XA].n

                        def scores(u):
                            j, tile = divmod(u, NT)
                            head = slice(j * DH, (j + 1) * DH)
                            mine = slice(tile * P, (tile + 1) * P)
                            band = slice(key_tiles(tile)[0] * P, (key_tiles(tile)[-1] + 1) * P)
                            pe.wait_ge(S[0].emptied, used[S[0]].n)
                            pe.matmul(S[0][:, 0:len(key_tiles(tile)) * P], qkv[0][0][head, mine],
                                      qkv[0][1][head, band], start=True, stop=True).then_inc(S[0].filled, 1)
                            used[S[0]].up()
                            pe.wait_ge(S[1].emptied, used[S[1]].n)
                            for x in range(2):
                                mm = pe.matmul(S[1][:, x * P:(x + 1) * P], qkv[1 + x][0][head, mine],
                                               qkv[1 + x][1][head, mine], start=True, stop=True)
                            mm.then_inc(S[1].filled, 1)
                            used[S[1]].up()

                        def transposes(u):
                            tile = u % NT
                            pe.wait_ge(dil_exped, t["exp"].n + 1)
                            t["exp"].up()
                            for bank, col, n in ((XA, 0, 2), (XV, 2 * P, len(key_tiles(tile)))):
                                pe.wait_ge(bank.emptied, used[bank].n)
                                for kt in range(n):
                                    mm = pe.transpose(bank[:, kt * P:(kt + 1) * P],
                                                      scores_sb[u % 2][:, col + kt * P:col + (kt + 1) * P],
                                                      flip[:, :])
                                mm.then_inc(bank.filled, 1)
                                used[bank].up()

                        def weigh(u):
                            tile = u % NT
                            pe.wait_ge(XA.emptied, evac[u][0])
                            pe.wait_ge(O.emptied, used[O].n)
                            for x in range(2):
                                pe.matmul(O[:, x * P:(x + 1) * P], qkv[1 + x][2][:, tile * P:(tile + 1) * P],
                                          probsT[u % 2][:, x * P:(x + 1) * P], start=True, stop=True)
                            pe.wait_ge(XV.emptied, evac[u][1])
                            kts = key_tiles(tile)
                            for n, kt in enumerate(kts):
                                mm = pe.matmul(O[:, 2 * P:3 * P], qkv[0][2][:, kt * P:(kt + 1) * P],
                                               probsT[u % 2][:, (2 + n) * P:(3 + n) * P],
                                               start=(n == 0), stop=(n == len(kts) - 1))
                            mm.then_inc(O.filled, 1)
                            used[O].up()

                        evac = {}
                        scores(0)
                        scores(1)
                        pe.wait_ge(XA.emptied, qkv_in)
                        for u in range(2 * NT):
                            if u:
                                weigh(u - 1)
                            transposes(u)
                            evac[u] = used[XA].n, used[XV].n
                            if u + 2 < 2 * NT:
                                scores(u + 2)
                            if u == 2 * NT - 1:
                                weigh(u)
                            hook.back(i * 16, 8 * b + u, 1)
                slab_base += 3 * PAIRS
                hook.end(1)
                hook.begin(2)

                pe.wait_ge(stats_ready, s + 1)
                for kind in range(2):
                    for x in range(3):
                        bank = (PV, XV)[(3 * kind + x) % 2]
                        pe.wait_ge(bank.emptied, used[bank].n)
                        for tile in range(NT):
                            mm = pe.transpose(bank[0:HEADS, tile * P:(tile + 1) * P],
                                              stat[:, kind, x, tile, :], flip[:, :])
                        mm.then_inc(bank.filled, 1)
                        used[bank].up()
                pe.wait_ge(factors_ready, s + 1)
                for pair in range(PAIRS):
                    for x, bank in enumerate((PV, XV, S[0])):
                        pe.wait_ge(bank.emptied, used[bank].n)
                        pe.matmul(bank[:, :], spread[:, pair * P:(pair + 1) * P], rows[:, 0, x, :],
                                  start=True, stop=True).then_inc(bank.filled, 1)
                        used[bank].up()

                base = slab_base // 2
                pe.wait_ge(oa_ready, HEADS * (s + 1))
                pe.wait_ge(ob_ready, s + 1)
                with turns(pe, C // 2, t, {"slab": 2, PA: 2, XA: 2, PV: 2, XV: 2}) as i:
                    for j in range(2):
                        pe.wait_ge(slab_in[j], 16 * (base + i + 1))
                        for bank, first, n, rhs in ((PA, 0, C, hT), (XA, C, C, hT), (PV, 2 * C, C, oaT),
                                                    (XV, 3 * C, PAIRS, obT)):
                            pe.wait_ge(bank.emptied, used[bank].n)
                            product(bank, j, lambda c: w[:, j, (first + c) * P:(first + c + 1) * P],
                                    lambda c: rhs[:, c, :], n, first=(first == 0))
                            if bank != PA:
                                hook.back(i * 6, 3 * j + (XA, PV, XV).index(bank), 2)
                        slabs.up()
                slab_base += C

                base = slab_base // 2
                pe.wait_ge(gated, C * (s + 1))
                for i in rounds(bool(hooks), pe, C // 2, t, {"slab": 2, PV: 2}):
                    for j in range(2):
                        pe.wait_ge(slab_in[j], 16 * (base + i + 1))
                        pe.wait_ge(PV.emptied, used[PV].n)
                        product(PV, j, lambda c: w[:, j, c * P:(c + 1) * P], lambda c: merged[:, c, :], C,
                                first=True)
                        slabs.up()
                        hook.back(i * 2, 3 * C + j, 2)
                slab_base += C
                hook.end(2)

                squares_sum(s, 1)
                pe.wait_ge(h_ready, 2 * C * s + 2 * C)
                hook.begin(3)
                for tile in range(NT):
                    for src in (x1T, hT):
                        for bank, first in ((XA, 0), (XV, NT)):
                            pe.wait_ge(bank.emptied, used[bank].n)
                            for c in range(4):
                                mm = pe.transpose(bank[:, c * P:(c + 1) * P],
                                                  src[:, first + c, tile * P:(tile + 1) * P], ident[:, :])
                            mm.then_inc(bank.filled, 1)
                            used[bank].up()
                    for x in range(2):
                        hook.back(0, 2 * tile + x, 3)

                base = slab_base // 2
                for i in rounds(bool(hooks), pe, HEADS // 2, t, {"slab": 4, PA: 2, XA: 2, S[0]: 2, S[1]: 2}):
                    for b in range(2):
                        for j, bank in ((0, PA), (1, XA)):
                            pe.wait_ge(slab_in[j], 16 * (base + 2 * i + b + 1))
                            pe.wait_ge(bank.emptied, used[bank].n)
                            product(bank, j, lambda c: w[:, j, c * P:(c + 1) * P], lambda c: hT[:, c, :], C,
                                    first=(j == 0))
                            slabs.up()
                            hook.back(i * 6, 8 + 3 * b + j, 3)
                        for j, bank in ((0, PA), (1, XA)):
                            pe.wait_ge(bank.emptied, used[bank].n)
                            pe.wait_ge(S[j].emptied, used[S[j]].n)
                            for tile in range(NT):
                                mm = pe.matmul(S[j][:, tile * P:(tile + 1) * P],
                                               qhalf[j][:, tile * P:(tile + 1) * P],
                                               w[:, j, C * P:(C + 1) * P], start=True, stop=True)
                                if (j, tile) == (1, 0):
                                    mm.then_inc(slab_begun, 1)
                            mm.then_inc(S[j].filled, 1)
                            used[S[j]].up()
                        hook.back(i * 6, 8 + 3 * b + 2, 3)
                slab_base += 2 * HEADS
                hook.end(3)

            slab_base = WADA_SLABS
            attend(0, None)
            attend(1, gather)
            gather_alone(pe, gather, t, {})

        @block.scalar
        def _(act):
            used = {b: Tally() for b in (PA, XA, O)}
            t = {**used, "exp": Tally(), "gate": Tally(), "rec": Tally()}

            act.wait_ge(consts_in, 15 * 16)
            act.wait_ge(consts_set, 1)
            act.activation(cvec[:, :, :], cvec[:, :, :], ACT.Silu).then_inc(silu_done, 1)
            act.wait_ge(lam_exp, 1)
            act.activation(lam[:, 2:4], lam[:, 0:2], ACT.Exp).then_inc(lam_exp, 1)

            def gather_begin(tile, b, turn):
                pass

            def gather_front(n, group, p, b, last):
                act.wait_ge(u_read[GS - 1], n + 1)
                act.activation(gelus[:, :], dots[:, p, :], ACT.Gelu).then_inc(gelu_done, 1)

            def gather_back(n, group, b):
                act.wait_ge(weighed, n + 1)
                for k in range(GS):
                    act.wait_ge(v_read_pe[k], n)
                    act.activation(vdiag[:, k, :], ident[:, :], ACT.Copy, scale=weights[:, k:k + 1])\
                        .then_inc(vdiag_ready, 1)

            def gather_end(tile, s, row):
                act.wait_ge(fsum_ready, tile + 1)
                act.activation(fstat[:, 1:2], fstat[:, 0:1], ACT.Sqrt, bias=eps[:, 0:1], scale=1.0 / D)\
                    .then_inc(froot_ready, 1)
                act.wait_ge(y_ready, tile + 1)
                act.dma_start(y[s][ds(row * P, P), :], x1_tile[:, :])\
                    .then_inc(y_out, 16)

            gather = (gather_begin, gather_front, gather_back, gather_end)

            def norm_root(s, which, src):
                for c in range(C):
                    if c >= 2:
                        act.wait_ge(square_read, (2 * s + which) * (C - 1) + c - 1)
                    act.activation(square[c % 2], src[:, c, :], ACT.Square).then_inc(squared, 1)
                act.wait_ge(PA.filled, used[PA].n + 1)
                act.activation(root, PA[:, :], ACT.Sqrt, bias=eps[:, 0:1], scale=1.0 / D)\
                    .then_inc(PA.emptied, 1)
                used[PA].up()

            def empty(bank, dst, src=None, scale=1.0, func=ACT.Copy):
                act.wait_ge(bank.filled, used[bank].n + 1)
                act.activation(dst, bank[:, :] if src is None else src, func, scale=scale)\
                    .then_inc(bank.emptied, 1)
                used[bank].up()

            def by_tile(bank, g=0):
                if g == 0:
                    return bank[:, :].rearrange("p (t q) -> p t q", q=P)
                return bank[:, :].rearrange("p (i r) -> p r i", r=STRIDE)

            def backwards(dst):
                return bass.AP(tensor=dst.tensor, offset=dst.offset + P - 1, ap=[dst.ap[0], [P, NT], [-1, P]])

            def unit_exps(u):
                j, tile = divmod(u, NT)
                act.wait_ge(maxed, t["exp"].n + 1)
                t["exp"].up()
                for x, (col, n) in enumerate(((0, P), (P, P), (2 * P, len(key_tiles(tile)) * P))):
                    e = act.activation(scores_sb[u % 2][:, col:col + n], scores_sb[u % 2][:, col:col + n],
                                       ACT.Exp, bias=unit_stat[:, j, 0, x, tile:tile + 1],
                                       accum_out=unit_stat[:, j, 1, x, tile:tile + 1])
                e.then_inc(dil_exped, 1)

            def exps(u, n):
                act.wait_ge(maxed, t["exp"].n + 1)
                t["exp"].up()
                for x in range(len(n)):
                    e = act.activation(scores_sb[u % 2][:, x * F:x * F + n[x]],
                                       scores_sb[u % 2][:, x * F:x * F + n[x]], ACT.Exp,
                                       bias=nm[:, u % 2, x:x + 1], accum_out=den[:, u % 2, x:x + 1])
                e.then_inc(exped, 1)

            def attend(s, hooks):
                if s == 0:
                    act.wait_ge(setup_done, 1)
                act.wait_ge(x_in, 16 * (s + 1))
                norm_root(s, 0, hT)
                hook = Hooks(hooks, s - 1)
                hook.begin(0)
                for i in rounds(bool(hooks), act, HEADS // 2, t, {PA: 4, XA: 6, O: 2, "exp": 8}):
                    for j in range(2):
                        empty(PA, backwards(qkv[0][0]), src=by_tile(PA), scale=DH ** -0.5)
                        empty(XA, qkv[0][2])
                        exps(0, (F, F))
                        for tile in range(NT):
                            if tile + 1 < NT:
                                exps(tile + 1, (F, F))
                            hook.front(i * 8, NT * j + tile, 0)
                            if tile % 2 == 0:
                                empty(XA, probsT[0][:, 0:F])
                            hook.back(i * 8, NT * j + tile, 0)
                        act.wait_ge(O.filled, used[O].n + 1)
                        used[O].up()
                        act.activation(o_square, O[:, :], ACT.Square).then_inc(o_squared, 1)
                        act.wait_ge(PA.filled, used[PA].n + 1)
                        act.activation(o_root, PA[:, :], ACT.Sqrt, bias=eps[:, 0:1], scale=1.0 / P)\
                            .then_inc(PA.emptied, 1)
                        used[PA].up()
                hook.end(0)

                hook.begin(1)
                for i in rounds(bool(hooks), act, PAIRS // 2, t, {PA: 6, XA: 22, O: 16, "exp": 16}):
                    for b in range(2):
                        for g in range(3):
                            empty(PA, backwards(qkv[g][0]), src=by_tile(PA, g), scale=DH ** -0.5)
                            empty(XA, qkv[g][2])

                        def unit_out(u):
                            j, tile = divmod(u, NT)
                            head = slice(j * DH, (j + 1) * DH)
                            act.wait_ge(O.filled, used[O].n + 1)
                            act.activation(
                                raw[head, :, ds(2 * i + b, 1), tile * P:(tile + 1) * P]
                                .rearrange("p g a f -> p g (a f)"),
                                O[head, 0:3 * P].rearrange("p (g f) -> p g f", g=3), ACT.Copy)\
                                .then_inc(O.emptied, 1)
                            used[O].up()

                        unit_exps(0)
                        for u in range(2 * NT):
                            if u + 1 < 2 * NT:
                                unit_exps(u + 1)
                            hook.front(i * 16, 8 * b + u, 1)
                            if u:
                                unit_out(u - 1)
                            empty(XA, probsT[u % 2][:, 0:2 * P], src=XA[:, 0:2 * P])
                            hook.back(i * 16, 8 * b + u, 1)
                        unit_out(2 * NT - 1)
                hook.end(1)
                hook.begin(2)
                act.wait_ge(gaps_ready, s + 1)
                act.activation(rows[:, 0, :, :], rows[:, 0, :, :], ACT.Exp).then_inc(gaps_exped, 1)

                with turns(act, C // 2, t, {PA: 2, XA: 2, "gate": 2}) as i:
                    for j in range(2):
                        hook.front(i * 6, 3 * j, 2)
                        hook.back(i * 6, 3 * j, 2)
                        act.wait_ge(gated, t["gate"].n)
                        t["gate"].up()
                        empty(PA, gate_sb[0], func=ACT.Sigmoid)
                        empty(XA, gate_sb[1], func=ACT.Sigmoid)
                        for x in range(1, 3):
                            hook.front(i * 6, 3 * j + x, 2)
                            hook.back(i * 6, 3 * j + x, 2)
                if hooks:
                    for i in rounds(True, act, C // 2, t, {}):
                        for j in range(2):
                            hook.front(i * 2, 3 * C + j, 2)
                            hook.back(i * 2, 3 * C + j, 2)
                hook.end(2)

                act.wait_ge(x1_ready, C * (s + 1))
                norm_root(s, 1, x1T)
                hook.begin(3)
                for tile in range(NT):
                    for which in range(2):
                        if NT * s + tile:
                            act.wait_ge(stage_out[which], 16 * (NT * s + tile))
                        act.wait_ge(XA.filled, used[XA].n + 1)
                        act.activation(stage[which][:, 0:F], XA[:, :], ACT.Copy).then_inc(XA.emptied, 1)
                        used[XA].up()
                        act.wait_ge(XA.emptied, used[XA].n)
                        act.activation(pad_a[:, :], eps[:, :], ACT.Copy).then_inc(staged_a, 1)
                    for x in range(2):
                        hook.front(0, 2 * tile + x, 3)
                        hook.back(0, 2 * tile + x, 3)

                for i in rounds(bool(hooks), act, HEADS // 2, t, {PA: 2, XA: 2, "rec": 2}):
                    for b in range(2):
                        for j, bank in enumerate((PA, XA)):
                            empty(bank, qhalf[j])
                            hook.front(i * 6, 8 + 3 * b + j, 3)
                            hook.back(i * 6, 8 + 3 * b + j, 3)
                        hook.front(i * 6, 8 + 3 * b + 2, 3)
                        hook.back(i * 6, 8 + 3 * b + 2, 3)
                        act.wait_ge(gap_ready, t["rec"].n + 1)
                        t["rec"].up()
                        act.activation(gexp, gap, ACT.Exp).then_inc(gap_exped, 1)
                hook.end(3)

            attend(0, None)
            attend(1, gather)
            gather_alone(act, gather, t, {})
            act.wait_ge(y_out, 16 * SEQS * NT)

        @block.vector
        def _(dve):
            used = {b: Tally() for b in BANKS}
            t = {**used, "step": Tally(), "exp": Tally(), "dil": Tally(),
                 "x1": Tally(), "rec": Tally()}
            steps = t["step"]

            def then(ins):
                ins.then_inc(step, 1)
                steps.up()
                dve.wait_ge(step, steps.n)

            def fence():
                dve.memset(spare(pad), 0.0)

            dve.wait_ge(consts_in, 15 * 16)
            then(dve.tensor_tensor(lamv[:, 0, :], lamv[:, 0, :], lamv[:, 1, :], ALU.mult))
            dve.tensor_reduce(lam[:, 0:1], lamv[:, 0, :], AX_X, ALU.add)
            then(dve.tensor_tensor(lamv[:, 2, :], lamv[:, 2, :], lamv[:, 3, :], ALU.mult))
            dve.tensor_reduce(lam[:, 1:2], lamv[:, 2, :], AX_X, ALU.add).then_inc(lam_exp, 1)
            dve.memset(mixsign[:, 0:1], 1.0)
            then(dve.tensor_scalar(gsub[:, :], gsub[:, :], 1.0 - LAM_INIT, None, ALU.mult))
            with turns(dve, WADA_SLABS // 2, t, {PV: 1, XV: 1}) as i:
                for j, bank in ((0, PV), (1, XV)):
                    dve.wait_ge(bank.filled, used[bank].n + 1)
                    dst = mod[:, ds((2 * i + j) * WADA_COLS, WADA_COLS)]
                    dve.tensor_tensor(dst, bank[0:SEQS, 0:WADA_COLS],
                                      b_ada[:, ds((2 * i + j) * WADA_COLS, WADA_COLS)], ALU.add)\
                        .then_inc(bank.emptied, 1)
                    used[bank].up()
                    dve.wait_ge(bank.emptied, used[bank].n)
                    dve.memset(spare(pad), 0.0).then_inc(mod_ready, 1)
            dve.wait_ge(lam_exp, 2)
            then(dve.tensor_tensor(lam[:, 0:1], lam[:, 3:4], lam[:, 2:3], ALU.subtract))
            then(dve.tensor_scalar(mixsign[:, 1:2], lam[:, 0:1], -LAM_INIT, None, ALU.add))
            dve.wait_ge(PV.filled, used[PV].n + 1)
            dve.tensor_copy(modT[:, :, :].rearrange("p c s -> p (c s)"), PV[:, 0:6 * C * SEQS])\
                .then_inc(PV.emptied, 1)
            used[PV].up()
            dve.wait_ge(PV.emptied, used[PV].n)
            for s in range(SEQS):
                for dst, part, g in ((scale1, 1, gmix), (scale2, 4, gffn)):
                    then(dve.scalar_tensor_tensor(out=dst[:, s, :], in0=modT[:, part * C:(part + 1) * C, s],
                                                  scalar=1.0, in1=g[:, :], op0=ALU.add, op1=ALU.mult))
            for s in range(SEQS):
                for half, bank in ((0, XV), (1, PV)):
                    dve.wait_ge(bank.filled, used[bank].n + 1)
                    dve.tensor_copy(oaT[:, 2 + 2 * s + half, :], bank[:, :]).then_inc(bank.emptied, 1)
                    used[bank].up()
            for half, bank in ((0, XV), (1, PV)):
                dve.wait_ge(bank.filled, used[bank].n + 1)
                dve.tensor_tensor(oaT[0:BIAS_ROWS, half, :], bank[0:BIAS_ROWS, :],
                                  mask[:, half * F:(half + 1) * F], ALU.add).then_inc(bank.emptied, 1)
                used[bank].up()
                dve.wait_ge(bank.emptied, used[bank].n)
            dve.wait_ge(XV.filled, used[XV].n + 1)
            dve.tensor_tensor(oaT[0:BIAS_ROWS, 6, 0:SUB], XV[0:BIAS_ROWS, 0:SUB], mask[:, 2 * F:2 * F + SUB], ALU.add)\
                .then_inc(XV.emptied, 1)
            used[XV].up()
            dve.wait_ge(XV.emptied, used[XV].n)
            dve.memset(spare(pad), 0.0).then_inc(rows_ready, 1)
            dve.wait_ge(rows_out, 64)
            dve.memset(spare(pad), 0.0).then_inc(setup_done, 1)

            def dot_products(n, p, b, ks=range(GS)):
                for k in ks:
                    dve.wait_ge(u_in[k], (n + 1) * 16)
                    dve.tensor_tensor_reduce(urows[:, k, :], urows[:, k, :], h2_tile[:, b, :], 1.0, 0.0,
                                             ALU.mult, ALU.add, dots[:, p, k:k + 1]).then_inc(u_read[k], 1)

            def gather_begin(tile, b, turn):
                then(dve.memset(vsum[:, :], 0.0))
                dve.wait_ge(tile_in[b], turn * 48)
                fence()
                dot_products(tile * GPT, 0, b)

            def gather_front(n, group, p, b, last):
                if not last:
                    dot_products(n + 1, 1 - p, b, range(GS // 2))
                dve.wait_ge(gelu_done, n + 1)
                dve.wait_ge(vdiag_ready, n * GS)
                dve.tensor_tensor(weights[:, :], gelus[:, :], shares[:, b, ds(group * GS, GS)], ALU.mult)\
                    .then_inc(weighed, 1)
                if not last:
                    dot_products(n + 1, 1 - p, b, range(GS // 2, GS))

            def gather_back(n, group, b):
                dve.wait_ge(weighed, n + 1)
                for k in range(GS):
                    dve.wait_ge(v_in[k], (n + 1) * 16)
                    dve.scalar_tensor_tensor(out=vsum[:, :], in0=vrows[:, k, F:D], scalar=weights[:, k:k + 1],
                                             in1=vsum[:, :], op0=ALU.mult, op1=ALU.add)\
                        .then_inc(v_read_dve[k], 1)
                    dve.wait_ge(v_read_dve[k], n + 1)

            def gather_end(tile, s, row):
                dve.wait_ge(final_in, (tile + 1) * 32)
                then(dve.tensor_tensor(vsum[:, :], vsum[:, :], gate2[:, F:D], ALU.mult))
                then(dve.tensor_tensor(x1_tile[:, F:D], x1_tile[:, F:D], vsum[:, :], ALU.add))
                dve.wait_ge(G.filled, tile + 1)
                dve.tensor_tensor(vsum[:, :], G[:, :], gate2[:, 0:F], ALU.mult).then_inc(G.emptied, 1)
                dve.wait_ge(G.emptied, tile + 1)
                then(dve.tensor_tensor(x1_tile[:, 0:F], x1_tile[:, 0:F], vsum[:, :], ALU.add))
                for half in range(2):
                    cols = slice(half * F, (half + 1) * F)
                    then(dve.tensor_tensor_reduce(vsum[:, :], x1_tile[:, cols], x1_tile[:, cols], 1.0, 0.0,
                                                  ALU.mult, ALU.add, fstat[:, 2 + half:3 + half]))
                dve.tensor_tensor(fstat[:, 0:1], fstat[:, 2:3], fstat[:, 3:4], ALU.add).then_inc(fsum_ready, 1)
                dve.wait_ge(froot_ready, tile + 1)
                then(dve.reciprocal(fstat[:, 2:3], fstat[:, 1:2]))
                dve.scalar_tensor_tensor(out=x1_tile[:, :], in0=x1_tile[:, :], scalar=fstat[:, 2:3],
                                         in1=gfin[:, :], op0=ALU.mult, op1=ALU.mult).then_inc(y_ready, 1)

            gather = (gather_begin, gather_front, gather_back, gather_end)

            def modulate(s, which, src):
                used[PA].up()
                dve.wait_ge(PA.emptied, used[PA].n)
                then(dve.reciprocal(root, root))
                scale, shift = ((scale1, 0), (scale2, 3))[which]
                for c in range(C):
                    last = dve.tensor_tensor(hT[:, c, :], src[:, c, :], root, ALU.mult)
                then(last)
                for c in range(C):
                    dve.tensor_scalar(hT[:, c, :], hT[:, c, :], scale[:, s, c:c + 1],
                                      modT[:, shift * C + c, s:s + 1], ALU.mult, ALU.add).then_inc(h_ready, 1)

            def bias_max(u, parts):
                for x, (bank, col, n, z) in enumerate(parts):
                    dve.wait_ge(bank.filled, used[bank].n + 1)
                    fence()
                    dve.tensor_tensor_reduce(scores_sb[u % 2][:, col:col + n], bank[:, 0:n], z, 1.0, LOWEST,
                                             ALU.add, ALU.max, mx[:, u % 2, x:x + 1]).then_inc(bank.emptied, 1)
                    used[bank].up()
                dve.wait_ge(parts[-1][0].emptied, used[parts[-1][0]].n)

            def in_order(x, g, back=False):
                if g == 0:
                    return x
                return x.rearrange("p (r i) -> p r i" if back else "p (i r) -> p r i", r=STRIDE)

            def merge_groups(s):
                dve.memset(spare(pad), 0.0).then_inc(stats_ready, 1)
                order = (1, 2, 0)
                for kind in range(2):
                    for x, g in enumerate(order):
                        bank = (PV, XV)[(3 * kind + x) % 2]
                        dve.wait_ge(bank.filled, used[bank].n + 1)
                        src, dst = bank[0:HEADS, :], rows[:, kind, x, :]
                        if g:
                            src = src.rearrange("p (r i) -> p r i", r=STRIDE)
                            dst = dst.rearrange("p (i r) -> p r i", r=STRIDE)
                        dve.tensor_copy(dst, src).then_inc(bank.emptied, 1)
                        used[bank].up()
                        dve.wait_ge(bank.emptied, used[bank].n)
                then(dve.tensor_tensor(least, rows[:, 0, 0, :], rows[:, 0, 1, :], ALU.min))
                then(dve.tensor_tensor(least, least, rows[:, 0, 2, :], ALU.min))
                dve.tensor_tensor(rows[:, 0, :, :], least.unsqueeze(1).broadcast_to([HEADS, 3, F]),
                                  rows[:, 0, :, :], ALU.subtract).then_inc(gaps_ready, 1)
                dve.wait_ge(gaps_exped, s + 1)
                then(dve.tensor_tensor(rows[:, 1, :, :], rows[:, 1, :, :], rows[:, 0, :, :], ALU.mult))
                then(dve.tensor_tensor(total, rows[:, 1, 0, :], rows[:, 1, 1, :], ALU.add))
                then(dve.tensor_tensor(total, total, rows[:, 1, 2, :], ALU.add))
                then(dve.reciprocal(total, total))
                dve.tensor_tensor(rows[:, 0, :, :], rows[:, 0, :, :],
                                  total.unsqueeze(1).broadcast_to([HEADS, 3, F]), ALU.mult)\
                    .then_inc(factors_ready, 1)
                for pair in range(PAIRS):
                    for x, (g, bank) in enumerate(zip(order, (PV, XV, S[0]))):
                        dve.wait_ge(bank.filled, used[bank].n + 1)
                        src, dst, factor = raw[:, x, pair, :], obT[:, pair, :], bank[:, :]
                        if g:
                            src = src.rearrange("p (r i) -> p i r", r=STRIDE)
                            dst = addend[x].rearrange("p (i r) -> p i r", r=STRIDE)
                            factor = factor.rearrange("p (i r) -> p i r", r=STRIDE)
                        dve.tensor_tensor(dst, factor, src, ALU.mult).then_inc(bank.emptied, 1)
                        used[bank].up()
                        dve.wait_ge(bank.emptied, used[bank].n)
                    for x in range(2):
                        last = dve.tensor_tensor(obT[:, pair, :], obT[:, pair, :], addend[x], ALU.add)
                        if (pair, x) == (PAIRS - 1, 1):
                            last.then_inc(ob_ready, 1)
                        else:
                            then(last)

            def attend(s, hooks):
                dve.wait_ge(x_in, 16 * (s + 1))
                modulate(s, 0, hT)
                hook = Hooks(hooks, s - 1)
                hook.begin(0)
                for i in rounds(bool(hooks), dve, HEADS // 2, t, {PA: 4, PV: 2, XV: 4, S[0]: 8, S[1]: 8, O: 2,
                                                "exp": 8, "step": 26}):
                    for j in range(2):
                        used[PA].up()
                        dve.wait_ge(PV.filled, used[PV].n + 1)
                        dve.tensor_copy(qkv[0][1], PV[:, :]).then_inc(PV.emptied, 1)
                        used[PV].up()
                        dve.wait_ge(z_in[j], (i + 1) * 16 + s * Z_PER_SEQ)

                        def unit_max(tile):
                            at = 384 - tile * P
                            bias_max(tile, [(S[x], x * F, F, zbuf[j][:, at:at + F]) for x in range(2)])
                            dve.tensor_scalar(nm[:, tile % 2, :], mx[:, tile % 2, 0:2], -1.0, None, ALU.mult)\
                                .then_inc(maxed, 1)

                        def unit_mix(tile):
                            dve.wait_ge(exped, t["exp"].n + 1)
                            t["exp"].up()
                            then(dve.reciprocal(rden[:, tile % 2, :], den[:, tile % 2, :]))
                            then(dve.tensor_tensor(rden[:, tile % 2, :], rden[:, tile % 2, :], mixsign[:, :],
                                                   ALU.mult))
                            p1, p2 = (scores_sb[tile % 2][:, x * F:(x + 1) * F] for x in range(2))
                            then(dve.tensor_scalar(p2, p2, rden[:, tile % 2, 1:2], None, ALU.mult))
                            dve.scalar_tensor_tensor(out=p1, in0=p1, scalar=rden[:, tile % 2, 0:1], in1=p2,
                                                     op0=ALU.mult, op1=ALU.add).then_inc(mixed, 1)

                        unit_max(0)
                        for tile in range(NT):
                            if tile + 1 < NT:
                                unit_max(tile + 1)
                            if tile == NT - 2:
                                dve.memset(spare(pad), 0.0).then_inc(z_read[j], 1)
                            unit_mix(tile)
                            hook.front(i * 8, NT * j + tile, 0)
                            if tile % 2 == 1:
                                dve.wait_ge(XV.filled, used[XV].n + 1)
                                dve.tensor_copy(probsT[1][:, 0:F], XV[:, :]).then_inc(XV.emptied, 1)
                                used[XV].up()
                            hook.back(i * 8, NT * j + tile, 0)
                        used[PA].up()
                        dve.wait_ge(PA.emptied, used[PA].n)
                        then(dve.reciprocal(o_root, o_root))
                        dve.wait_ge(O.filled, used[O].n + 1)
                        dve.scalar_tensor_tensor(
                            out=oaT[:, ds(2 * i + j, 1), :].rearrange("p a f -> p (a f)"), in0=O[:, :],
                            scalar=gsub[:, 0:1], in1=o_root, op0=ALU.mult, op1=ALU.mult).then_inc(O.emptied, 1)
                        used[O].up()
                dve.wait_ge(O.emptied, used[O].n)
                dve.memset(spare(pad), 0.0).then_inc(oa_ready, HEADS)
                hook.end(0)

                hook.begin(1)
                for i in rounds(bool(hooks), dve, PAIRS // 2, t, {PV: 6, XV: 16, S[0]: 16, S[1]: 16, "dil": 16,
                                                "step": 4}):
                    for b in range(2):
                        for g in range(3):
                            dve.wait_ge(PV.filled, used[PV].n + 1)
                            dve.tensor_copy(in_order(qkv[g][1], g, back=True), in_order(PV[:, :], g))\
                                .then_inc(PV.emptied, 1)
                            used[PV].up()

                        def unit_max(u):
                            j, tile = divmod(u, NT)
                            z = zbuf[j]
                            if tile == 0:
                                dve.wait_ge(z_in[j], (2 * i + b + 1) * 32 + (s * Z_PER_SEQ + HEADS // 2 * 16))
                            kts = key_tiles(tile)
                            band = 2 * P + (kts[0] - tile + 1) * P
                            dve.wait_ge(S[0].filled, used[S[0]].n + 1)
                            fence()
                            dve.tensor_tensor_reduce(scores_sb[u % 2][:, 2 * P:(2 + len(kts)) * P],
                                                     S[0][:, 0:len(kts) * P], z[:, band:band + len(kts) * P],
                                                     1.0, LOWEST, ALU.add, ALU.max, mx[:, u % 2, 2:3])\
                                .then_inc(S[0].emptied, 1)
                            used[S[0]].up()
                            dve.wait_ge(S[1].filled, used[S[1]].n + 1)
                            fence()
                            for x in range(2):
                                cols = slice(x * P, (x + 1) * P)
                                last = dve.tensor_tensor_reduce(scores_sb[u % 2][:, cols], S[1][:, cols], z[:, cols],
                                                                1.0, LOWEST, ALU.add, ALU.max,
                                                                mx[:, u % 2, x:x + 1])
                            last.then_inc(S[1].emptied, 1)
                            used[S[1]].up()
                            dve.wait_ge(S[1].emptied, used[S[1]].n)
                            dve.tensor_scalar(unit_stat[:, j, 0, :, tile], mx[:, u % 2, 0:3], -1.0, None, ALU.mult)\
                                .then_inc(maxed, 1)
                            if tile == NT - 1:
                                dve.memset(spare(pad), 0.0).then_inc(z_read[j], 1)

                        def head_stats(j):
                            dve.wait_ge(dil_exped, t["dil"].n + 1)
                            then(dve.tensor_copy(
                                stat[:, :, :, :, ds(4 * i + 2 * b + j, 1)].rearrange("p k g t h -> p (k g t h)"),
                                unit_stat[:, j, :, :, :].rearrange("p k g t -> p (k g t)")))

                        unit_max(0)
                        for u in range(2 * NT):
                            if u + 1 < 2 * NT:
                                unit_max(u + 1)
                            hook.front(i * 16, 8 * b + u, 1)
                            dve.wait_ge(XV.filled, used[XV].n + 1)
                            n = len(key_tiles(u % NT)) * P
                            dve.tensor_copy(probsT[u % 2][:, 2 * P:2 * P + n], XV[:, 0:n]).then_inc(XV.emptied, 1)
                            used[XV].up()
                            if u % NT == NT - 1:
                                head_stats(u // NT)
                            t["dil"].up()
                            hook.back(i * 16, 8 * b + u, 1)
                used[O].up(2 * NT * PAIRS)
                used[PA].up(3 * PAIRS)
                hook.end(1)
                hook.begin(2)

                merge_groups(s)

                used[XA].up(3 * HEADS + 11 * PAIRS)
                with turns(dve, C // 2, t, {PA: 2, XA: 2, PV: 2, XV: 2}) as i:
                    for j in range(2):
                        for x in range(3):
                            hook.front(i * 6, 3 * j + x, 2)
                            hook.back(i * 6, 3 * j + x, 2)
                        for x, (gate, bank) in enumerate(((PA, PV), (XA, XV))):
                            used[gate].up()
                            dve.wait_ge(gate.emptied, used[gate].n)
                            dve.wait_ge(bank.filled, used[bank].n + 1)
                            dve.tensor_tensor(gate_sb[2 + x], bank[:, :], gate_sb[x], ALU.mult)\
                                .then_inc(bank.emptied, 1)
                            used[bank].up()
                        dve.wait_ge(XV.emptied, used[XV].n)
                        dve.tensor_tensor(merged[:, ds(2 * i + j, 1), :].rearrange("p a f -> p (a f)"),
                                          gate_sb[2], gate_sb[3], ALU.add).then_inc(gated, 1)
                for i in rounds(bool(hooks), dve, C // 2, t, {PV: 2, "x1": 2}):
                    for j in range(2):
                        hook.front(i * 2, 3 * C + j, 2)
                        hook.back(i * 2, 3 * C + j, 2)
                        dve.wait_ge(PV.filled, used[PV].n + 1)
                        dve.wait_ge(xr_in[j], (i + (1 + s * C // 2)) * 16)
                        dve.scalar_tensor_tensor(
                            out=x1T[:, ds(2 * i + j, 1), :].rearrange("p a f -> p (a f)"), in0=PV[:, :],
                            scalar=modT[:, ds(2 * C + 2 * i + j, 1), s:s + 1].rearrange("p a b -> p (a b)"),
                            in1=xr[j], op0=ALU.mult, op1=ALU.add).then_inc(PV.emptied, 1)
                        used[PV].up()
                        dve.wait_ge(PV.emptied, used[PV].n)
                        dve.memset(spare(pad), 0.0).then_inc(x1_ready, 1)
                        t["x1"].up()
                hook.end(2)

                modulate(s, 1, x1T)
                hook.begin(3)
                for tile in range(NT):
                    for which in range(2):
                        if NT * s + tile:
                            dve.wait_ge(stage_out[which], 16 * (NT * s + tile))
                        dve.wait_ge(XV.filled, used[XV].n + 1)
                        dve.tensor_copy(stage[which][:, F:D], XV[:, :]).then_inc(XV.emptied, 1)
                        used[XV].up()
                        used[XA].up()
                        dve.wait_ge(XV.emptied, used[XV].n)
                        dve.memset(spare(pad), 0.0).then_inc(staged_v, 1)
                    for x in range(2):
                        hook.front(0, 2 * tile + x, 3)
                        hook.back(0, 2 * tile + x, 3)

                for i in rounds(bool(hooks), dve, HEADS // 2, t, {S[0]: 2, S[1]: 2, "rec": 2, "step": 48}):
                    for b in range(2):
                        for j in range(2):
                            hook.front(i * 6, 8 + 3 * b + j, 3)
                            hook.back(i * 6, 8 + 3 * b + j, 3)
                        for j in range(2):
                            dve.wait_ge(S[j].filled, used[S[j]].n + 1)
                            fence()
                            sc = S[j][:, :].rearrange("p (t k) -> p t k", k=P)
                            for tile in range(NT):
                                last = dve.max(topv[j][:, tile, 0:8], sc[:, tile, :])
                            then(last)
                            fence()
                            for tile in range(NT):
                                dve.match_replace(rest[:, tile, :], topv[j][:, tile, 0:8], sc[:, tile, :], LOWEST)
                            for tile in range(NT):
                                last = dve.max_index(topi[j][:, tile, 0:8], topv[j][:, tile, 0:8], sc[:, tile, :])
                            last.then_inc(S[j].emptied, 1)
                            used[S[j]].up()
                            dve.wait_ge(S[j].emptied, used[S[j]].n)
                            fence()
                            for tile in range(NT):
                                last = dve.max(topv[j][:, tile, 8:16], rest[:, tile, :])
                            then(last)
                            fence()
                            for tile in range(NT):
                                last = dve.max_index(topi[j][:, tile, 8:16], topv[j][:, tile, 8:16],
                                                     rest[:, tile, :])
                            then(last)
                            then(dve.tensor_copy(topf[j], topi[j].rearrange("p t k -> p (t k)")))
                        hook.front(i * 6, 8 + 3 * b + 2, 3)
                        hook.back(i * 6, 8 + 3 * b + 2, 3)
                        for tile in range(NT):
                            last = dve.tensor_tensor(
                                cand[:, tile, :].rearrange("p (a b) -> p a b", b=K16),
                                topv[0][:, tile, :].unsqueeze(2).broadcast_to([P, K16, K16]),
                                topv[1][:, tile, :].unsqueeze(1).broadcast_to([P, K16, K16]), ALU.add)
                        then(last)
                        fence()
                        for tile in range(NT):
                            last = dve.max(candv[:, tile, 0:8], cand[:, tile, :])
                        then(last)
                        fence()
                        for tile in range(NT):
                            dve.match_replace(cand2[:, tile, :], candv[:, tile, 0:8], cand[:, tile, :], LOWEST)
                        for tile in range(NT):
                            last = dve.max_index(candi[:, tile, 0:8], candv[:, tile, 0:8], cand[:, tile, :])
                        then(last)
                        fence()
                        for tile in range(NT):
                            last = dve.max(candv[:, tile, 8:16], cand2[:, tile, :])
                        then(last)
                        dve.tensor_tensor(gap.rearrange("p (t k) -> p t k", k=K16), candv,
                                          candv[:, :, 0:1].broadcast_to([P, NT, K16]), ALU.subtract)\
                            .then_inc(gap_ready, 1)
                        for tile in range(NT):
                            last = dve.max_index(candi[:, tile, 8:16], candv[:, tile, 8:16], cand2[:, tile, :])
                        then(last)
                        flat = candi.rearrange("p t k -> p (t k)")
                        dve.tensor_single_scalar(parti[0], flat, 4, op=ALU.logical_shift_right)
                        then(dve.tensor_single_scalar(parti[1], flat, 15, op=ALU.bitwise_and))
                        dve.tensor_copy(partf[0], parti[0])
                        then(dve.tensor_copy(partf[1], parti[1]))
                        for j in range(2):
                            then(dve.tensor_tensor(
                                hot.rearrange("p (a b) -> p a b", b=K16),
                                partf[j].unsqueeze(2).broadcast_to([P, TK, K16]),
                                iota16[:, :].unsqueeze(1).broadcast_to([P, TK, K16]), ALU.is_equal))
                            then(dve.tensor_tensor(
                                hot2.rearrange("p (t a b) -> p t a b", t=NT, b=K16),
                                hot.rearrange("p (t a b) -> p t a b", t=NT, b=K16),
                                topf[j].rearrange("p (t k) -> p t k", k=K16).unsqueeze(2)
                                .broadcast_to([P, NT, K16, K16]), ALU.mult))
                            then(dve.tensor_reduce(keyno[j], hot2.rearrange("p (a b) -> p a b", b=K16), AX_X,
                                                   ALU.add))
                        then(dve.scalar_tensor_tensor(out=expert_f, in0=keyno[0], scalar=float(P), in1=keyno[1],
                                                      op0=ALU.mult, op1=ALU.add))
                        dve.wait_ge(record_out[b], (i + s * HEADS // 2) * 32)
                        dve.tensor_copy(chosen[:, b, :], expert_f)
                        dve.wait_ge(gap_exped, t["rec"].n + 1)
                        then(dve.tensor_reduce(gsum, gexp.rearrange("p (t k) -> p t k", k=K16), AX_X, ALU.add))
                        then(dve.reciprocal(grec, gsum))
                        dve.tensor_tensor(share[:, b, :].rearrange("p (t k) -> p t k", k=K16),
                                          gexp.rearrange("p (t k) -> p t k", k=K16),
                                          grec.unsqueeze(2).broadcast_to([P, NT, K16]), ALU.mult)\
                            .then_inc(record_ready, 1)
                        t["rec"].up()
                used[PA].up(HEADS)
                used[XA].up(HEADS)
                for j in range(2):
                    dve.wait_ge(stage_out[j], 16 * NT * (s + 1))
                hook.end(3)

            attend(0, None)
            attend(1, gather)
            gather_alone(dve, gather, t, {"step": 14})


def slabs_of(weight, columns):
    rows = weight.shape[0] // P
    return np.stack([np.ascontiguousarray(weight[:, cols].reshape(rows, P, -1).transpose(1, 0, 2)).reshape(P, -1)
                     for cols in columns])


def bucket_table(rel):
    half, exact = BUCKETS // 2, BUCKETS // 4
    n = np.abs(rel)
    nf = np.maximum(n, exact).astype(np.float32)
    large = exact + (np.log(nf / np.float32(exact)) / np.float32(math.log(MAX_DISTANCE / exact))
                     * np.float32(half - exact)).astype(np.int32)
    bucket = np.where(rel > 0, half, 0) + np.where(n < exact, n, np.minimum(large, half - 1))
    return (np.arange(BUCKETS)[:, None] == bucket[None, :]).astype(np.float32)


def bias_tables():
    near, steps = np.arange(2 * F) - F, np.arange(SUB) - P
    onehot = np.concatenate([bucket_table(near), bucket_table(STRIDE * steps)], 1)
    mask = np.zeros((BIAS_ROWS, onehot.shape[1]), np.float32)
    mask[HEADS:, 0:2 * F] = np.where(np.abs(near) <= GROUPS[0][0] // 2, 0.0, MASKED)
    for g, (window, dilation) in enumerate(GROUPS):
        reached = (np.abs(STRIDE * steps) <= window // 2) & (STRIDE * steps % dilation == 0)
        mask[(1 + g) * HEADS:(2 + g) * HEADS, 2 * F:] = np.where(reached, 0.0, MASKED)
    return onehot, mask


def layout(inputs):
    def col(v):
        return np.ascontiguousarray(v.reshape(-1, P).T)

    a = {k: np.asarray(v) for k, v in inputs.items()}
    w_in, span = a["w_in"][0], np.arange(P)
    heads = [np.concatenate([x * D + h * P + span for x in range(3)]) for h in range(HEADS)]
    qkv_b = len(GROUPS) * HEADS * DH
    for pair in range(PAIRS):
        for g in range(len(GROUPS)):
            heads.append(np.concatenate([3 * D + x * qkv_b + g * HEADS * DH + pair * P + span for x in range(3)]))
    gates = 3 * D + 3 * qkv_b
    chunks = [c * P + span for c in range(C)]
    ga = slabs_of(w_in, [gates + c for c in chunks])
    gb = slabs_of(w_in, [gates + D + c for c in chunks])
    onehot, mask = bias_tables()
    keys = np.stack([a["sub_keys_1"][0], a["sub_keys_2"][0]], 1).reshape(2 * HEADS, P, P).transpose(0, 2, 1)
    xs = [a["x_prompt"][0], a["x_sample"][0]]
    return {
        "x_t": np.stack([x.T.reshape(C, P, F).transpose(1, 0, 2) for x in xs]),
        "c_t": np.stack([col(a["c_prompt"][0]), col(a["c_sample"][0])], -1),
        "w_ada": slabs_of(a["w_ada"][0], [n * WADA_COLS + np.arange(WADA_COLS) for n in range(WADA_SLABS)]),
        "b_ada": np.stack([a["b_ada"][0]] * SEQS),
        "g_mix": col(a["g_norm_mix"][0]),
        "g_ffn": col(a["g_norm_ffn"][0]),
        "g_final": np.stack([a["g_final"]] * P),
        "g_sub": col(a["g_subln"][0]),
        "lambdas": np.stack([np.stack([a[f"lambda_{x}"][0] for x in ("q1", "k1", "q2", "k2")])] * P),
        "rel_bias": a["rel_bias"],
        "w_heads": slabs_of(w_in, heads),
        "w_merge": np.concatenate([ga, gb, slabs_of(a["w_proj_a"][0], chunks), slabs_of(a["w_proj_b"][0], chunks)], 2),
        "w_out": slabs_of(a["w_out"][0], chunks),
        "w_query": np.concatenate([slabs_of(a["w_query"][0], [m * P + span for m in range(2 * HEADS)]), keys], 2),
        "expert_u": a["expert_u"][0],
        "expert_v": a["expert_v"][0],
        "ident": np.eye(P, dtype=np.float32),
        "flip": np.eye(P, dtype=np.float32)[::-1],
        "iota16": np.stack([np.arange(K16, dtype=np.float32)] * P),
        "pick": np.repeat(np.eye(SEQS, dtype=np.float32), P, 1),
        "onehot": onehot,
        "mask": mask,
        "spread": np.repeat(np.eye(HEADS, dtype=np.float32), DH, 1),
    }


def kernel(**inputs):
    import concourse.bacc as bacc
    from concourse.bass_utils import run_bass_kernel_spmd

    nc = bacc.Bacc("TRN2", target_bir_lowering=False, num_devices=1)
    arrays = {"in_" + name: np.ascontiguousarray(v) for name, v in layout(inputs).items()}
    ins = {name[3:]: nc.dram_tensor(name, v.shape, mybir.dt.from_np(v.dtype), kind="ExternalInput").ap()
           for name, v in arrays.items()}
    y = [nc.dram_tensor(name, (F, D), F32, kind="ExternalOutput").ap() for name in ("y_prompt", "y_sample")]
    build(nc, ins, y)
    r = run_bass_kernel_spmd(nc, [arrays], core_ids=[0])
    return tuple(r.results[0][name].reshape(1, F, D) for name in ("y_prompt", "y_sample"))
```

```python
import math
from contextlib import ExitStack, contextmanager

import numpy as np

import concourse.bass as bass
from concourse import mybir

F32 = mybir.dt.float32
U32 = mybir.dt.uint32
ALU = mybir.AluOpType
ACT = mybir.ActivationFunctionType
AX_X = mybir.AxisListType.X
ds = bass.ds

P = 128
D = 1024
C = D // P
F = 512
NT = F // P
SEQS = 2
HEADS = 8
DH = 64
GROUPS = ((128, 1), (512, 4), (2048, 16))
PAIRS = HEADS // 2
STRIDE = 4
BUCKETS = 32
MAX_DISTANCE = 1024
BIAS_ROWS = HEADS * (1 + len(GROUPS))
K16 = 16
SLOTS = HEADS * K16
GS = 4
GPT = SLOTS // GS
EPS = 1e-6
MASKED = -1e30
LOWEST = -3e38
LAM_INIT = 0.8 - 0.6 * math.exp(0.0)

W_FREE = 28 * P
WADA_COLS = 384
WADA_SLABS = 6 * D // WADA_COLS

Z_WIDE = 896
Z_BAND = 384
SUB = 2 * P
DIL_FREE = 2 * P + Z_BAND
R_Z = 0
R_SC = R_Z + 2 * Z_WIDE
R_PT = R_SC + 2 * 2 * F
R_QKV = R_PT + 2 * DIL_FREE
R_RAW = R_QKV + 9 * F
R_END = R_RAW + 3 * PAIRS * F
R_MOD = R_RAW
R_ONEHOT = R_QKV
R_MASK = R_ONEHOT + 2 * F + SUB
R_DIAG = R_MASK + 2 * F + SUB
R_ROWS = R_SC
R_PART = R_QKV
R_RT, R_SQ = R_SC, R_SC + F
R_GATE = R_SC
R_MERGED = R_QKV
R_X1T = R_RAW
R_XR = R_PT
R_STAGE = R_QKV
R_ROUTE = R_RAW


class Tally:

    def __init__(self):
        self.start, self.step = 0, 0

    @property
    def n(self):
        return self.start + self.step

    def up(self, k=1):
        self.step += k


@contextmanager
def turns(eng, count, tallies, per_turn):
    assert set(per_turn) <= set(tallies)
    starts = {t: tallies[t].n for t in tallies}
    with eng.Fori(0, count) as i:
        for t in tallies:
            k = per_turn.get(t, 0)
            tallies[t].start = i * k + starts[t] if k else starts[t]
            tallies[t].step = 0
        yield i
        for t in tallies:
            assert tallies[t].step == per_turn.get(t, 0), (t, tallies[t].step, per_turn.get(t, 0))
    for t in tallies:
        tallies[t].start, tallies[t].step = starts[t] + count * per_turn.get(t, 0), 0


def key_tiles(tile):
    return range(max(tile - 1, 0), min(tile + 2, NT))


def rounds(peel, eng, count, tallies, per_turn):
    with turns(eng, count - 1 if peel else count, tallies, per_turn) as i:
        yield i
    if peel:
        yield count - 1


def heads_of_attention(eng, tallies, per_turn, head):
    head(0, 0, 1, True, False)
    with turns(eng, HEADS // 2 - 1, tallies, per_turn) as i:
        head(2 * i + 1, 1, i + 2, False, False)
        head(2 * i + 2, 0, i + 2, False, False)
    head(HEADS - 1, 1, HEADS // 2 + 1, False, True)


class Hooks:

    def __init__(self, gather, seq):
        self.gather, self.seq = gather, seq

    def begin(self, tile):
        if self.gather:
            n = NT * self.seq + tile
            self.gather[0](n, tile % 2, n // 2 + 1)

    def front(self, base, k, tile):
        if self.gather:
            group = base + k
            last = isinstance(group, int) and group == GPT - 1
            self.gather[1]((NT * self.seq + tile) * GPT + group, group, k % 2, tile % 2, last)

    def back(self, base, k, tile):
        if self.gather:
            group = base + k
            self.gather[2]((NT * self.seq + tile) * GPT + group, group, tile % 2)

    def front_on(self, n, tile):
        self.front(0, n % GPT, tile + n // GPT)

    def back_on(self, n, tile):
        self.back(0, n % GPT, tile + n // GPT)
        if n % GPT == GPT - 1:
            self.end(tile + n // GPT)
            self.begin(tile + n // GPT + 1)

    def end(self, tile):
        if self.gather:
            self.gather[3](NT * self.seq + tile, self.seq, tile)


UNITS = (2 * NT, 2, 2)
PLACE = (2, 0, 1)


def hooks_of_step(pair, g, u):
    at = {0: (0, 2, 4, 6, 7), 1: (0, 1, 1), 2: (0, 1, 1)}[g]
    before = 11 * pair + (0, 5, 8)[g]
    return [before + n for n, unit in enumerate(at) if unit == u]


DIL_HOOKS = 11 * PAIRS - GPT


def steps_of_pairs(i):
    return [(3 * b + g, b, g, (i, b, g) == (PAIRS // 2 - 1, 1, 2)) for b in range(2) for g in range(3)]


def gather_alone(eng, gather, tallies, per_turn):
    begin, front, back, end = gather
    seq = SEQS - 1
    with turns(eng, NT // 2, tallies, per_turn) as i:
        for b in range(2):
            tile = 2 * i + (NT * seq + b)
            begin(tile, b, i + (NT * seq // 2 + 1))
            with eng.Fori(0, GPT // 2 - 1) as g:
                for p in range(2):
                    front(tile * GPT + (2 * g + p), 2 * g + p, p, b, False)
                    back(tile * GPT + (2 * g + p), 2 * g + p, b)
            for p in range(2):
                front(tile * GPT + (GPT - 2 + p), GPT - 2 + p, p, b, p == 1)
                back(tile * GPT + (GPT - 2 + p), GPT - 2 + p, b)
            end(tile, seq, 2 * i + b)


def build(nc, ins, y):
    es = ExitStack()
    with es:
        def sb(name, shape, dt=F32):
            return es.enter_context(nc.sbuf_tensor(name, shape, dt))

        def sem(name):
            return es.enter_context(nc.semaphore(name))

        def scratch(name, shape, dt=F32):
            return nc.dram_tensor(name, shape, dt, kind="Internal").ap()

        bias_d = scratch("bias_rows", [BIAS_ROWS, 2 * F])
        bias_sub_d = scratch("bias_rows_stride", [BIAS_ROWS, SUB])
        gate2_d = scratch("gate2_rows", [SEQS, P, D])
        x1_d = scratch("x1_tiles", [SEQS * NT, P, D])
        h2_d = scratch("h2_tiles", [SEQS * NT, P, D])
        experts_d = scratch("experts", [SEQS * NT, P, SLOTS], U32)
        shares_d = scratch("shares", [SEQS * NT, P, SLOTS])

        hT = sb("hT", [P, C, F])
        oaT = sb("oaT", [P, HEADS, F])
        region = sb("region", [P, R_END])
        w = sb("w", [P, 2, W_FREE])
        urows = sb("urows", [P, GS, D])
        vrows = sb("vrows", [P, GS, D])
        h2_tile = sb("h2_tile", [P, 2, D])
        x1_tile = sb("x1_tile", [P, D])
        gate2 = sb("gate2", [P, D])
        gfin = sb("gfin", [P, D])
        vsum = sb("vsum", [P, F])
        vdiag = sb("vdiag", [P, GS, P])
        experts = sb("experts_tile", [P, 2, SLOTS], U32)
        shares = sb("shares_tile", [P, 2, SLOTS])
        now_u = sb("experts_now_u", [P, 2, GS], U32)
        now_v = sb("experts_now_v", [P, 2, GS], U32)
        dots = sb("dots", [P, 2, GS])
        gelus = sb("gelus", [P, GS])
        weights = sb("weights", [P, GS])
        fstat = sb("fstat", [P, 4])
        ident = sb("ident", [P, P])
        flip = sb("flip", [P, P])
        ones = sb("ones", [P, P])
        zeros = sb("zeros", [P, P])
        eps = sb("eps", [P, 1])
        mx = sb("mx", [P, 2, NT])
        nm = sb("nm", [P, 2, 2])
        den = sb("den", [P, 2, 2])
        rden = sb("rden", [P, 2, 2])
        unit_stat = sb("unit_stat", [P, 3, 2, NT, 2])
        stat = sb("stat", [P, 3, 2, NT, HEADS])
        spread = sb("spread", [HEADS, PAIRS * P])
        cvec = sb("cvec", [P, C, SEQS])
        gmix = sb("gmix", [P, C])
        gffn = sb("gffn", [P, C])
        gsub = sb("gsub", [P, 1])
        lamv = sb("lamv", [P, 4, DH])
        lam = sb("lam", [P, 4])
        mixsign = sb("mixsign", [P, 2])
        relb = sb("relb", [BUCKETS, BIAS_ROWS])
        modT = sb("modT", [P, 6 * C, SEQS])
        b_ada = sb("b_ada", [P, 6 * C * SEQS])
        scale1 = sb("scale1", [P, SEQS, C])
        scale2 = sb("scale2", [P, SEQS, C])
        iota16 = sb("iota16", [P, K16])
        chosen = sb("chosen", [P, 2, NT * K16], U32)
        share = sb("share", [P, 2, NT * K16])
        pad = sb("pad", [1, 64])
        pad_a = sb("pad_a", [P, 1])
        pad_p = sb("pad_p", [1, 128])
        turn_of = {pad.name: 0, pad_p.name: 0}

        def spare(scrap):
            turn_of[scrap.name] = (turn_of[scrap.name] + 1) % scrap.shape[1]
            return scrap[:, turn_of[scrap.name]:turn_of[scrap.name] + 1]

        def reg(at, size):
            return region[:, at:at + size]

        zbuf = [reg(R_Z + j * Z_WIDE, Z_WIDE) for j in range(2)]
        scores_sb = [reg(R_SC + j * 2 * F, 2 * F) for j in range(2)]
        probsT = [reg(R_PT + j * DIL_FREE, DIL_FREE) for j in range(2)]
        qkv = [[reg(R_QKV + (3 * g + x) * F, F) for x in range(3)] for g in range(3)]
        raw = reg(R_RAW, 3 * PAIRS * F).rearrange("p (g a f) -> p g a f", g=3, a=PAIRS)
        obT = raw[:, 2, :, :]
        o_square, o_root = reg(R_RAW, F), reg(R_RAW + F, F)
        rows = region[0:HEADS, R_ROWS:R_ROWS + 6 * F].rearrange("p (k g f) -> p k g f", k=2, g=3)
        least = region[0:HEADS, R_PART:R_PART + F]
        total = region[0:HEADS, R_PART + F:R_PART + 2 * F]
        addend = [reg(R_PART + (2 + x) * F, F) for x in range(2)]
        mod = region[0:SEQS, R_MOD:R_MOD + 6 * D]
        gate_diag = [reg(R_DIAG + n * F, F).rearrange("p (c k) -> p c k", c=F // P) for n in range(4)]
        onehot = region[0:BUCKETS, R_ONEHOT:R_ONEHOT + 2 * F + SUB]
        mask = region[0:BIAS_ROWS, R_MASK:R_MASK + 2 * F + SUB]
        root = reg(R_RT, F)
        square = [reg(R_SQ + j * F, F) for j in range(2)]
        gate_sb = [reg(R_GATE + j * F, F) for j in range(4)]
        merged = reg(R_MERGED, C * F).rearrange("p (c f) -> p c f", c=C)
        x1T = reg(R_X1T, C * F).rearrange("p (c f) -> p c f", c=C)
        xr = [reg(R_XR + j * F, F) for j in range(2)]
        stage = [reg(R_STAGE + j * D, D) for j in range(2)]
        at = R_ROUTE

        def route(size, dt=F32):
            nonlocal at
            at += size
            assert at <= R_END
            r = region[:, at - size:at]
            return r if dt == F32 else r.bitcast(dt)

        TK = NT * K16
        qhalf = [route(F) for _ in range(2)]
        topv = [route(TK).rearrange("p (t k) -> p t k", k=K16) for _ in range(2)]
        topi = [route(TK, U32).rearrange("p (t k) -> p t k", k=K16) for _ in range(2)]
        topf = [route(TK) for _ in range(2)]
        rest = route(F).rearrange("p (t k) -> p t k", k=P)
        cand = route(NT * 256).rearrange("p (t k) -> p t k", k=256)
        cand2 = route(NT * 256).rearrange("p (t k) -> p t k", k=256)
        candv = route(TK).rearrange("p (t k) -> p t k", k=K16)
        candi = route(TK, U32).rearrange("p (t k) -> p t k", k=K16)
        parti = [route(TK, U32) for _ in range(2)]
        partf = [route(TK) for _ in range(2)]
        hot = cand.rearrange("p t k -> p (t k)")
        hot2 = cand2.rearrange("p t k -> p (t k)")
        keyno = [route(TK) for _ in range(2)]
        expert_f = route(TK)
        gap = route(TK)
        gexp = route(TK)
        gsum = route(NT)
        grec = route(NT)

        class Bank:
            def __init__(self, name):
                self.t = es.enter_context(nc.psum_tensor(name, [P, F], F32))
                self.filled, self.emptied = sem(name + "_filled"), sem(name + "_emptied")

            def __getitem__(self, i):
                return self.t[i]

        PA, XA = Bank("bank_pa"), Bank("bank_xa")
        PV, XV = Bank("bank_pv"), Bank("bank_xv")
        S = [Bank("bank_s0"), Bank("bank_s1")]
        O, G = Bank("bank_o"), Bank("bank_g")
        BANKS = [PA, XA, PV, XV, *S, O, G]

        consts_in = sem("consts_in")
        consts_set = sem("consts_set")
        silu_done = sem("silu_done")
        lam_exp = sem("lam_exp")
        mod_ready = sem("mod_ready")
        rows_ready = sem("rows_ready")
        rows_out = sem("rows_out")
        diag_ready = sem("diag_ready")
        gate2_out = sem("gate2_out")
        slab_in = [sem(f"slab_in{j}") for j in range(2)]
        slab_begun = sem("slab_begun")
        x_in = sem("x_in")
        z_in = [sem(f"z_in{j}") for j in range(2)]
        z_read = [sem(f"z_read{j}") for j in range(2)]
        step = sem("dve_step")
        squared = sem("squared")
        square_read = sem("square_read")
        h_ready = sem("h_ready")
        maxed = sem("maxed")
        exped = sem("exped")
        mixed = sem("mixed")
        dil_exped = sem("dil_exped")
        stats_ready = sem("stats_ready")
        gaps_ready = sem("gaps_ready")
        gaps_exped = sem("gaps_exped")
        factors_ready = sem("factors_ready")
        ob_ready = sem("ob_ready")
        o_squared = sem("o_squared")
        oa_ready = sem("oa_ready")
        gated = sem("gated")
        xr_in = [sem(f"xr_in{j}") for j in range(2)]
        x1_ready = sem("x1_ready")
        staged_a = sem("staged_a")
        staged_v = sem("staged_v")
        stage_out = [sem(f"stage_out{j}") for j in range(2)]
        gap_ready = sem("gap_ready")
        gap_exped = sem("gap_exped")
        record_ready = sem("record_ready")
        record_out = [sem(f"record_out{j}") for j in range(2)]
        tile_in = [sem(f"tile_in{j}") for j in range(2)]
        now_u_set = sem("now_u_set")
        now_v_set = sem("now_v_set")
        u_in = [sem(f"u_in{k}") for k in range(GS)]
        v_in = [sem(f"v_in{k}") for k in range(GS)]
        u_read = [sem(f"u_read{k}") for k in range(GS)]
        v_read_pe = [sem(f"v_read_pe{k}") for k in range(GS)]
        v_read_dve = [sem(f"v_read_dve{k}") for k in range(GS)]
        gelu_done = sem("gelu_done")
        weighed = sem("weighed")
        vdiag_ready = sem("vdiag_ready")
        final_in = sem("final_in")
        fsum_ready = sem("fsum_ready")
        froot_ready = sem("froot_ready")
        y_ready = sem("y_ready")
        y_out = sem("y_out")

        Z_PER_SEQ = 16 * (HEADS // 2) * (1 + 2)

        block = es.enter_context(nc.Block())

        @block.sync
        def _(sp):
            t = {"slab": Tally(), "xr": Tally(), "z0": Tally(), "z1": Tally()}
            sp.dma_start(hT[:, :, :], ins["x_t"][0]).then_inc(x_in, 16)
            for dst, name in ((cvec[:, :, :], "c_t"), (gmix[:, :], "g_mix"), (gffn[:, :], "g_ffn"),
                              (gsub[:, :], "g_sub"), (lamv[:, :, :], "lambdas"), (relb[:, :], "rel_bias"),
                              (ident[:, :], "ident"), (flip[:, :], "flip"),
                              (spread[:, :], "spread"), (iota16[:, :], "iota16"),
                              (b_ada[:, :], "b_ada"), (onehot, "onehot"), (mask, "mask"), (gfin[:, :], "g_final")):
                sp.dma_start(dst, ins[name]).then_inc(consts_in, 16)

            def slab(name, index, j, width):
                sp.wait_ge(slab_begun, t["slab"].n)
                sp.dma_start(w[:, j, 0:width], ins[name][ds(index, 1), :, :].rearrange("a p n -> (a p) n"))\
                    .then_inc(slab_in[j], 16)
                t["slab"].up()

            def ada_slab(index, j):
                sp.dma_start(w[:, j, 0:C * WADA_COLS], ins["w_ada"][ds(index, 1), :, :].rearrange("a p n -> (a p) n"))\
                    .then_inc(slab_in[j], 16)

            for j in range(2):
                ada_slab(j, j)
            with sp.Fori(0, WADA_SLABS // 2 - 1) as i:
                for j, bank, bias_uses in ((0, PV, 1), (1, XV, 2)):
                    sp.wait_ge(bank.filled, i + (bias_uses + 1))
                    ada_slab(2 * i + (2 + j), j)
            t["slab"].up(WADA_SLABS)

            sp.wait_ge(rows_ready, 1)
            sp.dma_start(bias_d, oaT[0:BIAS_ROWS, 0:2, :].rearrange("p a f -> p (a f)")).then_inc(rows_out, 16)
            sp.dma_start(bias_sub_d, oaT[0:BIAS_ROWS, 6, 0:SUB]).then_inc(rows_out, 16)
            sp.wait_ge(rows_out, 32)

            def z_load(j, table, start, width, at, rows=1, apart=0):
                src = bass.AP(tensor=table.tensor, offset=start - (P - 1), ap=[[1, P], [apart, rows], [1, width]])
                sp.dma_start(zbuf[j][:, at:at + rows * width].rearrange("p (a n) -> p a n", a=rows), src)\
                    .then_inc(z_in[j], 16)

            for s in range(SEQS):
                with turns(sp, HEADS // 2, t, {"slab": 2, "z0": 1, "z1": 1}) as i:
                    for j in range(2):
                        sp.wait_ge(z_read[j], t[f"z{j}"].n)
                        t[f"z{j}"].up()
                        z_load(j, bias_d, (2 * i + j) * 2 * F + (F - 384), Z_WIDE, 0)
                        slab("w_heads", 2 * i + j, j, C * 3 * P)
                with turns(sp, PAIRS // 2, t, {"slab": 6, "z0": 2, "z1": 2}) as i:
                    for b in range(2):
                        slab("w_heads", HEADS + 6 * i + 3 * b, 3 * b % 2, C * 3 * P)
                        for j in range(2):
                            sp.wait_ge(z_read[j], t[f"z{j}"].n)
                            t[f"z{j}"].up()
                            head = 2 * b + j + i * 4
                            z_load(j, bias_sub_d, (head + 2 * HEADS) * SUB + P, P, 0, 2, HEADS * SUB)
                            z_load(j, bias_d, (head + HEADS) * 2 * F + (F - P), Z_BAND, 2 * P)
                        for g in range(1, 3):
                            slab("w_heads", HEADS + 6 * i + 3 * b + g, (3 * b + g) % 2, C * 3 * P)
                with turns(sp, C // 2, t, {"slab": 2}) as i:
                    for j in range(2):
                        slab("w_merge", 2 * i + j, j, 28 * P)
                sp.wait_ge(gated, C * (s + 1))
                with turns(sp, C // 2, t, {"slab": 2, "xr": 2}) as i:
                    for j in range(2):
                        slab("w_out", 2 * i + j, j, C * P)
                        sp.wait_ge(x1_ready, t["xr"].n - j)
                        sp.dma_start(xr[j], ins["x_t"][s, :, ds(2 * i + j, 1), :].rearrange("p a f -> p (a f)"))\
                            .then_inc(xr_in[j], 16)
                        t["xr"].up()
                if s + 1 < SEQS:
                    sp.dma_start(oaT[:, :, :], ins["x_t"][s + 1]).then_inc(x_in, 16)
                for tile in range(NT):
                    for which, dst in ((0, x1_d), (1, h2_d)):
                        n = 2 * (NT * s + tile) + which + 1
                        sp.wait_ge(staged_a, n)
                        sp.wait_ge(staged_v, n)
                        sp.dma_start(dst[NT * s + tile], stage[which]).then_inc(stage_out[which], 16)

                def query_slabs(head):
                    for j in range(2):
                        slab("w_query", 2 * head + j, j, (C + 1) * P)

                def store_record(head, b):
                    sp.wait_ge(record_ready, s * HEADS + head + 1)
                    for dst, src in ((experts_d, chosen), (shares_d, share)):
                        sp.dma_start(
                            dst[s * NT:(s + 1) * NT, :, ds(head * K16, K16)].rearrange("t p k -> p t k"),
                            src[:, b, :].rearrange("p (t k) -> p t k", k=K16)).then_inc(record_out[b], 16)

                query_slabs(0)
                with turns(sp, HEADS // 2 - 1, t, {"slab": 4}) as i:
                    for b in range(2):
                        query_slabs(2 * i + b + 1)
                        store_record(2 * i + b, b)
                query_slabs(HEADS - 1)
                store_record(HEADS - 2, 0)
                store_record(HEADS - 1, 1)

        @block.gpsimd
        def _(pool):
            def fence():
                pool.tensor_tensor(spare(pad_p), zeros[0:1, 0:1], zeros[0:1, 0:1], ALU.add)

            pool.memset(ones[:, :], 1.0)
            pool.memset(zeros[:, :], 0.0)
            pool.memset(eps[:, :], EPS).then_inc(consts_set, 1)
            pool.wait_ge(consts_set, 1)
            for s in range(SEQS):
                for j in range(2):
                    pool.wait_ge(stage_out[j], 16 * NT * (s + 1))
                    pool.wait_ge(record_out[j], 16 * HEADS * (s + 1))
                with pool.Fori(0, NT // 2) as i:
                    for b in range(2):
                        tile = NT * s + 2 * i + b
                        for dst, src in ((experts[:, b, :], experts_d), (shares[:, b, :], shares_d),
                                         (h2_tile[:, b, :], h2_d)):
                            pool.dma_start(dst, src[ds(tile, 1), :, :].rearrange("a p n -> (a p) n"))\
                                .then_inc(tile_in[b], 16)
                        pool.wait_ge(tile_in[b], (NT // 2 * s + i + 1) * 48)
                        fence()

                        def gather_u(group, h):
                            n = tile * GPT + group
                            pool.tensor_copy(now_u[:, h, :], experts[:, b, ds(group * GS, GS)])\
                                .then_inc(now_u_set, 1)
                            pool.wait_ge(now_u_set, n + 1)
                            for k in range(GS):
                                pool.wait_ge(u_read[k], n)
                                fence()
                                pool.indirect_dma_start(
                                    out=urows[:, k, :], out_offset=None, in_=ins["expert_u"],
                                    in_offset=bass.IndirectOffsetOnAxis(ap=now_u[:, h, k:k + 1], axis=0))\
                                    .then_inc(u_in[k], 16)

                        def gather_v(group, h):
                            n = tile * GPT + group
                            pool.tensor_copy(now_v[:, h, :], experts[:, b, ds(group * GS, GS)])\
                                .then_inc(now_v_set, 1)
                            pool.wait_ge(now_v_set, n + 1)
                            for k in range(GS):
                                pool.wait_ge(v_read_pe[k], n)
                                pool.wait_ge(v_read_dve[k], n)
                                fence()
                                pool.indirect_dma_start(
                                    out=vrows[:, k, :], out_offset=None, in_=ins["expert_v"],
                                    in_offset=bass.IndirectOffsetOnAxis(ap=now_v[:, h, k:k + 1], axis=0))\
                                    .then_inc(v_in[k], 16)

                        gather_u(0, 0)
                        with pool.Fori(0, GPT // 2 - 1) as g:
                            for h in range(2):
                                gather_u(2 * g + (h + 1), 1 - h)
                                gather_v(2 * g + h, h)
                        gather_u(GPT - 1, 1)
                        gather_v(GPT - 2, 0)
                        gather_v(GPT - 1, 1)
                        pool.wait_ge(y_out, tile * 16)
                        fence()
                        pool.dma_start(x1_tile[:, :], x1_d[ds(tile, 1), :, :].rearrange("a p n -> (a p) n"))\
                            .then_inc(final_in, 16)
                        pool.dma_start(gate2[:, :], gate2_d[s]).then_inc(final_in, 16)

        @block.tensor
        def _(pe):
            used = {b: Tally() for b in BANKS}
            t = {**used, "slab": Tally(), "mix": Tally(), "exp": Tally(), "osq": Tally()}
            slabs = t["slab"]

            def product(bank, j, lhsT, rhs, n, out=None, first=False, last=True):
                out = bank[:, :] if out is None else out
                for c in range(n):
                    mm = pe.matmul(out, lhsT(c), rhs(c), start=(c == 0), stop=(c == n - 1))
                    if first and c == 0:
                        mm.then_inc(slab_begun, 1)
                if last:
                    mm.then_inc(bank.filled, 1)
                    used[bank].up()

            def gather_begin(tile, b, turn):
                pe.wait_ge(G.emptied, tile)
                pe.matmul(G[:, :], zeros[:, :], gfin[:, 0:F], start=True, stop=False, skip_group_check=True)

            def gather_front(n, group, p, b, last):
                pass

            def gather_back(n, group, b):
                for k in range(GS):
                    pe.wait_ge(vdiag_ready, n * GS + k + 1)
                    pe.wait_ge(v_in[k], (n + 1) * 16)
                    pe.matmul(G[:, :], vdiag[:, k, :], vrows[:, k, 0:F], start=False, stop=False,
                              skip_group_check=True).then_inc(v_read_pe[k], 1)

            def gather_end(tile, s, row):
                pe.matmul(G[:, :], zeros[:, :], gfin[:, 0:F], start=False, stop=True, skip_group_check=True)\
                    .then_inc(G.filled, 1)

            gather = (gather_begin, gather_front, gather_back, gather_end)

            def squares_sum(s, which):
                pe.wait_ge(PA.emptied, used[PA].n)
                for c in range(C):
                    pe.wait_ge(squared, (2 * s + which) * C + c + 1)
                    pe.matmul(PA[:, :], ones[:, :], square[c % 2], start=(c == 0), stop=(c == C - 1))\
                        .then_inc(square_read if c < C - 1 else PA.filled, 1)
                used[PA].up()

            def tokens(g, tile, c):
                if g == 0:
                    return hT[:, c, tile * P:(tile + 1) * P]
                return hT[:, c, :].rearrange("p (i r) -> p r i", r=STRIDE)[:, tile, :]

            def attend(s, hooks):
                nonlocal slab_base
                pe.wait_ge(h_ready, 2 * C * s + C)

                hook = Hooks(hooks, s - 1)
                hook.begin(0)
                base = slab_base // 2

                def project_part(x, turn, j, g=0):
                    bank = (PA, PV, PA)[x]
                    if x == 0:
                        pe.wait_ge(slab_in[j], 16 * turn)
                    pe.wait_ge(bank.emptied, used[bank].n)
                    if x < 2:
                        product(bank, j, lambda c: w[:, j, (3 * c + x) * P:(3 * c + x + 1) * P],
                                lambda c: hT[:, c, :], C, first=(x == 0))
                        return
                    for tile in range(NT):
                        product(bank, j, lambda c: tokens(g, tile, c),
                                lambda c: w[:, j, (3 * c + 2) * P:(3 * c + 3) * P], C,
                                out=bank[:, tile * P:(tile + 1) * P], last=(tile == NT - 1))
                    slabs.up()

                def scores(tile, j):
                    q, k, v = qkv[j]
                    for x in range(2):
                        pe.wait_ge(S[x].emptied, used[S[x]].n)
                        rows = slice(x * DH, (x + 1) * DH)
                        pe.matmul(S[x][:, :], q[rows, tile * P:(tile + 1) * P], k[rows, :],
                                  start=True, stop=True).then_inc(S[x].filled, 1)
                        used[S[x]].up()

                def first_scores(j):
                    pe.wait_ge(PA.emptied, used[PA].n)
                    pe.wait_ge(PV.emptied, used[PV].n)
                    scores(0, j)
                    scores(1, j)

                for x in range(3):
                    project_part(x, base + 1, 0)
                first_scores(0)

                def head(h, j, turn, first, last):
                    v = qkv[j][2]

                    def transposes(tile):
                        bank = (XA, XV)[tile % 2]
                        pe.wait_ge(bank.emptied, used[bank].n)
                        pe.wait_ge(mixed, t["mix"].n + 1)
                        t["mix"].up()
                        for kt in range(NT):
                            mm = pe.transpose(bank[:, kt * P:(kt + 1) * P],
                                              scores_sb[tile % 2][:, kt * P:(kt + 1) * P], flip[:, :])
                        mm.then_inc(bank.filled, 1)
                        used[bank].up()

                    def weigh(tile):
                        bank = (XA, XV)[tile % 2]
                        pe.wait_ge(bank.emptied, evac[tile])
                        if tile == 0:
                            pe.wait_ge(O.emptied, used[O].n)
                        for kt in range(NT):
                            mm = pe.matmul(O[:, tile * P:(tile + 1) * P], v[:, kt * P:(kt + 1) * P],
                                           probsT[tile % 2][:, kt * P:(kt + 1) * P],
                                           start=(kt == 0), stop=(kt == NT - 1))
                        if tile == NT - 1:
                            mm.then_inc(O.filled, 1)
                            used[O].up()

                    evac = {}
                    if not first:
                        norm_sum()
                    for tile in range(NT):
                        if tile < 3:
                            project_part(tile, turn + base, 1 - j)
                        if tile:
                            weigh(tile - 1)
                        transposes(tile)
                        evac[tile] = used[(XA, XV)[tile % 2]].n
                        if tile + 2 < NT:
                            scores(tile + 2, j)
                        if tile == NT - 1:
                            weigh(tile)
                        hook.back(h * NT, tile, 0)
                    if not last:
                        first_scores(1 - j)

                def norm_sum():
                    pe.wait_ge(o_squared, t["osq"].n + 1)
                    t["osq"].up()
                    pe.wait_ge(PV.emptied, used[PV].n)
                    pe.matmul(PV[:, :], ones[:, :], o_square, start=True, stop=True).then_inc(PV.filled, 1)
                    used[PV].up()

                heads_of_attention(pe, t, {"slab": 2, PA: 4, PV: 4, XA: 4, XV: 4, S[0]: 8, S[1]: 8, O: 2,
                                           "mix": 8, "osq": 2}, head)
                norm_sum()
                slab_base += HEADS
                hook.end(0)

                hook.begin(1)
                base = slab_base // 2

                def step_scores(u, buf, g):
                    bank, (q, k, v) = S[u % 2], qkv[buf]
                    pe.wait_ge(bank.emptied, used[bank].n)
                    if g == 0:
                        j, tile = divmod(u, NT)
                        head, kts = slice(j * DH, (j + 1) * DH), key_tiles(tile)
                        mm = pe.matmul(bank[:, 0:len(kts) * P], q[head, tile * P:(tile + 1) * P],
                                       k[head, kts[0] * P:(kts[-1] + 1) * P], start=True, stop=True)
                    else:
                        head = slice(u * DH, (u + 1) * DH)
                        for tile in range(NT):
                            mine = slice(tile * P, (tile + 1) * P)
                            mm = pe.matmul(bank[:, mine], q[head, mine], k[head, mine], start=True, stop=True)
                    mm.then_inc(bank.filled, 1)
                    used[bank].up()

                def step_begin(buf, g):
                    pe.wait_ge(PA.emptied, used[PA].n)
                    pe.wait_ge(PV.emptied, used[PV].n)
                    step_scores(0, buf, g)
                    step_scores(1, buf, g)

                def step_of_pair(at, g, last):
                    units, buf = UNITS[g], at % 2
                    v = qkv[buf][2]

                    def transposes(u):
                        bank = (XA, XV)[u % 2]
                        pe.wait_ge(bank.emptied, used[bank].n)
                        pe.wait_ge(dil_exped, t["exp"].n + 1)
                        t["exp"].up()
                        for kt in range(len(key_tiles(u % NT)) if g == 0 else NT):
                            mm = pe.transpose(bank[:, kt * P:(kt + 1) * P],
                                              scores_sb[u % 2][:, kt * P:(kt + 1) * P], flip[:, :])
                        mm.then_inc(bank.filled, 1)
                        used[bank].up()

                    def weigh(u):
                        pe.wait_ge((XA, XV)[u % 2].emptied, evac[u])
                        pe.wait_ge(O.emptied, used[O].n)
                        kts = key_tiles(u % NT) if g == 0 else range(NT)
                        for n, kt in enumerate(kts):
                            mm = pe.matmul(O[:, 0:P] if g == 0 else O[:, n * P:(n + 1) * P],
                                           v[:, kt * P:(kt + 1) * P], probsT[u % 2][:, n * P:(n + 1) * P],
                                           start=(g > 0 or n == 0), stop=(g > 0 or n == len(kts) - 1))
                        mm.then_inc(O.filled, 1)
                        used[O].up()

                    parts = {0: 0, 2: 1, 4: 2} if g == 0 else {0: 0, 1: 1}

                    def part(x):
                        if not last:
                            project_part(x, i * 3 + (base + (at + 1) // 2 + 1), 1 - buf, (g + 1) % 3)

                    evac = {}
                    for u in range(units):
                        if u in parts:
                            part(parts[u])
                        if u:
                            weigh(u - 1)
                        transposes(u)
                        evac[u] = used[(XA, XV)[u % 2]].n
                        if u + 2 < units:
                            step_scores(u + 2, buf, g)
                        if u == units - 1:
                            if g:
                                part(2)
                            weigh(u)
                        for n in hooks_of_step(2 * i + at // 3, g, u):
                            hook.back_on(n, 1)
                    if not last:
                        step_begin(1 - buf, (g + 1) % 3)

                step_begin(0, 0)
                for i in range(PAIRS // 2):
                    for at, b, g, last in steps_of_pairs(i):
                        step_of_pair(at, g, last)
                slab_base += 3 * PAIRS

                pe.wait_ge(stats_ready, s + 1)
                for kind in range(2):
                    for x in range(3):
                        bank = (PV, XV)[(3 * kind + x) % 2]
                        pe.wait_ge(bank.emptied, used[bank].n)
                        for tile in range(NT):
                            mm = pe.transpose(bank[0:HEADS, tile * P:(tile + 1) * P],
                                              stat[:, x, kind, tile, :], flip[:, :])
                        mm.then_inc(bank.filled, 1)
                        used[bank].up()
                hook.back(0, DIL_HOOKS, 2)
                pe.wait_ge(factors_ready, s + 1)
                for pair in range(PAIRS):
                    for x, bank in enumerate((PV, XV, S[0])):
                        pe.wait_ge(bank.emptied, used[bank].n)
                        pe.matmul(bank[:, :], spread[:, pair * P:(pair + 1) * P], rows[:, 0, x, :],
                                  start=True, stop=True).then_inc(bank.filled, 1)
                        used[bank].up()
                    if pair:
                        hook.back(0, DIL_HOOKS + pair, 2)

                base = slab_base // 2
                pe.wait_ge(oa_ready, HEADS * (s + 1))
                pe.wait_ge(ob_ready, s + 1)
                for i in rounds(bool(hooks), pe, C // 2, t, {"slab": 2, PA: 2, XA: 2, PV: 2, XV: 2}):
                    for j in range(2):
                        pe.wait_ge(slab_in[j], 16 * (base + i + 1))
                        for bank, first, n, rhs in ((PA, 0, C, hT), (XA, C, C, hT), (PV, 2 * C, C, oaT),
                                                    (XV, 3 * C, PAIRS, obT)):
                            pe.wait_ge(bank.emptied, used[bank].n)
                            product(bank, j, lambda c: w[:, j, (first + c) * P:(first + c + 1) * P],
                                    lambda c: rhs[:, c, :], n, first=(first == 0))
                            if bank in (XA, XV):
                                hook.back(i * 4, DIL_HOOKS + 4 + 2 * j + (XA, XV).index(bank), 2)
                        slabs.up()
                slab_base += C

                hook.end(2)
                hook.begin(3)

                base = slab_base // 2
                pe.wait_ge(gated, C * (s + 1))
                with turns(pe, C // 2, t, {"slab": 2, PV: 2}) as i:
                    for j in range(2):
                        pe.wait_ge(slab_in[j], 16 * (base + i + 1))
                        pe.wait_ge(PV.emptied, used[PV].n)
                        product(PV, j, lambda c: w[:, j, c * P:(c + 1) * P], lambda c: merged[:, c, :], C,
                                first=True)
                        slabs.up()
                        hook.back(i * 2, j, 3)
                slab_base += C

                squares_sum(s, 1)
                for k in range(C, C + 4):
                    hook.back(0, k, 3)
                pe.wait_ge(h_ready, 2 * C * s + 2 * C)
                for tile in range(NT):
                    for src in (x1T, hT):
                        for bank, first in ((XA, 0), (XV, NT)):
                            pe.wait_ge(bank.emptied, used[bank].n)
                            for c in range(4):
                                mm = pe.transpose(bank[:, c * P:(c + 1) * P],
                                                  src[:, first + c, tile * P:(tile + 1) * P], ident[:, :])
                            mm.then_inc(bank.filled, 1)
                            used[bank].up()
                    hook.back(0, C + 4 + tile, 3)
                if s + 1 < SEQS:
                    squares_sum(s + 1, 0)

                base = slab_base // 2
                for i in rounds(bool(hooks), pe, HEADS // 2, t, {"slab": 4, PA: 2, XA: 2, S[0]: 2, S[1]: 2}):
                    for b in range(2):
                        for j, bank in ((0, PA), (1, XA)):
                            pe.wait_ge(slab_in[j], 16 * (base + 2 * i + b + 1))
                            pe.wait_ge(bank.emptied, used[bank].n)
                            product(bank, j, lambda c: w[:, j, c * P:(c + 1) * P], lambda c: hT[:, c, :], C,
                                    first=(j == 0))
                            slabs.up()
                            hook.back(i * 4, 16 + 2 * b + j, 3)
                        for j, bank in ((0, PA), (1, XA)):
                            pe.wait_ge(bank.emptied, used[bank].n)
                            pe.wait_ge(S[j].emptied, used[S[j]].n)
                            for tile in range(NT):
                                mm = pe.matmul(S[j][:, tile * P:(tile + 1) * P],
                                               qhalf[j][:, tile * P:(tile + 1) * P],
                                               w[:, j, C * P:(C + 1) * P], start=True, stop=True)
                                if (j, tile) == (1, 0):
                                    mm.then_inc(slab_begun, 1)
                            mm.then_inc(S[j].filled, 1)
                            used[S[j]].up()
                slab_base += 2 * HEADS
                hook.end(3)

            pe.wait_ge(consts_in, 14 * 16)
            pe.wait_ge(consts_set, 1)
            for bank, cols in ((XV, slice(0, F)), (PV, slice(F, 2 * F)), (XV, slice(2 * F, 2 * F + SUB))):
                pe.wait_ge(bank.emptied, used[bank].n)
                pe.matmul(bank[0:BIAS_ROWS, 0:cols.stop - cols.start], relb[:, :], onehot[:, cols],
                          start=True, stop=True).then_inc(bank.filled, 1)
                used[bank].up()
            pe.wait_ge(silu_done, 1)
            squares_sum(0, 0)
            with turns(pe, WADA_SLABS // 2, t, {"slab": 2, PV: 1, XV: 1}) as i:
                for j, bank in ((0, PV), (1, XV)):
                    pe.wait_ge(slab_in[j], 16 * (i + 1))
                    pe.wait_ge(bank.emptied, used[bank].n)
                    product(bank, j, lambda c: cvec[:, c, :],
                            lambda c: w[:, j, c * WADA_COLS:(c + 1) * WADA_COLS], C,
                            out=bank[0:SEQS, 0:WADA_COLS], first=True)
                    slabs.up()
            for bank in (PV, XV):
                pe.wait_ge(bank.emptied, used[bank].n)
            for c in range(6 * C):
                mm = pe.transpose(PV[:, SEQS * c:SEQS * (c + 1)], mod[:, c * P:(c + 1) * P],
                                  ident[0:SEQS, 0:SEQS])
            mm.then_inc(PV.filled, 1)
            used[PV].up()
            for n, bank in enumerate((PA, XA, O, PA)):
                pe.wait_ge(diag_ready, n + 1)
                pe.wait_ge(bank.emptied, used[bank].n)
                for c in range(F // P):
                    mm = pe.matmul(bank[:, c * P:(c + 1) * P], ones[:, :], gate_diag[n][:, c, :],
                                   start=True, stop=True)
                mm.then_inc(bank.filled, 1)
                used[bank].up()

            slab_base = WADA_SLABS
            attend(0, None)
            attend(1, gather)
            gather_alone(pe, gather, t, {})

        @block.scalar
        def _(act):
            used = {b: Tally() for b in (PA, PV, XA, O)}
            t = {**used, "exp": Tally(), "gate": Tally(), "rec": Tally()}

            def gather_begin(tile, b, turn):
                pass

            def gather_front(n, group, p, b, last):
                act.wait_ge(u_read[GS - 1], n + 1)
                act.activation(gelus[:, :], dots[:, p, :], ACT.Gelu).then_inc(gelu_done, 1)

            def gather_back(n, group, b):
                act.wait_ge(weighed, n + 1)
                for k in range(GS):
                    act.wait_ge(v_read_pe[k], n)
                    act.activation(vdiag[:, k, :], ident[:, :], ACT.Copy, scale=weights[:, k:k + 1])\
                        .then_inc(vdiag_ready, 1)

            def gather_end(tile, s, row):
                act.wait_ge(fsum_ready, tile + 1)
                act.activation(fstat[:, 1:2], fstat[:, 0:1], ACT.Sqrt, bias=eps[:, 0:1], scale=1.0 / D)\
                    .then_inc(froot_ready, 1)
                act.wait_ge(y_ready, tile + 1)
                act.dma_start(y[s][ds(row * P, P), :], x1_tile[:, :])\
                    .then_inc(y_out, 16)

            gather = (gather_begin, gather_front, gather_back, gather_end)

            def norm_root(s, which, src):
                for c in range(C):
                    if c >= 2:
                        act.wait_ge(square_read, (2 * s + which) * (C - 1) + c - 1)
                    act.activation(square[c % 2], src[:, c, :], ACT.Square).then_inc(squared, 1)
                act.wait_ge(PA.filled, used[PA].n + 1)
                act.activation(root, PA[:, :], ACT.Sqrt, bias=eps[:, 0:1], scale=1.0 / D)\
                    .then_inc(PA.emptied, 1)
                used[PA].up()

            def empty(bank, dst, src=None, scale=1.0, func=ACT.Copy):
                act.wait_ge(bank.filled, used[bank].n + 1)
                act.activation(dst, bank[:, :] if src is None else src, func, scale=scale)\
                    .then_inc(bank.emptied, 1)
                used[bank].up()

            def by_tile(bank, g=0):
                if g == 0:
                    return bank[:, :].rearrange("p (t q) -> p t q", q=P)
                return bank[:, :].rearrange("p (i r) -> p r i", r=STRIDE)

            def backwards(dst):
                return bass.AP(tensor=dst.tensor, offset=dst.offset + P - 1, ap=[dst.ap[0], [P, NT], [-1, P]])

            def exps(u, n):
                act.wait_ge(maxed, t["exp"].n + 1)
                t["exp"].up()
                for x in range(len(n)):
                    e = act.activation(scores_sb[u % 2][:, x * F:x * F + n[x]],
                                       scores_sb[u % 2][:, x * F:x * F + n[x]], ACT.Exp,
                                       bias=nm[:, u % 2, x:x + 1], accum_out=den[:, u % 2, x:x + 1])
                e.then_inc(exped, 1)

            def attend(s, hooks):
                hook = Hooks(hooks, s - 1)
                hook.begin(0)
                empty(PA, backwards(qkv[0][0]), src=by_tile(PA), scale=DH ** -0.5)
                empty(PA, qkv[0][2])

                def head(h, j, turn, first, last):
                    if not first:
                        act.wait_ge(O.filled, used[O].n + 1)
                        used[O].up()
                        act.activation(o_square, O[:, :], ACT.Square).then_inc(o_squared, 1)
                    exps(0, (F, F))
                    for tile in range(NT):
                        if tile + 1 < NT:
                            exps(tile + 1, (F, F))
                        if tile == 0 and not first:
                            norm_root_of_head()
                        hook.front(h * NT, tile, 0)
                        if tile == 0:
                            empty(PA, backwards(qkv[1 - j][0]), src=by_tile(PA), scale=DH ** -0.5)
                        if tile % 2 == 0:
                            empty(XA, probsT[0][:, 0:F])
                        if tile == 1:
                            used[PV].up()
                        if tile == 3:
                            empty(PA, qkv[1 - j][2])
                        hook.back(h * NT, tile, 0)

                def norm_root_of_head():
                    act.wait_ge(PV.filled, used[PV].n + 1)
                    act.activation(o_root, PV[:, :], ACT.Sqrt, bias=eps[:, 0:1], scale=1.0 / P)\
                        .then_inc(PV.emptied, 1)
                    used[PV].up()

                used[PV].up()
                heads_of_attention(act, t, {PA: 4, PV: 4, XA: 4, O: 2, "exp": 8}, head)
                act.wait_ge(O.filled, used[O].n + 1)
                used[O].up()
                act.activation(o_square, O[:, :], ACT.Square).then_inc(o_squared, 1)
                norm_root_of_head()
                hook.end(0)

                hook.begin(1)

                def step_exps(u, g):
                    act.wait_ge(maxed, t["exp"].n + 1)
                    t["exp"].up()
                    if g == 0:
                        j, tile = divmod(u, NT)
                        tiles = [(j, tile, 0, len(key_tiles(tile)) * P)]
                    else:
                        tiles = [(u, tile, tile * P, P) for tile in range(NT)]
                    for j, tile, col, n in tiles:
                        e = act.activation(scores_sb[u % 2][:, col:col + n], scores_sb[u % 2][:, col:col + n],
                                           ACT.Exp, bias=unit_stat[:, PLACE[g], 0, tile, j:j + 1],
                                           accum_out=unit_stat[:, PLACE[g], 1, tile, j:j + 1])
                    e.then_inc(dil_exped, 1)

                def unit_out(u, g, pair):
                    j, cols = (u // NT, slice(u % NT * P, (u % NT + 1) * P)) if g == 0 else (u, slice(0, F))
                    head = slice(j * DH, (j + 1) * DH)
                    act.wait_ge(O.filled, used[O].n + 1)
                    act.activation(raw[head, PLACE[g], pair, cols].rearrange("p a f -> p (a f)"),
                                   O[head, 0:cols.stop - cols.start], ACT.Copy).then_inc(O.emptied, 1)
                    used[O].up()

                for i in range(PAIRS // 2):
                    for at, b, g, last in steps_of_pairs(i):
                        units, following, pair = UNITS[g], (g + 1) % 3, ds(2 * i + b, 1)
                        step_exps(0, g)
                        for u in range(units):
                            ns = hooks_of_step(2 * i + b, g, u)
                            if u + 1 < units:
                                step_exps(u + 1, g)
                            for n in ns[:1]:
                                hook.front_on(n, 1)
                            if u:
                                unit_out(u - 1, g, pair)
                            if u == 0 and not last:
                                empty(PA, backwards(qkv[1 - at % 2][0]), src=by_tile(PA, following),
                                      scale=DH ** -0.5)
                            if u % 2 == 0:
                                width = len(key_tiles(u % NT)) * P if g == 0 else F
                                empty(XA, probsT[0][:, 0:width], src=XA[:, 0:width])
                            if u == (5 if g == 0 else 1) and not last:
                                empty(PA, qkv[1 - at % 2][2])
                            for n in ns:
                                if n > ns[0]:
                                    hook.front_on(n, 1)
                                hook.back_on(n, 1)
                        unit_out(units - 1, g, pair)
                used[PV].up((3 * PAIRS - 1) + (3 + PAIRS) + C + C)
                hook.front(0, DIL_HOOKS, 2)
                hook.back(0, DIL_HOOKS, 2)
                act.wait_ge(gaps_ready, s + 1)
                act.activation(rows[:, 0, :, :], rows[:, 0, :, :], ACT.Exp).then_inc(gaps_exped, 1)
                for k in range(DIL_HOOKS + 1, DIL_HOOKS + PAIRS):
                    hook.front(0, k, 2)
                    hook.back(0, k, 2)

                for i in rounds(bool(hooks), act, C // 2, t, {PA: 2, XA: 2, "gate": 2}):
                    for j in range(2):
                        hook.front(i * 4, DIL_HOOKS + 4 + 2 * j, 2)
                        hook.back(i * 4, DIL_HOOKS + 4 + 2 * j, 2)
                        act.wait_ge(gated, t["gate"].n)
                        t["gate"].up()
                        empty(PA, gate_sb[0], func=ACT.Sigmoid)
                        empty(XA, gate_sb[1], func=ACT.Sigmoid)
                        hook.front(i * 4, DIL_HOOKS + 4 + 2 * j + 1, 2)
                        hook.back(i * 4, DIL_HOOKS + 4 + 2 * j + 1, 2)
                hook.end(2)
                hook.begin(3)
                if hooks:
                    with act.Fori(0, C // 2) as i:
                        for j in range(2):
                            hook.front(i * 2, j, 3)
                            hook.back(i * 2, j, 3)

                hook.front(0, C, 3)
                hook.back(0, C, 3)
                act.wait_ge(x1_ready, C * (s + 1))
                norm_root(s, 1, x1T)
                for k in range(C + 1, C + 4):
                    hook.front(0, k, 3)
                    hook.back(0, k, 3)
                for tile in range(NT):
                    for which in range(2):
                        if NT * s + tile:
                            act.wait_ge(stage_out[which], 16 * (NT * s + tile))
                        act.wait_ge(XA.filled, used[XA].n + 1)
                        act.activation(stage[which][:, 0:F], XA[:, :], ACT.Copy).then_inc(XA.emptied, 1)
                        used[XA].up()
                        act.wait_ge(XA.emptied, used[XA].n)
                        act.activation(pad_a[:, :], eps[:, :], ACT.Copy).then_inc(staged_a, 1)
                    hook.front(0, C + 4 + tile, 3)
                    hook.back(0, C + 4 + tile, 3)
                if s + 1 < SEQS:
                    act.wait_ge(x_in, 16 * (s + 2))
                    norm_root(s + 1, 0, oaT)

                for i in rounds(bool(hooks), act, HEADS // 2, t, {PA: 2, XA: 2, "rec": 2}):
                    for b in range(2):
                        for j, bank in enumerate((PA, XA)):
                            empty(bank, qhalf[j])
                            hook.front(i * 4, 16 + 2 * b + j, 3)
                            hook.back(i * 4, 16 + 2 * b + j, 3)
                        act.wait_ge(gap_ready, t["rec"].n + 1)
                        t["rec"].up()
                        act.activation(gexp, gap, ACT.Exp).then_inc(gap_exped, 1)
                hook.end(3)

            act.wait_ge(consts_in, 14 * 16)
            act.wait_ge(consts_set, 1)
            act.activation(cvec[:, :, :], cvec[:, :, :], ACT.Silu).then_inc(silu_done, 1)
            act.wait_ge(lam_exp, 1)
            act.activation(lam[:, 2:4], lam[:, 0:2], ACT.Exp).then_inc(lam_exp, 1)
            used[PV].up(1 + WADA_SLABS // 2 + 1)
            act.wait_ge(x_in, 16)
            norm_root(0, 0, hT)
            act.wait_ge(mod_ready, 1)
            places = [(s, half) for s in range(SEQS) for half in range(2)]
            for n, (s, half) in enumerate(places):
                for c in range(F // P):
                    at = 5 * C + half * (F // P) + c
                    last = act.activation(gate_diag[n][:, c, :], ident[:, :], ACT.Copy, scale=modT[:, at, s:s + 1])
                last.then_inc(diag_ready, 1)
            for (s, half), bank in zip(places, (PA, XA, O, PA)):
                empty(bank, oaT[:, 2 + 2 * s + half, :])
                act.wait_ge(bank.emptied, used[bank].n)
                act.dma_start(gate2_d[s, :, half * F:(half + 1) * F], oaT[:, 2 + 2 * s + half, :])\
                    .then_inc(gate2_out, 16)

            attend(0, None)
            attend(1, gather)
            gather_alone(act, gather, t, {})
            act.wait_ge(y_out, 16 * SEQS * NT)

        @block.vector
        def _(dve):
            used = {b: Tally() for b in BANKS}
            t = {**used, "step": Tally(), "exp": Tally(), "dil": Tally(),
                 "x1": Tally(), "rec": Tally()}
            steps = t["step"]

            def then(ins):
                ins.then_inc(step, 1)
                steps.up()
                dve.wait_ge(step, steps.n)

            def fence():
                dve.memset(spare(pad), 0.0)

            def dot_products(n, p, b, ks=range(GS)):
                for k in ks:
                    dve.wait_ge(u_in[k], (n + 1) * 16)
                    dve.tensor_tensor_reduce(urows[:, k, :], urows[:, k, :], h2_tile[:, b, :], 1.0, 0.0,
                                             ALU.mult, ALU.add, dots[:, p, k:k + 1]).then_inc(u_read[k], 1)

            def gather_begin(tile, b, turn):
                then(dve.memset(vsum[:, :], 0.0))
                dve.wait_ge(tile_in[b], turn * 48)
                fence()
                dot_products(tile * GPT, 0, b)

            def gather_front(n, group, p, b, last):
                if not last:
                    dot_products(n + 1, 1 - p, b, range(GS // 2))
                dve.wait_ge(gelu_done, n + 1)
                dve.wait_ge(vdiag_ready, n * GS)
                dve.tensor_tensor(weights[:, :], gelus[:, :], shares[:, b, ds(group * GS, GS)], ALU.mult)\
                    .then_inc(weighed, 1)
                if not last:
                    dot_products(n + 1, 1 - p, b, range(GS // 2, GS))

            def gather_back(n, group, b):
                dve.wait_ge(weighed, n + 1)
                for k in range(GS):
                    dve.wait_ge(v_in[k], (n + 1) * 16)
                    dve.scalar_tensor_tensor(out=vsum[:, :], in0=vrows[:, k, F:D], scalar=weights[:, k:k + 1],
                                             in1=vsum[:, :], op0=ALU.mult, op1=ALU.add)\
                        .then_inc(v_read_dve[k], 1)
                    dve.wait_ge(v_read_dve[k], n + 1)

            def gather_end(tile, s, row):
                dve.wait_ge(final_in, (tile + 1) * 32)
                then(dve.tensor_tensor(vsum[:, :], vsum[:, :], gate2[:, F:D], ALU.mult))
                then(dve.tensor_tensor(x1_tile[:, F:D], x1_tile[:, F:D], vsum[:, :], ALU.add))
                dve.wait_ge(G.filled, tile + 1)
                dve.tensor_tensor(vsum[:, :], G[:, :], gate2[:, 0:F], ALU.mult).then_inc(G.emptied, 1)
                dve.wait_ge(G.emptied, tile + 1)
                then(dve.tensor_tensor(x1_tile[:, 0:F], x1_tile[:, 0:F], vsum[:, :], ALU.add))
                for half in range(2):
                    cols = slice(half * F, (half + 1) * F)
                    then(dve.tensor_tensor_reduce(vsum[:, :], x1_tile[:, cols], x1_tile[:, cols], 1.0, 0.0,
                                                  ALU.mult, ALU.add, fstat[:, 2 + half:3 + half]))
                dve.tensor_tensor(fstat[:, 0:1], fstat[:, 2:3], fstat[:, 3:4], ALU.add).then_inc(fsum_ready, 1)
                dve.wait_ge(froot_ready, tile + 1)
                then(dve.reciprocal(fstat[:, 2:3], fstat[:, 1:2]))
                dve.scalar_tensor_tensor(out=x1_tile[:, :], in0=x1_tile[:, :], scalar=fstat[:, 2:3],
                                         in1=gfin[:, :], op0=ALU.mult, op1=ALU.mult).then_inc(y_ready, 1)

            gather = (gather_begin, gather_front, gather_back, gather_end)

            def normalise(src, dst):
                used[PA].up()
                dve.wait_ge(PA.emptied, used[PA].n)
                then(dve.reciprocal(root, root))
                for c in range(C):
                    last = dve.tensor_tensor(dst[:, c, :], src[:, c, :], root, ALU.mult)
                then(last)

            def modulate(s, which, src):
                scale, shift = ((scale1, 0), (scale2, 3))[which]
                for c in range(C):
                    dve.tensor_scalar(hT[:, c, :], src[:, c, :], scale[:, s, c:c + 1],
                                      modT[:, shift * C + c, s:s + 1], ALU.mult, ALU.add).then_inc(h_ready, 1)

            def bias_max(u, parts):
                for x, (bank, col, n, z) in enumerate(parts):
                    dve.wait_ge(bank.filled, used[bank].n + 1)
                    fence()
                    dve.tensor_tensor_reduce(scores_sb[u % 2][:, col:col + n], bank[:, 0:n], z, 1.0, LOWEST,
                                             ALU.add, ALU.max, mx[:, u % 2, x:x + 1]).then_inc(bank.emptied, 1)
                    used[bank].up()
                dve.wait_ge(parts[-1][0].emptied, used[parts[-1][0]].n)

            def merge_groups(s, hook):
                dve.memset(spare(pad), 0.0).then_inc(stats_ready, 1)
                order = (1, 2, 0)
                for kind in range(2):
                    for x, g in enumerate(order):
                        bank = (PV, XV)[(3 * kind + x) % 2]
                        dve.wait_ge(bank.filled, used[bank].n + 1)
                        src, dst = bank[0:HEADS, :], rows[:, kind, x, :]
                        if g:
                            src = src.rearrange("p (r i) -> p r i", r=STRIDE)
                            dst = dst.rearrange("p (i r) -> p r i", r=STRIDE)
                        dve.tensor_copy(dst, src).then_inc(bank.emptied, 1)
                        used[bank].up()
                        dve.wait_ge(bank.emptied, used[bank].n)
                hook.front(0, DIL_HOOKS, 2)
                hook.back(0, DIL_HOOKS, 2)
                then(dve.tensor_tensor(least, rows[:, 0, 0, :], rows[:, 0, 1, :], ALU.min))
                then(dve.tensor_tensor(least, least, rows[:, 0, 2, :], ALU.min))
                dve.tensor_tensor(rows[:, 0, :, :], least.unsqueeze(1).broadcast_to([HEADS, 3, F]),
                                  rows[:, 0, :, :], ALU.subtract).then_inc(gaps_ready, 1)
                dve.wait_ge(gaps_exped, s + 1)
                then(dve.tensor_tensor(rows[:, 1, :, :], rows[:, 1, :, :], rows[:, 0, :, :], ALU.mult))
                then(dve.tensor_tensor(total, rows[:, 1, 0, :], rows[:, 1, 1, :], ALU.add))
                then(dve.tensor_tensor(total, total, rows[:, 1, 2, :], ALU.add))
                then(dve.reciprocal(total, total))
                dve.tensor_tensor(rows[:, 0, :, :], rows[:, 0, :, :],
                                  total.unsqueeze(1).broadcast_to([HEADS, 3, F]), ALU.mult)\
                    .then_inc(factors_ready, 1)
                for pair in range(PAIRS):
                    for x, (g, bank) in enumerate(zip(order, (PV, XV, S[0]))):
                        dve.wait_ge(bank.filled, used[bank].n + 1)
                        src, dst, factor = raw[:, x, pair, :], obT[:, pair, :], bank[:, :]
                        if g:
                            src = src.rearrange("p (r i) -> p i r", r=STRIDE)
                            dst = addend[x].rearrange("p (i r) -> p i r", r=STRIDE)
                            factor = factor.rearrange("p (i r) -> p i r", r=STRIDE)
                        dve.tensor_tensor(dst, factor, src, ALU.mult).then_inc(bank.emptied, 1)
                        used[bank].up()
                        dve.wait_ge(bank.emptied, used[bank].n)
                    for x in range(2):
                        last = dve.tensor_tensor(obT[:, pair, :], obT[:, pair, :], addend[x], ALU.add)
                        if (pair, x) == (PAIRS - 1, 1):
                            last.then_inc(ob_ready, 1)
                        else:
                            then(last)
                    if pair < PAIRS - 1:
                        hook.front(0, DIL_HOOKS + 1 + pair, 2)
                        hook.back(0, DIL_HOOKS + 1 + pair, 2)

            def attend(s, hooks):
                modulate(s, 0, oaT if s else hT)
                hook = Hooks(hooks, s - 1)
                hook.begin(0)

                def key_out(j, g=0):
                    dve.wait_ge(PV.filled, used[PV].n + 1)
                    if g == 0:
                        dve.tensor_copy(qkv[j][1], PV[:, :]).then_inc(PV.emptied, 1)
                    else:
                        dve.tensor_copy(qkv[j][1].rearrange("p (r i) -> p r i", r=STRIDE),
                                        PV[:, :].rearrange("p (i r) -> p r i", r=STRIDE)).then_inc(PV.emptied, 1)
                    used[PV].up()

                def unit_max(tile, j):
                    at = 384 - tile * P
                    bias_max(tile, [(S[x], x * F, F, zbuf[j][:, at:at + F]) for x in range(2)])
                    dve.tensor_scalar(nm[:, tile % 2, :], mx[:, tile % 2, 0:2], -1.0, None, ALU.mult)\
                        .then_inc(maxed, 1)

                used[PA].up(2)
                key_out(0)
                dve.wait_ge(z_in[0], 16 + s * Z_PER_SEQ)
                unit_max(0, 0)

                def head(h, j, turn, first, last):
                    def unit_mix(tile):
                        dve.wait_ge(exped, t["exp"].n + 1)
                        t["exp"].up()
                        then(dve.reciprocal(rden[:, tile % 2, :], den[:, tile % 2, :]))
                        then(dve.tensor_tensor(rden[:, tile % 2, :], rden[:, tile % 2, :], mixsign[:, :],
                                               ALU.mult))
                        p1, p2 = (scores_sb[tile % 2][:, x * F:(x + 1) * F] for x in range(2))
                        then(dve.tensor_scalar(p2, p2, rden[:, tile % 2, 1:2], None, ALU.mult))
                        dve.scalar_tensor_tensor(out=p1, in0=p1, scalar=rden[:, tile % 2, 0:1], in1=p2,
                                                 op0=ALU.mult, op1=ALU.add).then_inc(mixed, 1)

                    for tile in range(NT):
                        if tile + 1 < NT:
                            unit_max(tile + 1, j)
                        if tile == NT - 2:
                            dve.memset(spare(pad), 0.0).then_inc(z_read[j], 1)
                        unit_mix(tile)
                        if tile == 0 and not first:
                            head_out(h - 1)
                        if tile < NT - 1:
                            hook.front(h * NT, tile, 0)
                        if tile % 2 == 1:
                            dve.wait_ge(XV.filled, used[XV].n + 1)
                            dve.tensor_copy(probsT[1][:, 0:F], XV[:, :]).then_inc(XV.emptied, 1)
                            used[XV].up()
                        if tile == NT - 1:
                            hook.front(h * NT, tile, 0)
                        if tile == 1:
                            key_out(1 - j)
                        hook.back(h * NT, tile, 0)
                    used[PA].up(2)
                    if not last:
                        dve.wait_ge(z_in[1 - j], turn * 16 + s * Z_PER_SEQ)
                        unit_max(0, 1 - j)

                def head_out(h):
                    used[PV].up()
                    dve.wait_ge(PV.emptied, used[PV].n)
                    then(dve.reciprocal(o_root, o_root))
                    dve.wait_ge(O.filled, used[O].n + 1)
                    dve.scalar_tensor_tensor(
                        out=oaT[:, ds(h, 1), :].rearrange("p a f -> p (a f)"), in0=O[:, :],
                        scalar=gsub[:, 0:1], in1=o_root, op0=ALU.mult, op1=ALU.mult).then_inc(O.emptied, 1)
                    used[O].up()

                if s == 0:
                    dve.wait_ge(rows_out, 32)
                    dve.wait_ge(gate2_out, 16 * 2 * SEQS)
                heads_of_attention(dve, t, {PA: 4, PV: 4, XV: 4, S[0]: 8, S[1]: 8, O: 2, "exp": 8, "step": 26},
                                   head)
                head_out(HEADS - 1)
                dve.wait_ge(O.emptied, used[O].n)
                dve.memset(spare(pad), 0.0).then_inc(oa_ready, HEADS)
                hook.end(0)

                hook.begin(1)

                def step_max(u, g, pair):
                    bank, j = S[u % 2], u // NT if g == 0 else u
                    z = zbuf[j]
                    if g == 0 and u % NT == 0:
                        dve.wait_ge(z_in[j], pair * 32 + (s * Z_PER_SEQ + HEADS // 2 * 16 + 32))
                        fence()
                    dve.wait_ge(bank.filled, used[bank].n + 1)
                    if g == 0:
                        tile = u % NT
                        kts = key_tiles(tile)
                        n, band = len(kts) * P, 2 * P + (kts[0] - tile + 1) * P
                        fence()
                        dve.tensor_tensor_reduce(scores_sb[u % 2][:, 0:n], bank[:, 0:n], z[:, band:band + n],
                                                 1.0, LOWEST, ALU.add, ALU.max, mx[:, u % 2, 0:1])\
                            .then_inc(bank.emptied, 1)
                        used[bank].up()
                        dve.wait_ge(bank.emptied, used[bank].n)
                        dve.tensor_scalar(unit_stat[:, PLACE[g], 0, tile, j:j + 1], mx[:, u % 2, 0:1], -1.0, None,
                                          ALU.mult).then_inc(maxed, 1)
                    else:
                        by_tile = scores_sb[u % 2][:, 0:F].rearrange("p (t k) -> p t k", k=P)
                        dve.tensor_tensor(by_tile, bank[:, :].rearrange("p (t k) -> p t k", k=P),
                                          z[:, PLACE[g] * P:(PLACE[g] + 1) * P].unsqueeze(1)
                                          .broadcast_to([P, NT, P]), ALU.add).then_inc(bank.emptied, 1)
                        used[bank].up()
                        dve.wait_ge(bank.emptied, used[bank].n)
                        then(dve.tensor_reduce(mx[:, u % 2, :], by_tile, AX_X, ALU.max))
                        dve.tensor_scalar(unit_stat[:, PLACE[g], 0, :, j], mx[:, u % 2, :], -1.0, None, ALU.mult)\
                            .then_inc(maxed, 1)
                    if g == 2:
                        dve.memset(spare(pad), 0.0).then_inc(z_read[j], 1)

                def keep_stats(g, pair):
                    then(dve.tensor_copy(
                        stat[:, PLACE[g], :, :, ds(2 * pair, 2)].rearrange("p k t h -> p (k t) h"),
                        unit_stat[:, PLACE[g], :, :, :].rearrange("p k t h -> p (k t) h")))

                step_max(0, 0, 0)
                for i in range(PAIRS // 2):
                    for at, b, g, last in steps_of_pairs(i):
                        units, following, pair = UNITS[g], (g + 1) % 3, 2 * i + b
                        for u in range(units):
                            ns = hooks_of_step(2 * i + b, g, u)
                            if u + 1 < units:
                                step_max(u + 1, g, pair)
                            for n in ns[:1]:
                                hook.front_on(n, 1)
                            if u == (3 if g == 0 else 1) and not last:
                                key_out(1 - at % 2, following)
                            if u % 2 == 1:
                                width = len(key_tiles(u % NT)) * P if g == 0 else F
                                dve.wait_ge(XV.filled, used[XV].n + 1)
                                dve.tensor_copy(probsT[1][:, 0:width], XV[:, 0:width]).then_inc(XV.emptied, 1)
                                used[XV].up()
                            for n in ns:
                                if n > ns[0]:
                                    hook.front_on(n, 1)
                                hook.back_on(n, 1)
                        t["dil"].up(units)
                        if g == 2:
                            keep_stats(0, pair)
                            keep_stats(1, pair)
                        if not last:
                            step_max(0, following, pair + (g == 2))
                        if g == 2:
                            dve.wait_ge(dil_exped, t["dil"].n)
                            keep_stats(2, pair)
                used[O].up(12 * PAIRS)
                used[PA].up(2 * (3 * PAIRS - 1))

                merge_groups(s, hook)

                used[XA].up(2 * HEADS + 6 * PAIRS)
                for i in rounds(bool(hooks), dve, C // 2, t, {PA: 2, XA: 2, PV: 2, XV: 2}):
                    for j in range(2):
                        for x in range(2):
                            hook.front(i * 4, DIL_HOOKS + 4 + 2 * j + x, 2)
                            hook.back(i * 4, DIL_HOOKS + 4 + 2 * j + x, 2)
                        for x, (gate, bank) in enumerate(((PA, PV), (XA, XV))):
                            used[gate].up()
                            dve.wait_ge(gate.emptied, used[gate].n)
                            dve.wait_ge(bank.filled, used[bank].n + 1)
                            dve.tensor_tensor(gate_sb[2 + x], bank[:, :], gate_sb[x], ALU.mult)\
                                .then_inc(bank.emptied, 1)
                            used[bank].up()
                        dve.wait_ge(XV.emptied, used[XV].n)
                        dve.tensor_tensor(merged[:, ds(2 * i + j, 1), :].rearrange("p a f -> p (a f)"),
                                          gate_sb[2], gate_sb[3], ALU.add).then_inc(gated, 1)
                hook.end(2)
                hook.begin(3)
                with turns(dve, C // 2, t, {PV: 2, "x1": 2}) as i:
                    for j in range(2):
                        hook.front(i * 2, j, 3)
                        hook.back(i * 2, j, 3)
                        dve.wait_ge(PV.filled, used[PV].n + 1)
                        dve.wait_ge(xr_in[j], (i + (1 + s * C // 2)) * 16)
                        dve.scalar_tensor_tensor(
                            out=x1T[:, ds(2 * i + j, 1), :].rearrange("p a f -> p (a f)"), in0=PV[:, :],
                            scalar=modT[:, ds(2 * C + 2 * i + j, 1), s:s + 1].rearrange("p a b -> p (a b)"),
                            in1=xr[j], op0=ALU.mult, op1=ALU.add).then_inc(PV.emptied, 1)
                        used[PV].up()
                        dve.wait_ge(PV.emptied, used[PV].n)
                        dve.memset(spare(pad), 0.0).then_inc(x1_ready, 1)
                        t["x1"].up()

                hook.front(0, C, 3)
                hook.back(0, C, 3)
                normalise(x1T, hT)
                hook.front(0, C + 1, 3)
                hook.back(0, C + 1, 3)
                modulate(s, 1, hT)
                for k in range(C + 2, C + 4):
                    hook.front(0, k, 3)
                    hook.back(0, k, 3)
                for tile in range(NT):
                    for which in range(2):
                        if NT * s + tile:
                            dve.wait_ge(stage_out[which], 16 * (NT * s + tile))
                        dve.wait_ge(XV.filled, used[XV].n + 1)
                        dve.tensor_copy(stage[which][:, F:D], XV[:, :]).then_inc(XV.emptied, 1)
                        used[XV].up()
                        used[XA].up()
                        dve.wait_ge(XV.emptied, used[XV].n)
                        dve.memset(spare(pad), 0.0).then_inc(staged_v, 1)
                    hook.front(0, C + 4 + tile, 3)
                    hook.back(0, C + 4 + tile, 3)
                if s + 1 < SEQS:
                    dve.wait_ge(x_in, 16 * (s + 2))
                    normalise(oaT, oaT)

                for i in rounds(bool(hooks), dve, HEADS // 2, t, {S[0]: 2, S[1]: 2, "rec": 2, "step": 48}):
                    for b in range(2):
                        for j in range(2):
                            hook.front(i * 4, 16 + 2 * b + j, 3)
                            hook.back(i * 4, 16 + 2 * b + j, 3)
                        for j in range(2):
                            dve.wait_ge(S[j].filled, used[S[j]].n + 1)
                            fence()
                            sc = S[j][:, :].rearrange("p (t k) -> p t k", k=P)
                            for tile in range(NT):
                                last = dve.max(topv[j][:, tile, 0:8], sc[:, tile, :])
                            then(last)
                            fence()
                            for tile in range(NT):
                                dve.match_replace(rest[:, tile, :], topv[j][:, tile, 0:8], sc[:, tile, :], LOWEST)
                            for tile in range(NT):
                                last = dve.max_index(topi[j][:, tile, 0:8], topv[j][:, tile, 0:8], sc[:, tile, :])
                            last.then_inc(S[j].emptied, 1)
                            used[S[j]].up()
                            dve.wait_ge(S[j].emptied, used[S[j]].n)
                            fence()
                            for tile in range(NT):
                                last = dve.max(topv[j][:, tile, 8:16], rest[:, tile, :])
                            then(last)
                            fence()
                            for tile in range(NT):
                                last = dve.max_index(topi[j][:, tile, 8:16], topv[j][:, tile, 8:16],
                                                     rest[:, tile, :])
                            then(last)
                            then(dve.tensor_copy(topf[j], topi[j].rearrange("p t k -> p (t k)")))
                        for tile in range(NT):
                            last = dve.tensor_tensor(
                                cand[:, tile, :].rearrange("p (a b) -> p a b", b=K16),
                                topv[0][:, tile, :].unsqueeze(2).broadcast_to([P, K16, K16]),
                                topv[1][:, tile, :].unsqueeze(1).broadcast_to([P, K16, K16]), ALU.add)
                        then(last)
                        fence()
                        for tile in range(NT):
                            last = dve.max(candv[:, tile, 0:8], cand[:, tile, :])
                        then(last)
                        fence()
                        for tile in range(NT):
                            dve.match_replace(cand2[:, tile, :], candv[:, tile, 0:8], cand[:, tile, :], LOWEST)
                        for tile in range(NT):
                            last = dve.max_index(candi[:, tile, 0:8], candv[:, tile, 0:8], cand[:, tile, :])
                        then(last)
                        fence()
                        for tile in range(NT):
                            last = dve.max(candv[:, tile, 8:16], cand2[:, tile, :])
                        then(last)
                        dve.tensor_tensor(gap.rearrange("p (t k) -> p t k", k=K16), candv,
                                          candv[:, :, 0:1].broadcast_to([P, NT, K16]), ALU.subtract)\
                            .then_inc(gap_ready, 1)
                        for tile in range(NT):
                            last = dve.max_index(candi[:, tile, 8:16], candv[:, tile, 8:16], cand2[:, tile, :])
                        then(last)
                        flat = candi.rearrange("p t k -> p (t k)")
                        dve.tensor_single_scalar(parti[0], flat, 4, op=ALU.logical_shift_right)
                        then(dve.tensor_single_scalar(parti[1], flat, 15, op=ALU.bitwise_and))
                        dve.tensor_copy(partf[0], parti[0])
                        then(dve.tensor_copy(partf[1], parti[1]))
                        for j in range(2):
                            then(dve.tensor_tensor(
                                hot.rearrange("p (a b) -> p a b", b=K16),
                                partf[j].unsqueeze(2).broadcast_to([P, TK, K16]),
                                iota16[:, :].unsqueeze(1).broadcast_to([P, TK, K16]), ALU.is_equal))
                            then(dve.tensor_tensor(
                                hot2.rearrange("p (t a b) -> p t a b", t=NT, b=K16),
                                hot.rearrange("p (t a b) -> p t a b", t=NT, b=K16),
                                topf[j].rearrange("p (t k) -> p t k", k=K16).unsqueeze(2)
                                .broadcast_to([P, NT, K16, K16]), ALU.mult))
                            then(dve.tensor_reduce(keyno[j], hot2.rearrange("p (a b) -> p a b", b=K16), AX_X,
                                                   ALU.add))
                        then(dve.scalar_tensor_tensor(out=expert_f, in0=keyno[0], scalar=float(P), in1=keyno[1],
                                                      op0=ALU.mult, op1=ALU.add))
                        dve.wait_ge(record_out[b], (i + s * HEADS // 2) * 32)
                        dve.tensor_copy(chosen[:, b, :], expert_f)
                        dve.wait_ge(gap_exped, t["rec"].n + 1)
                        then(dve.tensor_reduce(gsum, gexp.rearrange("p (t k) -> p t k", k=K16), AX_X, ALU.add))
                        then(dve.reciprocal(grec, gsum))
                        dve.tensor_tensor(share[:, b, :].rearrange("p (t k) -> p t k", k=K16),
                                          gexp.rearrange("p (t k) -> p t k", k=K16),
                                          grec.unsqueeze(2).broadcast_to([P, NT, K16]), ALU.mult)\
                            .then_inc(record_ready, 1)
                        t["rec"].up()
                used[PA].up(HEADS)
                used[XA].up(HEADS)
                for j in range(2):
                    dve.wait_ge(stage_out[j], 16 * NT * (s + 1))
                hook.end(3)

            dve.wait_ge(consts_in, 14 * 16)
            then(dve.tensor_tensor(lamv[:, 0, :], lamv[:, 0, :], lamv[:, 1, :], ALU.mult))
            dve.tensor_reduce(lam[:, 0:1], lamv[:, 0, :], AX_X, ALU.add)
            then(dve.tensor_tensor(lamv[:, 2, :], lamv[:, 2, :], lamv[:, 3, :], ALU.mult))
            dve.tensor_reduce(lam[:, 1:2], lamv[:, 2, :], AX_X, ALU.add).then_inc(lam_exp, 1)
            dve.memset(mixsign[:, 0:1], 1.0)
            then(dve.tensor_scalar(gsub[:, :], gsub[:, :], 1.0 - LAM_INIT, None, ALU.mult))
            for bank, dst, cols in ((XV, oaT[0:BIAS_ROWS, 0, :], slice(0, F)),
                                    (PV, oaT[0:BIAS_ROWS, 1, :], slice(F, 2 * F)),
                                    (XV, oaT[0:BIAS_ROWS, 6, 0:SUB], slice(2 * F, 2 * F + SUB))):
                dve.wait_ge(bank.filled, used[bank].n + 1)
                dve.tensor_tensor(dst, bank[0:BIAS_ROWS, 0:cols.stop - cols.start], mask[:, cols], ALU.add)\
                    .then_inc(bank.emptied, 1)
                used[bank].up()
                dve.wait_ge(bank.emptied, used[bank].n)
            dve.memset(spare(pad), 0.0).then_inc(rows_ready, 1)
            dve.wait_ge(x_in, 16)
            normalise(hT, hT)
            with turns(dve, WADA_SLABS // 2, t, {PV: 1, XV: 1}) as i:
                for j, bank in ((0, PV), (1, XV)):
                    dve.wait_ge(bank.filled, used[bank].n + 1)
                    dve.tensor_copy(mod[:, ds((2 * i + j) * WADA_COLS, WADA_COLS)], bank[0:SEQS, 0:WADA_COLS])\
                        .then_inc(bank.emptied, 1)
                    used[bank].up()
            dve.wait_ge(PV.filled, used[PV].n + 1)
            dve.tensor_tensor(modT[:, :, :].rearrange("p c s -> p (c s)"), PV[:, 0:6 * C * SEQS], b_ada[:, :],
                              ALU.add).then_inc(PV.emptied, 1)
            used[PV].up()
            dve.wait_ge(PV.emptied, used[PV].n)
            dve.memset(spare(pad), 0.0).then_inc(mod_ready, 1)
            for s in range(SEQS):
                for dst, part, g in ((scale1, 1, gmix), (scale2, 4, gffn)):
                    then(dve.scalar_tensor_tensor(out=dst[:, s, :], in0=modT[:, part * C:(part + 1) * C, s],
                                                  scalar=1.0, in1=g[:, :], op0=ALU.add, op1=ALU.mult))
            dve.wait_ge(lam_exp, 2)
            then(dve.tensor_tensor(lam[:, 0:1], lam[:, 3:4], lam[:, 2:3], ALU.subtract))
            then(dve.tensor_scalar(mixsign[:, 1:2], lam[:, 0:1], -LAM_INIT, None, ALU.add))
            used[PA].up(2)
            used[XA].up()
            used[O].up()

            attend(0, None)
            attend(1, gather)
            gather_alone(dve, gather, t, {"step": 14})


def slabs_of(weight, columns):
    rows = weight.shape[0] // P
    return np.stack([np.ascontiguousarray(weight[:, cols].reshape(rows, P, -1).transpose(1, 0, 2)).reshape(P, -1)
                     for cols in columns])


def bucket_table(rel):
    half, exact = BUCKETS // 2, BUCKETS // 4
    n = np.abs(rel)
    nf = np.maximum(n, exact).astype(np.float32)
    large = exact + (np.log(nf / np.float32(exact)) / np.float32(math.log(MAX_DISTANCE / exact))
                     * np.float32(half - exact)).astype(np.int32)
    bucket = np.where(rel > 0, half, 0) + np.where(n < exact, n, np.minimum(large, half - 1))
    return (np.arange(BUCKETS)[:, None] == bucket[None, :]).astype(np.float32)


def bias_tables():
    near, steps = np.arange(2 * F) - F, np.arange(SUB) - P
    onehot = np.concatenate([bucket_table(near), bucket_table(STRIDE * steps)], 1)
    mask = np.zeros((BIAS_ROWS, onehot.shape[1]), np.float32)
    mask[HEADS:, 0:2 * F] = np.where(np.abs(near) <= GROUPS[0][0] // 2, 0.0, MASKED)
    for g, (window, dilation) in enumerate(GROUPS):
        reached = (np.abs(STRIDE * steps) <= window // 2) & (STRIDE * steps % dilation == 0)
        mask[(1 + g) * HEADS:(2 + g) * HEADS, 2 * F:] = np.where(reached, 0.0, MASKED)
    return onehot, mask


def layout(inputs):
    def col(v):
        return np.ascontiguousarray(v.reshape(-1, P).T)

    a = {k: np.asarray(v) for k, v in inputs.items()}
    w_in, span = a["w_in"][0], np.arange(P)
    heads = [np.concatenate([x * D + h * P + span for x in range(3)]) for h in range(HEADS)]
    qkv_b = len(GROUPS) * HEADS * DH
    for pair in range(PAIRS):
        for g in range(len(GROUPS)):
            heads.append(np.concatenate([3 * D + x * qkv_b + g * HEADS * DH + pair * P + span for x in range(3)]))
    gates = 3 * D + 3 * qkv_b
    chunks = [c * P + span for c in range(C)]
    ga = slabs_of(w_in, [gates + c for c in chunks])
    gb = slabs_of(w_in, [gates + D + c for c in chunks])
    onehot, mask = bias_tables()
    keys = np.stack([a["sub_keys_1"][0], a["sub_keys_2"][0]], 1).reshape(2 * HEADS, P, P).transpose(0, 2, 1)
    xs = [a["x_prompt"][0], a["x_sample"][0]]
    return {
        "x_t": np.stack([x.T.reshape(C, P, F).transpose(1, 0, 2) for x in xs]),
        "c_t": np.stack([col(a["c_prompt"][0]), col(a["c_sample"][0])], -1),
        "w_ada": slabs_of(a["w_ada"][0], [n * WADA_COLS + np.arange(WADA_COLS) for n in range(WADA_SLABS)]),
        "b_ada": np.repeat(col(a["b_ada"][0]), SEQS, 1),
        "g_mix": col(a["g_norm_mix"][0]),
        "g_ffn": col(a["g_norm_ffn"][0]),
        "g_final": np.stack([a["g_final"]] * P),
        "g_sub": col(a["g_subln"][0]),
        "lambdas": np.stack([np.stack([a[f"lambda_{x}"][0] for x in ("q1", "k1", "q2", "k2")])] * P),
        "rel_bias": a["rel_bias"],
        "w_heads": slabs_of(w_in, heads),
        "w_merge": np.concatenate([ga, gb, slabs_of(a["w_proj_a"][0], chunks), slabs_of(a["w_proj_b"][0], chunks)], 2),
        "w_out": slabs_of(a["w_out"][0], chunks),
        "w_query": np.concatenate([slabs_of(a["w_query"][0], [m * P + span for m in range(2 * HEADS)]), keys], 2),
        "expert_u": a["expert_u"][0],
        "expert_v": a["expert_v"][0],
        "ident": np.eye(P, dtype=np.float32),
        "flip": np.eye(P, dtype=np.float32)[::-1],
        "iota16": np.stack([np.arange(K16, dtype=np.float32)] * P),
        "onehot": onehot,
        "mask": mask,
        "spread": np.repeat(np.eye(HEADS, dtype=np.float32), DH, 1),
    }


def kernel(**inputs):
    import concourse.bacc as bacc
    from concourse.bass_utils import run_bass_kernel_spmd

    nc = bacc.Bacc("TRN2", target_bir_lowering=False, num_devices=1)
    arrays = {"in_" + name: np.ascontiguousarray(v) for name, v in layout(inputs).items()}
    ins = {name[3:]: nc.dram_tensor(name, v.shape, mybir.dt.from_np(v.dtype), kind="ExternalInput").ap()
           for name, v in arrays.items()}
    y = [nc.dram_tensor(name, (F, D), F32, kind="ExternalOutput").ap() for name in ("y_prompt", "y_sample")]
    build(nc, ins, y)
    r = run_bass_kernel_spmd(nc, [arrays], core_ids=[0])
    return tuple(r.results[0][name].reshape(1, F, D) for name in ("y_prompt", "y_sample"))
```
